# Optimizing a Trainium2 kernel written in Bass

```python
import math
import jax, jax.numpy as jnp
from jax import lax
import numpy as np

D_MODEL = 1024
BATCH = 1
SEQ = 1024
DEPTH = 2

EPS_RMS = 1e-6
EPS_LN = 1e-5
CONV_K = 4
CHUNK = 128
SSD_HEADS = 16
SSD_HEAD_DIM = 64
D_SSD = SSD_HEADS * SSD_HEAD_DIM
SSD_GROUPS = 2
SSD_STATE = 64
XBC = D_SSD + 2 * SSD_GROUPS * SSD_STATE
SGU_GROUPS = 8
SGU_CH = 128
D_SGU = SGU_GROUPS * SGU_CH
IN_COLS = D_SSD + XBC + SSD_HEADS + 2 * D_SGU
MIX_OUT = D_SSD + D_SGU
LRU_WIDTH = D_MODEL
LRU_HEADS = 8
LRU_BW = LRU_WIDTH // LRU_HEADS
LRU_C = 8.0
MOE_GROUPS = 4
EXPERTS_PER_GROUP = 8
N_EXPERTS = MOE_GROUPS * EXPERTS_PER_GROUP
TOP_K = 2
D_EXPERT = 512
DISPATCH_BLOCK = 128

N_EVEN = (DEPTH + 1) // 2
N_ODD = DEPTH // 2

kernel_name = "hybrid_ssd_sgu_rglru_hmoe"

def rmsnorm(x, g):
    xf = x.astype(jnp.float32)
    y = xf * lax.rsqrt(jnp.mean(xf * xf, axis=-1, keepdims=True) + EPS_RMS)
    return (y * g.astype(jnp.float32)).astype(x.dtype)

def layernorm(x, g, b):
    xf = x.astype(jnp.float32)
    mu = jnp.mean(xf, axis=-1, keepdims=True)
    var = jnp.mean(jnp.square(xf - mu), axis=-1, keepdims=True)
    y = (xf - mu) * lax.rsqrt(var + EPS_LN)
    return (y * g.astype(jnp.float32) + b.astype(jnp.float32)).astype(x.dtype)

def causal_conv(x, w, b):
    c = x.shape[-1]
    y = lax.conv_general_dilated(
        x, w[:, None, :].astype(x.dtype), window_strides=(1,),
        padding=[(CONV_K - 1, 0)], dimension_numbers=("NWC", "WIO", "NWC"),
        feature_group_count=c)
    return y + b.astype(x.dtype)

def segsum(z):
    cs = jnp.cumsum(z, axis=-1)
    diff = cs[..., :, None] - cs[..., None, :]
    t = z.shape[-1]
    mask = jnp.tril(jnp.ones((t, t), dtype=bool))
    return jnp.where(mask, diff, -jnp.inf)

def ssd_chunked(x, dt, a, b, c):
    bn, l, h, p = x.shape
    n = b.shape[-1]
    nc = l // CHUNK
    xd = (x * dt[..., None]).reshape(bn, nc, CHUNK, h, p)
    adt = (dt * a).reshape(bn, nc, CHUNK, h).transpose(0, 3, 1, 2)
    b = b.reshape(bn, nc, CHUNK, h, n)
    c = c.reshape(bn, nc, CHUNK, h, n)
    a_cs = jnp.cumsum(adt, axis=-1)
    lmat = jnp.exp(segsum(adt))
    y_diag = jnp.einsum("bclhn,bcshn,bhcls,bcshp->bclhp", c, b, lmat, xd)
    decay_states = jnp.exp(a_cs[..., -1:] - a_cs)
    states = jnp.einsum("bclhn,bhcl,bclhp->bchpn", b, decay_states, xd)
    states = jnp.concatenate([jnp.zeros_like(states[:, :1]), states], axis=1)
    chunk_decay = jnp.exp(segsum(jnp.pad(a_cs[..., -1], ((0, 0), (0, 0), (1, 0)))))
    states = jnp.einsum("bhzc,bchpn->bzhpn", chunk_decay, states)[:, :-1]
    y_off = jnp.einsum("bclhn,bchpn,bhcl->bclhp", c, states, jnp.exp(a_cs))
    return (y_diag + y_off).reshape(bn, l, h, p)

def ssd_sgu_mixer(h, w_in, conv_w, conv_b, dt_bias, a_log, d_skip, ssd_norm,
                  ln_v_g, ln_v_b, spatial_w, spatial_b, w_out):
    bn, l, _ = h.shape
    proj = h @ w_in
    s1 = D_SSD
    s2 = s1 + XBC
    s3 = s2 + SSD_HEADS
    s4 = s3 + D_SGU
    z, xbc, dt_raw, u, v = jnp.split(proj, [s1, s2, s3, s4], axis=-1)
    xbc = jax.nn.silu(causal_conv(xbc, conv_w, conv_b))
    xs, bs, cs = jnp.split(xbc, [D_SSD, D_SSD + SSD_GROUPS * SSD_STATE], axis=-1)
    xs = xs.reshape(bn, l, SSD_HEADS, SSD_HEAD_DIM).astype(jnp.float32)
    rep = SSD_HEADS // SSD_GROUPS
    bs = jnp.repeat(bs.reshape(bn, l, SSD_GROUPS, SSD_STATE), rep, axis=2).astype(jnp.float32)
    cs = jnp.repeat(cs.reshape(bn, l, SSD_GROUPS, SSD_STATE), rep, axis=2).astype(jnp.float32)
    dt = jax.nn.softplus(dt_raw.astype(jnp.float32) + dt_bias.astype(jnp.float32))
    a = -jnp.exp(a_log.astype(jnp.float32))
    y = ssd_chunked(xs, dt, a, bs, cs) + d_skip.astype(jnp.float32)[:, None] * xs
    y = y.reshape(bn, l, D_SSD) * jax.nn.silu(z.astype(jnp.float32))
    y_ssd = rmsnorm(y, ssd_norm).astype(h.dtype)
    u = jax.nn.gelu(u)
    v = layernorm(jax.nn.gelu(v), ln_v_g, ln_v_b)
    v = v.reshape(bn, l // CHUNK, CHUNK, SGU_GROUPS, SGU_CH)
    w_causal = jnp.tril(spatial_w).astype(v.dtype)
    s = jnp.einsum("gts,bcsgd->bctgd", w_causal, v) + spatial_b.T.astype(v.dtype)[None, None, :, :, None]
    y_sgu = u * s.reshape(bn, l, D_SGU)
    return jnp.concatenate([y_ssd, y_sgu], axis=-1) @ w_out

def _lru_combine(c1, c2):
    a1, b1 = c1
    a2, b2 = c2
    return a1 * a2, a2 * b1 + b2

def rglru_block(h, w_in, conv_w, conv_b, w_a, b_a, w_i, b_i, lam, w_out):
    bn, l, _ = h.shape
    gate, xr = jnp.split(h @ w_in, 2, axis=-1)
    gate = jax.nn.gelu(gate)
    xr = causal_conv(xr, conv_w, conv_b)
    xh = xr.reshape(bn, l, LRU_HEADS, LRU_BW)
    r = jax.nn.sigmoid(jnp.einsum("blhi,hij->blhj", xh, w_a).reshape(bn, l, LRU_WIDTH).astype(jnp.float32)
                       + b_a.astype(jnp.float32))
    ig = jax.nn.sigmoid(jnp.einsum("blhi,hij->blhj", xh, w_i).reshape(bn, l, LRU_WIDTH).astype(jnp.float32)
                        + b_i.astype(jnp.float32))
    log_a = -LRU_C * r * jax.nn.softplus(-lam.astype(jnp.float32))
    a = jnp.exp(log_a)
    mult = jnp.sqrt(-jnp.expm1(2.0 * log_a))
    bx = xr.astype(jnp.float32) * ig * mult
    _, hs = lax.associative_scan(_lru_combine, (a, bx), axis=1)
    return (hs.astype(h.dtype) * gate) @ w_out

def hier_moe(h, w_group, b_group, w_expert, b_expert, w1, w3, w2):
    bn, l, d = h.shape
    t = bn * l
    xf = h.reshape(t, d)
    g_logits = (xf @ w_group).astype(jnp.float32) + b_group.astype(jnp.float32)
    g_prob = jax.nn.softmax(g_logits, axis=-1)
    g_idx = jnp.argmax(g_logits, axis=-1)
    p_g = jnp.take_along_axis(g_prob, g_idx[:, None], axis=1)[:, 0]
    e_logits = ((xf @ w_expert).astype(jnp.float32) + b_expert.astype(jnp.float32)).reshape(
        t, MOE_GROUPS, EXPERTS_PER_GROUP)
    e_logits = jnp.take_along_axis(e_logits, g_idx[:, None, None], axis=1)[:, 0]
    e_prob = jax.nn.softmax(e_logits, axis=-1)
    top_p, top_i = lax.top_k(e_prob, TOP_K)
    top_p = top_p / jnp.sum(top_p, axis=-1, keepdims=True)
    gates = p_g[:, None] * top_p
    ids = g_idx[:, None].astype(jnp.int32) * EXPERTS_PER_GROUP + top_i.astype(jnp.int32)
    n_assign = t * TOP_K
    e_flat = ids.reshape(n_assign)
    tok_flat = jnp.repeat(jnp.arange(t, dtype=jnp.int32), TOP_K)
    gate_flat = gates.reshape(n_assign)
    order = jnp.argsort(e_flat)
    e_sorted = e_flat[order]
    counts = jnp.zeros((N_EXPERTS,), jnp.int32).at[e_flat].add(1)
    starts = jnp.cumsum(counts) - counts
    pcounts = (counts + DISPATCH_BLOCK - 1) // DISPATCH_BLOCK * DISPATCH_BLOCK
    pends = jnp.cumsum(pcounts)
    pstarts = pends - pcounts
    dest = pstarts[e_sorted] + jnp.arange(n_assign, dtype=jnp.int32) - starts[e_sorted]
    n_blocks = -(-n_assign // DISPATCH_BLOCK) + N_EXPERTS
    n_rows = n_blocks * DISPATCH_BLOCK
    tok_buf = jnp.full((n_rows,), t, jnp.int32).at[dest].set(tok_flat[order])
    gate_buf = jnp.zeros((n_rows,), jnp.float32).at[dest].set(gate_flat[order])
    block_eid = jnp.clip(jnp.searchsorted(pends, jnp.arange(n_blocks, dtype=jnp.int32) * DISPATCH_BLOCK,
                                          side="right"), 0, N_EXPERTS - 1)
    xpad = jnp.concatenate([xf, jnp.zeros((1, d), xf.dtype)], axis=0)
    xb = xpad[tok_buf].reshape(n_blocks, DISPATCH_BLOCK, d)

    def expert_block(args):
        xblk, e = args
        hid = jax.nn.silu(xblk @ w1[e]) * (xblk @ w3[e])
        return hid @ w2[e]

    yb = lax.map(expert_block, (xb, block_eid)).reshape(n_rows, d)
    y = jax.ops.segment_sum(yb * gate_buf[:, None].astype(yb.dtype), tok_buf, num_segments=t + 1)[:t]
    return y.reshape(bn, l, d)

def setup_inputs(seed: int = 0) -> dict:
    key = jax.random.key(seed)
    ks = iter(jax.random.split(key, 64))
    nk = lambda: next(ks)
    f32 = jnp.float32
    nrm = lambda shape, scale: jax.random.normal(nk(), shape, f32) * scale
    x = jax.random.normal(nk(), (BATCH, SEQ, D_MODEL), f32)
    norm_mix = 1.0 + nrm((DEPTH, D_MODEL), 0.02)
    norm_ffn = 1.0 + nrm((DEPTH, D_MODEL), 0.02)
    norm_final = 1.0 + nrm((D_MODEL,), 0.02)
    ev_w_in = nrm((N_EVEN, D_MODEL, IN_COLS), D_MODEL ** -0.5)
    ev_conv_w = nrm((N_EVEN, CONV_K, XBC), CONV_K ** -0.5)
    ev_conv_b = nrm((N_EVEN, XBC), 0.02)
    dt0 = jnp.exp(jax.random.uniform(nk(), (N_EVEN, SSD_HEADS), f32) * (math.log(0.1) - math.log(0.001))
                  + math.log(0.001))
    ev_dt_bias = dt0 + jnp.log(-jnp.expm1(-dt0))
    ev_a_log = jnp.log(jax.random.uniform(nk(), (N_EVEN, SSD_HEADS), f32, 1.0, 16.0))
    ev_d_skip = 1.0 + nrm((N_EVEN, SSD_HEADS), 0.1)
    ev_ssd_norm = 1.0 + nrm((N_EVEN, D_SSD), 0.02)
    ev_ln_v_g = 1.0 + nrm((N_EVEN, D_SGU), 0.02)
    ev_ln_v_b = nrm((N_EVEN, D_SGU), 0.02)
    ev_spatial_w = nrm((N_EVEN, SGU_GROUPS, CHUNK, CHUNK), 0.5 * CHUNK ** -0.5)
    ev_spatial_b = 1.0 + nrm((N_EVEN, SGU_GROUPS, CHUNK), 0.02)
    ev_w_out = nrm((N_EVEN, MIX_OUT, D_MODEL), MIX_OUT ** -0.5)
    od_w_in = nrm((N_ODD, D_MODEL, 2 * LRU_WIDTH), D_MODEL ** -0.5)
    od_conv_w = nrm((N_ODD, CONV_K, LRU_WIDTH), CONV_K ** -0.5)
    od_conv_b = nrm((N_ODD, LRU_WIDTH), 0.02)
    od_w_a = nrm((N_ODD, LRU_HEADS, LRU_BW, LRU_BW), LRU_BW ** -0.5)
    od_b_a = nrm((N_ODD, LRU_WIDTH), 0.02)
    od_w_i = nrm((N_ODD, LRU_HEADS, LRU_BW, LRU_BW), LRU_BW ** -0.5)
    od_b_i = nrm((N_ODD, LRU_WIDTH), 0.02)
    a0 = jax.random.uniform(nk(), (N_ODD, LRU_WIDTH), f32, 0.9, 0.999) ** (1.0 / LRU_C)
    od_lam = jnp.log(a0) - jnp.log1p(-a0)
    od_w_out = nrm((N_ODD, LRU_WIDTH, D_MODEL), LRU_WIDTH ** -0.5)
    moe_w_group = nrm((DEPTH, D_MODEL, MOE_GROUPS), D_MODEL ** -0.5)
    moe_b_group = nrm((DEPTH, MOE_GROUPS), 0.01)
    moe_w_expert = nrm((DEPTH, D_MODEL, N_EXPERTS), D_MODEL ** -0.5)
    moe_b_expert = nrm((DEPTH, N_EXPERTS), 0.01)
    moe_w1 = nrm((DEPTH, N_EXPERTS, D_MODEL, D_EXPERT), D_MODEL ** -0.5)
    moe_w3 = nrm((DEPTH, N_EXPERTS, D_MODEL, D_EXPERT), D_MODEL ** -0.5)
    moe_w2 = nrm((DEPTH, N_EXPERTS, D_EXPERT, D_MODEL), D_EXPERT ** -0.5)
    return {
        "x": x, "norm_mix": norm_mix, "norm_ffn": norm_ffn, "norm_final": norm_final,
        "ev_w_in": ev_w_in, "ev_conv_w": ev_conv_w, "ev_conv_b": ev_conv_b,
        "ev_dt_bias": ev_dt_bias, "ev_a_log": ev_a_log, "ev_d_skip": ev_d_skip,
        "ev_ssd_norm": ev_ssd_norm, "ev_ln_v_g": ev_ln_v_g, "ev_ln_v_b": ev_ln_v_b,
        "ev_spatial_w": ev_spatial_w, "ev_spatial_b": ev_spatial_b, "ev_w_out": ev_w_out,
        "od_w_in": od_w_in, "od_conv_w": od_conv_w, "od_conv_b": od_conv_b,
        "od_w_a": od_w_a, "od_b_a": od_b_a, "od_w_i": od_w_i, "od_b_i": od_b_i,
        "od_lam": od_lam, "od_w_out": od_w_out,
        "moe_w_group": moe_w_group, "moe_b_group": moe_b_group,
        "moe_w_expert": moe_w_expert, "moe_b_expert": moe_b_expert,
        "moe_w1": moe_w1, "moe_w3": moe_w3, "moe_w2": moe_w2,
    }

def reference(x, norm_mix, norm_ffn, norm_final,
              ev_w_in, ev_conv_w, ev_conv_b, ev_dt_bias, ev_a_log, ev_d_skip,
              ev_ssd_norm, ev_ln_v_g, ev_ln_v_b, ev_spatial_w, ev_spatial_b, ev_w_out,
              od_w_in, od_conv_w, od_conv_b, od_w_a, od_b_a, od_w_i, od_b_i, od_lam, od_w_out,
              moe_w_group, moe_b_group, moe_w_expert, moe_b_expert, moe_w1, moe_w3, moe_w2):
    for i in range(DEPTH):
        j = i // 2
        h = rmsnorm(x, norm_mix[i])
        if i % 2 == 0:
            x = x + ssd_sgu_mixer(h, ev_w_in[j], ev_conv_w[j], ev_conv_b[j], ev_dt_bias[j],
                                  ev_a_log[j], ev_d_skip[j], ev_ssd_norm[j], ev_ln_v_g[j],
                                  ev_ln_v_b[j], ev_spatial_w[j], ev_spatial_b[j], ev_w_out[j])
        else:
            x = x + rglru_block(h, od_w_in[j], od_conv_w[j], od_conv_b[j], od_w_a[j], od_b_a[j],
                                od_w_i[j], od_b_i[j], od_lam[j], od_w_out[j])
        h = rmsnorm(x, norm_ffn[i])
        x = x + hier_moe(h, moe_w_group[i], moe_b_group[i], moe_w_expert[i], moe_b_expert[i],
                         moe_w1[i], moe_w3[i], moe_w2[i])
    return rmsnorm(x, norm_final)


_drawn_inputs = setup_inputs


def setup_inputs(seed=0):
    import zlib

    import numpy as np

    out = dict(_drawn_inputs(seed))
    spreads = {}
    factors = {'norm_final': 27.055,
     'ev_ln_v_g': 30.167,
     'ev_ln_v_b': 24.389,
     'od_b_a': 24.842,
     'od_b_i': 8.0,
     'moe_b_group': 13.637,
     'moe_b_expert': 11.611,
     'ev_spatial_b': 9.953,
     'norm_ffn': 3.507,
     'ev_conv_b': 4.445,
     'ev_ssd_norm': 4.924}
    for name, (base, spread) in spreads.items():
        noise = np.random.default_rng([zlib.crc32(name.encode()), seed]).standard_normal(out[name].shape)
        drawn = base * np.exp(spread * noise) if base else spread * noise
        out[name] = __import__('jax').numpy.asarray(drawn.astype(out[name].dtype))
    for name, factor in factors.items():
        out[name] = (out[name] * factor).astype(out[name].dtype)
    return out
```

```python
from contextlib import ExitStack

import numpy as np

import concourse.bass as bass
from concourse import mybir

F32 = mybir.dt.float32
F32R = mybir.dt.float32r
BF16 = mybir.dt.bfloat16
I32 = mybir.dt.int32
U32 = mybir.dt.uint32
ALU = mybir.AluOpType
ACT = mybir.ActivationFunctionType
AX = mybir.AxisListType.X

P = 128
T = 1024
D = 1024
MT = T // P
KD = D // P
H = 16
HP = 64
SG = 2
NS = 64
NG = 8
CONVK = 4
XBC0, DT0, U0, V0 = 1024, 2304, 2320, 3344
XTILES = 10
NE, EG, GE = 32, 4, 8
F = 512
LRU_C = 8.0
BLK = 128
OVF = (2 * T) // BLK - 1
YROWS = (NE + OVF) * BLK
EPS_RMS, EPS_LN = 1e-6, 1e-5
BIG = 1e30

SLICES = (
    [("ev_w_in", 0, V0, 512), ("ev_w_in", 0, V0 + 512, 512),
     ("ev_w_in", 0, U0, 512), ("ev_w_in", 0, U0 + 512, 512),
     ("ev_w_in", 0, XBC0 + 1024, 272), ("ev_w_in", 0, XBC0, 512), ("ev_w_in", 0, XBC0 + 512, 512),
     ("ev_w_in", 0, 0, 512), ("ev_w_in", 0, 512, 512),
     ("ev_w_out", 0, 0, 512), ("ev_w_out", 0, 512, 512),
     ("ev_w_out", 1024, 0, 512), ("ev_w_out", 1024, 512, 512)]
    + [("od_w_in", 0, c, 512) for c in (0, 512, 1024, 1536)]
    + [("od_w_out", 0, 0, 512), ("od_w_out", 0, 512, 512)]
)
S_V, S_U, S_X2, S_X0, S_Z, S_A, S_I, S_O = 0, 2, 4, 5, 7, 9, 13, 17
N_SL0 = 13

CV_CW, CV_CB, CV_SB = 0, 40, 50
CV_OW, CV_OB, CV_BA, CV_BI, CV_LAM, CV_N = 58, 90, 98, 106, 114, 122

NORM_MIX0, LN_G, LN_B, SSD_NORM, NORM_FFN0, NORM_MIX1, NORM_FFN1, NORM_FINAL = range(8)


class Chain:

    def __init__(self, eng, sem):
        self.eng, self.sem, self.n = eng, sem, 0

    def add(self, ins):
        self.n += 1
        ins.then_inc(self.sem, 1)

    def wait(self):
        self.eng.wait_ge(self.sem, self.n)

    def step(self, ins):
        self.add(ins)
        self.wait()


def trunk(nc, A, out):
    with ExitStack() as ctx:
        base = (nc.sbuf_base + 63) // 64 * 64
        place = [base]

        def region(nbytes):
            at = place[0]
            place[0] = at + (nbytes + 31) // 32 * 32
            assert place[0] <= nc.sbuf_usable_end
            return at

        def at(name, shape, dtype, offset):
            return nc.alloc_sbuf_tensor_at(name, shape, dtype, offset=offset)

        def sem(name):
            return ctx.enter_context(nc.semaphore(name))

        r_at = region(65536)
        r_raw = region(16384)
        r_whi = region(32768)
        r_wlo = region(32768)
        r_v = region(32768)
        ATH = at("act_t_hi", [P, KD, T], F32R, r_at)
        ATL = at("act_t_lo", [P, KD, T], F32R, r_at + 32768)
        WRAW = at("w_raw", [P, 2, 4, 512], F32, r_raw)
        WHI = at("w_hi", [P, 4, 4, 512], F32R, r_whi)
        WLO = at("w_lo", [P, 4, 4, 512], F32R, r_wlo)
        V = at("wide", [P, MT, D], F32, r_v)
        SP1, SP2 = (V[:, i, D - P:] for i in range(2))
        MRAW = [at(f"moe_raw{i}", [P, 4, 512], F32,
                   r_raw + 8192 * i if i < 2 else r_at + 8192 * (i - 2) if i < 10 else r_v + 8192 * (i - 10))
                for i in range(12)]
        XTH = at("moe_xt_hi", [P, KD, P], F32R, r_v + 16384)
        XTL = at("moe_xt_lo", [P, KD, P], F32R, r_v + 20480)
        GTH = at("moe_gt_hi", [P, 4, P], F32R, r_v + 24576)
        GTL = at("moe_gt_lo", [P, 4, P], F32R, r_v + 26624)
        SIL = at("moe_silu", [P, F], F32, r_v + 28672)
        GAT = at("moe_gated", [P, F], F32, r_v + 30720)
        CX = [at(f"comb_x{i}", [P, D], F32, r_v + 4096 * i) for i in range(4)]
        CY = [at(f"comb_y{i}", [P, D], F32, r_v + 16384 + 4096 * i) for i in range(4)]
        EX = [at(f"ssd_e{i}", [P, 4, P], F32, r_raw + 8192 + 2048 * i) for i in range(2)]
        ZS = at("ssd_z", [P, D], F32, r_raw + 12288)

        def small(name, shape, dtype=F32):
            n = int(np.prod(shape[1:])) * (2 if dtype == BF16 else 4)
            return at(name, shape, dtype, region(n))

        CONST = small("const", [P, 5 * P + 64])
        IDENT, UINC, USTR, IOTA, ONES = (CONST[:, P * i:P * (i + 1)] for i in range(5))
        MISC = CONST[:, 5 * P:]
        TOKID, THRESH, SLOTI, MHALF = MISC[:, 0:8], MISC[:, 8:15], MISC[:, 16:31], MISC[:, 32:33]
        E128 = MISC[:, 33:34]
        CBF = small("const_bf", [P, 2 * P], BF16)
        IDENTB, NEGB = CBF[:, 0:P], CBF[:, P:2 * P]
        COLV = small("colvecs", [P, CV_N])
        HROW = small("head_rows", [P, 3, H])
        RB = small("router_bias", [P, 2, EG + NE])
        BM = at("ssd_b", [P, P], F32, place[0])
        WR = small("router_w", [P, KD, EG + NE])
        XDD = at("ssd_xdd", [P, H, HP], F32, place[0])
        ECL = at("ssd_ecl", [P, MT, H], F32, place[0])
        GAM = [small(f"gain{i}", [P, D]) for i in range(2)]
        SS = small("ss", [P, 56])
        MS = small("ms", [P, 56])
        RSTD = small("rstd", [P, 56])
        ROWI = small("row_index", [P, MT, 2], I32)
        GATE = small("gates", [P, MT, 2])
        VPOS = small("ovf_pos", [P, MT, 2])
        IDXA = small("block_tokens", [P, NE], I32)
        CUR = [small(f"cur_idx{i}", [P, 2], I32) for i in range(2)]
        REGS = small("ovf_table", [P, 16], I32)
        r_s = region(0)
        s_room = nc.sbuf_usable_end - r_s
        plans = {}

        def scratch(plan, name, shape, dtype=F32):
            n = (int(np.prod(shape[1:])) * 4 + 31) // 32 * 32
            o = plans.get(plan, 0)
            plans[plan] = o + n
            assert plans[plan] <= s_room, (plan, name, plans[plan], s_room)
            return at(f"{plan}_{name}", shape, dtype, r_s + o)

        XTILE = [scratch("norm", f"x{i}", [P, D]) for i in range(2)]
        HTILE = [scratch("norm", f"h{i}", [P, D]) for i in range(2)]
        UT = [scratch("uz", f"t{i}", [P, 512]) for i in range(2)]
        BNS = scratch("uz", "bn", [P, 2, 6])
        MV = scratch("uz", "mv", [P, MT, 2])
        WSP = scratch("uz", "spatial", [P, NG, P])
        WSPT = scratch("uz", "spatial_t", [P, NG, P])
        BCT = [scratch("ssd", n, [P, T]) for n in ("bt", "ct")]
        DT = scratch("ssd", "dt", [P, MT, H])
        ADT = scratch("ssd", "adt", [P, MT, H])
        CACC = [scratch("ssd", f"conv{i}", [P, T]) for i in range(2)]
        o_c = plans["ssd"] - 8192 + r_s
        CSC = at("ssd_cs", [P, MT, H], F32, o_c)
        DEC = at("ssd_dec", [P, MT, H], F32, o_c + 512)
        ECS = at("ssd_ecs", [P, MT, H], F32, o_c + 1024)
        ECL2 = at("ssd_ecl2", [P, MT, 8], F32, o_c + 1536)
        XD = at("ssd_xd", [P, H, HP], F32, o_c + 1792)
        STATE = at("ssd_state", [P, 8, HP], F32, o_c + 5888)
        RES = [scratch("moe", f"res{i}", [P, 512]) for i in range(2)]
        HM = [scratch("moe", f"h{i}", [P, D]) for i in range(2)]
        HTF = scratch("moe", "ht", [P, KD, P])
        LOG = scratch("moe", "logits", [P, MT, EG + NE])
        G8 = scratch("route", "g8", [P, MT, 8])
        GV = scratch("route", "gv", [P, MT, 8])
        GI = scratch("route", "gi", [P, MT, 8], U32)
        EV = scratch("route", "ev", [P, MT, 8])
        EI = scratch("route", "ei", [P, MT, 8], U32)
        GIF = scratch("route", "gif", [P, MT, 1])
        EIF = scratch("route", "eif", [P, MT, 2])
        GM = scratch("route", "gmask", [P, MT, EG])
        EL = scratch("route", "el", [P, MT, NE])
        OH = scratch("route", "onehot", [P, 2, MT, NE])
        MM = scratch("route", "mask", [P, MT, NE])
        PR = scratch("route", "prod", [P, MT, NE])
        OT = scratch("route", "oht", [P, 2, MT, NE])
        POSK = scratch("route", "posk", [P, MT, 2])
        BK = scratch("route", "bk", [P, MT, 2])
        TMP = scratch("route", "tmp", [P, MT, 4])
        DEN = scratch("route", "den", [P, MT, 4])
        assert plans["route"] <= plans["moe"] - MT * 36 * 4
        PH = at("route_ph", [P, 4, P], F32, r_v)
        NOV = at("route_nov", [P, 3, NE], F32, r_v + 2048)
        CMP = at("route_cmp", [P, NE, 7], F32, r_v + 4096)
        CMS = at("route_cms", [P, OVF, NE], F32, r_v + 8192)
        ESL = at("route_esl", [P, 16], F32, r_v + 12288)
        XG = [scratch("loop", f"xg{i}", [P, D]) for i in range(2)]
        YSB = [scratch("loop", f"y{i}", [P, D]) for i in range(2)]
        XRC = [scratch("lru", "xr", [P, T]), GAM[1]]
        RGA, RGI, RGT = (scratch("lru", n, [P, T]) for n in ("a", "i", "t"))
        LW = GAM[0][:].rearrange("p (s w j) -> p s w j", s=4, w=2)
        LSP = scratch("lru", "sp", [P, 4, 8])
        HN = [scratch("comb", f"h{i}", [P, D]) for i in range(2)]
        OHB = at("ovf_onehot", [P, 2 * MT, P], F32, r_v)
        OXG = at("ovf_xg", [P, D], F32, r_v + 8192)
        OXT = at("ovf_xt", [P, KD, P], F32, r_v + 12288)
        OSIL = at("ovf_silu", [P, F], F32, r_v + 16384)
        OGAT = at("ovf_gated", [P, F], F32, r_v + 18432)
        OGT = at("ovf_gt", [P, 4, P], F32, r_v + 20480)
        OY = at("ovf_y", [P, D], F32, r_v + 22528)
        OIDX = at("ovf_idx", [P, 1], I32, r_v + 26624)

        PS = ctx.enter_context(nc.psum_tensor("psum", [P, 8, 512], F32))

        YG = nc.dram_tensor("scratch_ysgu", [T, D], F32).ap()
        XM = nc.dram_tensor("scratch_xmid", [T, D], F32).ap()
        X2 = nc.dram_tensor("scratch_x2", [T, D], F32).ap()
        HD = nc.dram_tensor("scratch_h", [T, D], F32).ap()
        YB = nc.dram_tensor("scratch_yb", [YROWS, D], F32).ap()

        phase_s = sem("phase_finished")
        const_in, vec_in, wsp_in, wr_in = sem("const_in"), sem("vectors_in"), sem("spatial_w_in"), sem("router_w_in")
        gain_in = [sem("gain_in0"), sem("gain_in1")]
        dve_ch, cb_done = sem("dve_chain"), sem("cb_done")
        dve_loop = [sem("ovf_pos_set0"), sem("ovf_pos_set1")]
        raw_in = [sem(f"raw_in{i}") for i in range(12)]
        w_hi_done, w_lo_done, pass_done = sem("w_hi_done"), sem("w_lo_done"), sem("pass_done")
        step_mm, step_use = sem("step_products"), sem("step_consumed")
        n_sq, n_ms, n_rstd, n_h = sem("norm_sq"), sem("norm_ms"), sem("norm_rstd"), sem("norm_h")
        n_tr, n_hi, n_lo = sem("tile_turned"), sem("turned_hi"), sem("turned_lo")
        x_in = [sem("x_in0"), sem("x_in1")]
        tile_st = [sem("tile_stored0"), sem("tile_stored1")]
        yg_in = [sem("ysgu_in0"), sem("ysgu_in1")]
        res_in = [sem("residual_in0"), sem("residual_in1")]
        a_tok, d_tok, p_tok, g_tok = sem("act_step"), sem("dve_step"), sem("pe_step"), sem("pool_step")
        h_st, xm_st = [sem("h_stored0"), sem("h_stored1")], sem("xmid_stored")
        zero_st = sem("zeros_stored")
        r_mm, r_log = sem("router_products"), sem("router_logits")
        m_hi, m_lo, m_unit = sem("moe_hi"), sem("moe_lo"), sem("moe_unit_used")
        m_xtr, m_xhi, m_xlo = sem("moe_x_turned"), sem("moe_x_hi"), sem("moe_x_lo")
        m_silu, m_gmul, m_gtr = sem("moe_silu"), sem("moe_gated"), sem("moe_g_turned")
        m_ghi, m_glo, m_yev = sem("moe_g_hi"), sem("moe_g_lo"), sem("moe_y_out_of_psum")
        y_st = [sem("y_stored0"), sem("y_stored1")]
        xg_in = [sem("xg_in0"), sem("xg_in1")]
        cur_set, gather_go = sem("cur_idx_set"), sem("gather_go")
        o_raw, o_xg, o_yst, o_v, o_a, o_p = ([sem(f"ovf_{n}{i}") for i in range(2)]
                                             for n in ("w_in", "x_in", "y_stored", "dve", "act", "pe"))
        cx_in = [sem(f"comb_x_in{i}") for i in range(4)]
        cy_in = [sem(f"comb_y_in{i}") for i in range(4)]
        c_add = sem("comb_added")
        x2_st = [sem(f"x2_stored{i}") for i in range(4)]
        out_st = [sem(f"out_stored{i}") for i in range(2)]
        l_w = [sem(f"lru_w_in{i}") for i in range(4)]
        l_a, l_v, l_p = sem("lru_act"), sem("lru_tile"), sem("lru_gates")
        l_hi, l_lo, l_taps = sem("lru_hi"), sem("lru_lo"), sem("lru_sp")

        block = ctx.enter_context(nc.Block())

        dve_chain = Chain(nc.vector, dve_ch)

        def finished(eng, k):
            eng.drain().then_inc(phase_s, 1)
            eng.wait_ge(phase_s, 4 * k)

        def rows(t, m):
            return t[m * P:(m + 1) * P, :]

        Q_MIX0, Q_LN, Q_SSD, Q_FFN, Q_MIX1, Q_FIN = 0, 8, 16, (24, 40), 32, 48
        T_MIX0, T_SSD, T_SGU, T_FFN, T_MIX1 = 0, 8, 16, (24, 40), 32
        L_OF = {0: 0, 8: 8, 16: 16, 32: 24}
        U_V, U_U, U_X, U_A, U_I, U_O = 0, 16, 32, 43, 75, 91

        def sq_index(q):
            return q + 1 if q < 8 else q - 7

        def act_square(q, x, h):
            nc.scalar.activation(h, x, ACT.Square, accum_out=SS[:, q:q + 1]).then_inc(n_sq, 1)

        def dve_mean(dve, q):
            dve.wait_ge(n_sq, sq_index(q))
            nc.vector.tensor_scalar(MS[:, q:q + 1], SS[:, q:q + 1], 1.0 / D, EPS_RMS, ALU.mult, ALU.add).then_inc(n_ms, 1)

        def pool_rstd(pool, q):
            pool.wait_ge(n_ms, q + 1)
            nc.gpsimd.tensor_tensor(RSTD[:, q:q + 1], MS[:, q:q + 1], MHALF, ALU.pow).then_inc(n_rstd, 1)

        def dve_scale(dve, q, x, h, gain):
            dve.wait_ge(n_rstd, q + 1)
            nc.vector.scalar_tensor_tensor(out=h, in0=x, scalar=RSTD[:, q:q + 1], in1=gain, op0=ALU.mult,
                                           op1=ALU.mult).then_inc(n_h, 1)

        def pe_turn(pe, ti, tile):
            if ti:
                pe.wait_ge(n_hi, 2 * ti)
                if lo_before(ti):
                    pe.wait_ge(n_lo, 2 * lo_before(ti))
            for hb in range(2):
                for c in range(4):
                    k = 4 * hb + c
                    last = nc.tensor.transpose(PS[:, 6 + hb, c * P:(c + 1) * P], tile[:, k * P:(k + 1) * P], IDENT)
                last.then_inc(n_tr, 1)

        def lo_before(ti):
            return ti - 8 * (ti > T_FFN[0] + 7) if ti <= T_FFN[0] or ti > T_FFN[0] + 7 and ti <= T_FFN[1] else \
                24 if ti <= T_FFN[0] + 7 else 32

        def act_turn_hi(act, ti, m):
            for hb in range(2):
                act.wait_ge(n_tr, 2 * ti + hb + 1)
                nc.scalar.activation(ATH[:, 4 * hb:4 * hb + 4, m * P:(m + 1) * P],
                                     PS[:, 6 + hb, :].rearrange("p (c t) -> p c t", c=4), ACT.Copy).then_inc(n_hi, 1)

        def dve_turn_lo(dve, ti, m):
            for hb in range(2):
                dve.wait_ge(n_hi, 2 * ti + hb + 1)
                sl = (slice(None), slice(4 * hb, 4 * hb + 4), slice(m * P, (m + 1) * P))
                nc.vector.tensor_tensor(ATL[sl], PS[:, 6 + hb, :].rearrange("p (c t) -> p c t", c=4),
                                        ATH[sl].bitcast(F32), ALU.subtract).then_inc(n_lo, 1)

        def sp_half_slice(sp, s, h):
            name, r0, c0, w = SLICES[s]
            src = A[name][0, r0:r0 + D, c0:c0 + w].rearrange("(h c p) n -> h p c n", p=P, c=4)
            sp.dma_start(WRAW[:, h, :, 0:w], src[h]).then_inc(raw_in[h], 16)

        def sp_slice(sp, s):
            for h in range(2):
                n = 2 * s + h
                if n >= 2:
                    sp.wait_ge(w_lo_done, n - 1)
                sp_half_slice(sp, s, h)

        def mixer_raw(s):
            return 16 * (s + 1 + (16 if s >= N_SL0 else 0))

        def act_split(act, s):
            w = SLICES[s][3]
            for h in range(2):
                act.wait_ge(raw_in[h], mixer_raw(s))
                if s >= 2:
                    act.wait_ge(pass_done, s - 1)
                nc.scalar.activation(WHI[:, 2 * (s % 2) + h, :, 0:w], WRAW[:, h, :, 0:w], ACT.Copy).then_inc(w_hi_done, 1)

        def dve_split(dve, s):
            w = SLICES[s][3]
            for h in range(2):
                dve.wait_ge(w_hi_done, 2 * s + h + 1)
                slot = 2 * (s % 2) + h
                nc.vector.tensor_tensor(WLO[:, slot, :, 0:w], WRAW[:, h, :, 0:w], WHI[:, slot, :, 0:w].bitcast(F32),
                                        ALU.subtract).then_inc(w_lo_done, 1)

        def three(o, lh, ll, rh, rl, first, last):
            nc.tensor.matmul(o, lh, rh, start=first, stop=False)
            nc.tensor.matmul(o, lh, rl, start=False, stop=False)
            return nc.tensor.matmul(o, ll, rh, start=False, stop=last)

        def pe_token_step(pe, s, m, u, u0):
            if m == 0:
                pe.wait_ge(w_lo_done, 2 * s + 2)
            if u - u0 >= 4:
                pe.wait_ge(step_use, u - 3)
            bank = (u - u0) % 4
            for k in range(KD):
                slot, c = 2 * (s % 2) + k // 4, k % 4
                mm = three(PS[:, bank, :], ATH[:, k, m * P:(m + 1) * P], ATL[:, k, m * P:(m + 1) * P],
                           WHI[:, slot, c, :], WLO[:, slot, c, :], k == 0, k == KD - 1)
            mm.then_inc(step_mm, 1)

        def pe_pass_end(s):
            nc.tensor.drain().then_inc(pass_done, 1)

        def pe_chan_step(pe, s, j, u, u0):
            if j == 0:
                pe.wait_ge(w_lo_done, 2 * s + 2)
            if u - u0 >= 2:
                pe.wait_ge(step_use, u - 1)
            b0 = 2 * ((u - u0) % 2)
            for nh in range(2):
                for k in range(KD):
                    slot, c = 2 * (s % 2) + k // 4, k % 4
                    mm = three(PS[:, b0 + nh, :], WHI[:, slot, c, j * P:(j + 1) * P], WLO[:, slot, c, j * P:(j + 1) * P],
                               ATH[:, k, nh * 512:(nh + 1) * 512], ATL[:, k, nh * 512:(nh + 1) * 512],
                               k == 0, k == KD - 1)
            mm.then_inc(step_mm, 1)

        def two_banks(b0):
            return PS[:, b0:b0 + 2, :].rearrange("p b n -> p (b n)")

        def head_bc(t, m, n):
            return t[:, m, :].unsqueeze(2).to_broadcast([P, H, n])

        def sp_phase0(sp):
            sp.dma_start(CONST[:], A["c_f32"]).then_inc(const_in, 16)
            sp.dma_start(GAM[0][:], A["norm_mix"][0:1, :].to_broadcast([P, D])).then_inc(gain_in[0], 16)
            for m in range(2):
                sp.dma_start(XTILE[m][:], rows(A["x"][0], m)).then_inc(x_in[m], 16)
            sp_slice(sp, 0)
            for r0, src in ((CV_CW, A["ev_conv_w"][0].rearrange("k (j p) -> (k j) p", p=P)),
                            (CV_CB, A["ev_conv_b"][0].rearrange("(j p) -> j p", p=P)),
                            (CV_SB, A["ev_spatial_b"][0]),
                            (CV_OW, A["od_conv_w"][0].rearrange("k (j p) -> (k j) p", p=P)),
                            (CV_OB, A["od_conv_b"][0].rearrange("(j p) -> j p", p=P)),
                            (CV_BA, A["od_b_a"][0].rearrange("(j p) -> j p", p=P)),
                            (CV_BI, A["od_b_i"][0].rearrange("(j p) -> j p", p=P)),
                            (CV_LAM, A["od_lam"][0].rearrange("(j p) -> j p", p=P))):
                sp.dma_start(V[r0:r0 + src.shape[0], 0, 0:P], src).then_inc(vec_in, 16)
            for i, n in enumerate(("ev_dt_bias", "ev_a_log", "ev_d_skip")):
                sp.dma_start(HROW[:, i, :], A[n].to_broadcast([P, H])).then_inc(vec_in, 16)
            for l in range(2):
                sp.dma_start(RB[:, l, 0:EG], A["moe_b_group"][l:l + 1, :].to_broadcast([P, EG])).then_inc(vec_in, 16)
                sp.dma_start(RB[:, l, EG:], A["moe_b_expert"][l:l + 1, :].to_broadcast([P, NE])).then_inc(vec_in, 16)
            for m in range(2, MT):
                sp.wait_ge(n_h, m - 1)
                sp.dma_start(XTILE[m % 2][:], rows(A["x"][0], m)).then_inc(x_in[m % 2], 16)

        VEC_DMAS = 8 + 3 + 4

        def act_phase0(act):
            for m in range(MT + 1):
                if m < MT:
                    act.wait_ge(x_in[m % 2], 16 * (m // 2 + 1))
                    if m >= 2:
                        act.wait_ge(n_tr, 2 * (m - 1))
                    act_square(m, XTILE[m % 2][:], HTILE[m % 2][:])
                if m >= 1:
                    act_turn_hi(act, m - 1, m - 1)
            act_split(act, 0)

        def dve_phase0(dve):
            dve.wait_ge(gain_in[0], 16)
            for m in range(MT + 2):
                if m < MT:
                    dve_mean(dve, m)
                if 1 <= m <= MT:
                    dve_scale(dve, m - 1, XTILE[(m - 1) % 2][:], HTILE[(m - 1) % 2][:], GAM[0][:])
                if m >= 2:
                    dve_turn_lo(dve, m - 2, m - 2)
            dve_split(dve, 0)
            dve.wait_ge(p_tok, 1)
            nc.vector.tensor_copy(COLV[:], PS[:, 5, 0:CV_N])
            dve.wait_ge(const_in, 16)
            nc.vector.tensor_copy(IDENTB, IDENT)
            nc.vector.tensor_scalar(NEGB, UINC, -1.0, BIG, ALU.add, ALU.mult)

        def pool_phase0(pool):
            pool.wait_ge(const_in, 16)
            for m in range(MT):
                pool_rstd(pool, m)

        def pe_phase0(pe):
            pe.wait_ge(const_in, 16)
            for m in range(MT):
                pe.wait_ge(n_h, m + 1)
                pe_turn(pe, m, HTILE[m % 2])
            pe.wait_ge(vec_in, 16 * VEC_DMAS)
            nc.tensor.transpose(PS[:, 5, 0:CV_N], V[0:CV_N, 0, 0:P], IDENT[0:CV_N, 0:CV_N]).then_inc(p_tok, 1)

        def sp_phase1(sp):
            sp.wait_ge(n_h, MT)
            sp.dma_start(GAM[0][:], A["ev_ln_v_b"].to_broadcast([P, D])).then_inc(gain_in[0], 16)
            sp.dma_start(GAM[1][:], A["ev_ln_v_g"].to_broadcast([P, D])).then_inc(gain_in[1], 16)
            sp.wait_ge(phase_s, 4)
            sp_slice(sp, 1)
            sp.dma_start(WSP[:], A["ev_spatial_w"][0].rearrange("g t s -> t g s")).then_inc(wsp_in, 16)
            sp_slice(sp, 2)

        def act_phase1(act):
            act_split(act, 1)
            for m in range(MT):
                act.wait_ge(step_mm, U_V + m + 1)
                nc.scalar.activation(V[:, m, 0:512], PS[:, m % 4, :], ACT.Gelu_apprx_tanh).then_inc(step_use, 1)
            act_split(act, 2)
            for m in range(MT):
                act.wait_ge(step_mm, U_V + 8 + m + 1)
                nc.scalar.activation(V[:, m, 512:1024], PS[:, m % 4, :], ACT.Gelu_apprx_tanh).then_inc(step_use, 1)

        def dve_phase1(dve):
            ch = dve_chain
            dve_split(dve, 1)
            for hb in range(2):
                dve.wait_ge(p_tok, 2 + hb)
                nc.vector.tensor_tensor(WSPT[:, 4 * hb:4 * hb + 4, :], PS[:, 4 + hb, :].rearrange("p (g t) -> p g t", g=4),
                                        UINC.unsqueeze(1).to_broadcast([P, 4, P]), ALU.mult).then_inc(d_tok, 1)
            dve_split(dve, 2)
            dve.wait_ge(gain_in[0], 32)
            dve.wait_ge(gain_in[1], 16)
            for m in range(MT):
                dve.wait_ge(step_use, U_V + 8 + m + 1)
                ch.add(nc.vector.bn_stats(BNS[:, 0, :], V[:, m, 0:512]))
                ch.step(nc.vector.bn_stats(BNS[:, 1, :], V[:, m, 512:1024]))
                ch.step(nc.vector.bn_aggr(MV[:, m, :], BNS[:]))
                nc.vector.tensor_scalar(MS[:, Q_LN + m:Q_LN + m + 1], MV[:, m, 1:2], EPS_LN, None, ALU.add).then_inc(n_ms, 1)
                dve.wait_ge(n_rstd, Q_LN + m + 1)
                ch.step(nc.vector.tensor_scalar(V[:, m, :], V[:, m, :], MV[:, m, 0:1], RSTD[:, Q_LN + m:Q_LN + m + 1],
                                                ALU.subtract, ALU.mult))
                ch.step(nc.vector.tensor_tensor(V[:, m, :], V[:, m, :], GAM[1][:], ALU.mult))
                nc.vector.tensor_tensor(V[:, m, :], V[:, m, :], GAM[0][:], ALU.add).then_inc(n_h, 1)
                if m >= 1:
                    dve_spatial(dve, m - 1)
            dve_spatial(dve, MT - 1)

        def dve_spatial(dve, m):
            for hb in range(2):
                dve.wait_ge(p_tok, 4 + 2 * m + hb)
                nc.vector.tensor_tensor(V[:, m, hb * 512:(hb + 1) * 512].rearrange("p (g d) -> p g d", g=4),
                                        PS[:, 4 + hb, :].rearrange("p (g d) -> p g d", g=4),
                                        COLV[:, CV_SB + 4 * hb:CV_SB + 4 * hb + 4].unsqueeze(2).to_broadcast([P, 4, P]),
                                        ALU.add).then_inc(d_tok, 1)

        def pool_phase1(pool):
            for m in range(MT):
                pool_rstd(pool, Q_LN + m)

        def pe_phase1(pe):
            for m in range(MT):
                pe_token_step(pe, 0, m, U_V + m, U_V)
            pe_pass_end(0)
            pe.wait_ge(wsp_in, 16)
            for hb in range(2):
                for g in range(4):
                    mm = nc.tensor.transpose(PS[:, 4 + hb, g * P:(g + 1) * P], WSP[:, 4 * hb + g, :], IDENT)
                mm.then_inc(p_tok, 1)
            for m in range(MT + 1):
                if m < MT:
                    pe_token_step(pe, 1, m, U_V + 8 + m, U_V)
                if m >= 1:
                    pe_spatial(pe, m - 1)
            pe_pass_end(1)

        def pe_spatial(pe, m):
            pe.wait_ge(n_h, Q_LN + m + 1)
            for hb in range(2):
                pe.wait_ge(d_tok, 2 + 2 * (m - 1) + hb + 1 if m else 2)
                for g in range(4):
                    mm = nc.tensor.matmul(PS[:, 4 + hb, g * P:(g + 1) * P], WSPT[:, 4 * hb + g, :],
                                          V[:, m, (4 * hb + g) * P:(4 * hb + g + 1) * P], start=True, stop=True)
                mm.then_inc(p_tok, 1)

        def sp_phase2(sp):
            sp.wait_ge(n_h, Q_LN + MT)
            sp.dma_start(GAM[1][:], A["ev_ssd_norm"].to_broadcast([P, D])).then_inc(gain_in[1], 16)
            for s in (3, 4):
                sp_slice(sp, s)

        def act_phase2(act):
            for n in range(2):
                act_split(act, S_U + n + 1)
                for m in range(MT):
                    u = U_U + 8 * n + m
                    act.wait_ge(step_mm, u + 1)
                    if 8 * n + m >= 2:
                        act.wait_ge(d_tok, D_U + 8 * n + m - 1)
                    nc.scalar.activation(UT[m % 2][:], PS[:, (8 * n + m) % 4, :], ACT.Gelu_apprx_tanh).then_inc(step_use, 1)

        D_U = 18

        def dve_phase2(dve):
            for n in range(2):
                dve_split(dve, S_U + n + 1)
                for m in range(MT):
                    u = U_U + 8 * n + m
                    dve.wait_ge(step_use, u + 1)
                    sl = V[:, m, n * 512:(n + 1) * 512]
                    nc.vector.tensor_tensor(sl, UT[m % 2][:], sl, ALU.mult).then_inc(d_tok, 1)

        def pool_phase2(pool):
            for n in range(2):
                for m in range(MT):
                    pool.wait_ge(d_tok, D_U + 8 * n + m + 1)
                    pool.dma_start(rows(YG, m)[:, n * 512:(n + 1) * 512], V[:, m, n * 512:(n + 1) * 512])\
                        .then_inc(tile_st[0], 16)
            pool.wait_ge(tile_st[0], 16 * 16)

        def pe_phase2(pe):
            for n in range(2):
                for m in range(MT):
                    pe_token_step(pe, S_U + n, m, U_U + 8 * n + m, U_U)
                pe_pass_end(S_U + n)

        def sp_phase4(sp):
            for s in (5, 6, 7, 8):
                sp_slice(sp, s)

        CH_OF = {0: 8, 1: 9, **{3 + i: i for i in range(8)}}
        A_X = 0

        def act_phase4(act):
            act_split(act, 5)
            for j in range(11):
                if j in (3, 7):
                    act_split(act, 6 if j == 3 else 7)
                if j == 2:
                    act.wait_ge(step_mm, U_X + 3)
                    nc.scalar.activation(CACC[0][0:H, :], two_banks(0)[0:H], ACT.Copy).then_inc(step_use, 1)
                    continue
                if j == 4:
                    act_softplus(act)
                t, i = CH_OF[j], j if j < 2 else j - 1
                acc = BCT[j] if j < 2 else CACC[j % 2]
                act.wait_ge(step_mm, U_X + j + 1)
                if j >= 5:
                    act.wait_ge(p_tok, P_X + 1 + 2 * (j - 4))
                nc.scalar.activation(acc[:], two_banks(2 * (j % 2)), ACT.Identity, bias=COLV[:, CV_CB + t:CV_CB + t + 1],
                                     scale=COLV[:, CV_CW + 30 + t:CV_CW + 31 + t]).then_inc(a_tok, 1)
                act.wait_ge(step_use, U_X + j + 1)
                nc.scalar.activation(acc[:], acc[:], ACT.Silu).then_inc(a_tok, 1)
            act_split(act, 8)

        P_X = 19
        D_X = D_U + 16

        def a_count(j):
            return A_X + (2 * j + 2 if j < 2 else 6 if j == 3 else 2 * j + 2)

        def act_softplus(act):
            act.wait_ge(d_tok, D_X + 1)
            nc.scalar.activation(SP2, SP1, ACT.Exp, scale=-1.0).then_inc(a_tok, 1)
            nc.scalar.activation(HROW[:, 1, :], HROW[:, 1, :], ACT.Exp).then_inc(a_tok, 1)

        def log1p_of(ch, u, z, w):
            ch.step(nc.vector.tensor_scalar(z, u, 2.0, None, ALU.add))
            ch.step(nc.vector.reciprocal(z, z))
            ch.step(nc.vector.tensor_tensor(z, z, u, ALU.mult))
            ch.step(nc.vector.tensor_tensor(w, z, z, ALU.mult))
            ch.step(nc.vector.tensor_scalar(u, w, 2.0 / 15, 2.0 / 13, ALU.mult, ALU.add))
            for c in (11, 9, 7, 5, 3, 1):
                ch.step(nc.vector.tensor_tensor(u, u, w, ALU.mult))
                ch.step(nc.vector.tensor_scalar(u, u, 2.0 / c, None, ALU.add))
            ch.step(nc.vector.tensor_tensor(u, u, z, ALU.mult))

        def dve_phase4(dve):
            ch = dve_chain
            dve_split(dve, 5)
            for j in range(11):
                if j in (3, 7):
                    dve_split(dve, 6 if j == 3 else 7)
                if j == 2:
                    continue
                if j == 4:
                    dve.wait_ge(p_tok, P_X + 1)
                    ch.step(nc.vector.tensor_tensor(DT[:], PS[:, 4, 0:MT * H].rearrange("p (m h) -> p m h", m=MT),
                                                    HROW[:, 0, :].unsqueeze(1).to_broadcast([P, MT, H]), ALU.add))
                    dt = DT[:].rearrange("p m h -> p (m h)")
                    nc.vector.scalar_tensor_tensor(out=SP1, in0=dt, scalar=-1.0, in1=dt, op0=ALU.mult, op1=ALU.max).then_inc(d_tok, 1)
                if j == 6:
                    dve.wait_ge(a_tok, a_count(3) + 2)
                    log1p_of(ch, SP2, SP1, ADT[:].rearrange("p m h -> p (m h)"))
                    ch.step(nc.vector.tensor_scalar(dt, dt, 0.0, None, ALU.max))
                    ch.step(nc.vector.tensor_tensor(dt, dt, SP2, ALU.add))
                    ch.step(nc.vector.tensor_scalar(HROW[:, 1, :], HROW[:, 1, :], -1.0, None, ALU.mult))
                    ch.step(nc.vector.tensor_tensor(ADT[:], DT[:], HROW[:, 1, :].unsqueeze(1).to_broadcast([P, MT, H]),
                                                    ALU.mult))
                t = CH_OF[j]
                acc = BCT[j] if j < 2 else CACC[j % 2]
                dve.wait_ge(a_tok, a_count(j) - 1)
                src = two_banks(2 * (j % 2))
                for tap in (2, 1, 0):
                    sh = 3 - tap
                    w = COLV[:, CV_CW + 10 * tap + t:CV_CW + 10 * tap + t + 1]
                    ins = nc.vector.scalar_tensor_tensor(out=acc[:, sh:], in0=src[:, :T - sh], scalar=w, in1=acc[:, sh:],
                                                         op0=ALU.mult, op1=ALU.add)
                    if tap:
                        ch.step(ins)
                    else:
                        ins.then_inc(step_use, 1)
                if j >= 4:
                    dve_xs(dve, j - 1)
            dve_split(dve, 8)
            dve_xs(dve, 10)

        def dve_xs(dve, j):
            for hb in range(2):
                dve.wait_ge(p_tok, P_X + 1 + 2 * (j - 3) + hb + 1)
                nc.vector.tensor_copy(V[:, 4 * hb:4 * hb + 4, (j - 3) * P:(j - 2) * P],
                                      PS[:, 4 + hb, :].rearrange("p (m c) -> p m c", m=4)).then_inc(d_tok, 1)

        def pool_phase4(pool):
            nc.gpsimd.memset(GAM[0][:], 0.0).then_inc(g_tok, 1)
            pool.wait_ge(g_tok, 1)
            for b in range(OVF):
                r0 = (NE + b) * BLK
                pool.dma_start(YB[r0:r0 + BLK, :], GAM[0][:]).then_inc(zero_st, 16)
            pool.wait_ge(zero_st, 16 * OVF)

        def pe_phase4(pe):
            for j in range(2):
                pe_chan_step(pe, S_X2, j, U_X + j, U_X)
            pe.wait_ge(step_use, U_X + 1)
            for nh in range(2):
                for k in range(KD):
                    slot, c = k // 4, k % 4
                    mm = three(PS[0:H, nh, :], WHI[:, slot, c, 256:272], WLO[:, slot, c, 256:272],
                               ATH[:, k, nh * 512:(nh + 1) * 512], ATL[:, k, nh * 512:(nh + 1) * 512], k == 0, k == KD - 1)
            mm.then_inc(step_mm, 1)
            pe_pass_end(S_X2)
            for j in range(3, 12):
                if j < 11:
                    s = S_X0 + (j - 3) // 4
                    pe_chan_step(pe, s, (j - 3) % 4, U_X + j, U_X)
                    if j in (6, 10):
                        pe_pass_end(s)
                if j == 3:
                    pe.wait_ge(step_use, U_X + 3)
                    for m in range(MT):
                        mm = nc.tensor.transpose(PS[:, 4, m * H:(m + 1) * H], CACC[0][0:H, m * P:(m + 1) * P], IDENT[0:H, 0:H])
                    mm.then_inc(p_tok, 1)
                if j >= 4:
                    i = j - 1
                    pe.wait_ge(a_tok, a_count(i))
                    for hb in range(2):
                        if i == 3:
                            pe.wait_ge(d_tok, D_X + 1)
                        else:
                            pe.wait_ge(d_tok, D_X + 1 + 2 * (i - 4) + hb + 1)
                        for q in range(4):
                            m = 4 * hb + q
                            mm = nc.tensor.transpose(PS[:, 4 + hb, q * P:(q + 1) * P], CACC[i % 2][:, m * P:(m + 1) * P], IDENT)
                        mm.then_inc(p_tok, 1)

        P_S, D_S, A_S = P_X + 17, D_X + 17, A_X + 6 + 16
        PPC, DPC, APC = 13, 13, 7
        P_S1, D_S1, A_S1 = P_S + 1, D_S + 2, A_S + 1
        PC_CB, PC_DEC, PC_Z, PC_YO, PC_YD, PC_ST = 1, (2, 3, 7, 10), (4, 8), 5, (6, 9, 11, 12), 13
        DC_XDD, DC_BM, DC_DIFF, DC_SC, DC_ST, DC_Y = 2, 3, (4, 6, 8, 10), (5, 7, 9, 11), 12, 13
        AC_EXP, AC_Z, AC_SILU = (1, 2, 4, 6), (3, 5), 7

        def sp_phase5(sp):
            sp.wait_ge(w_lo_done, 2 * S_A - 1)
            sp_half_slice(sp, S_A, 0)
            sp.wait_ge(n_sq, sq_index(Q_SSD + MT - 1))
            sp_half_slice(sp, S_A, 1)

        def pe_phase5(pe):
            adt = ADT[:].rearrange("p m h -> p (m h)")
            nc.tensor.matmul(PS[:, 0, 0:P], UINC, adt, start=True, stop=True)
            nc.tensor.matmul(PS[:, 1, 0:P], ONES, adt, start=True, stop=True).then_inc(p_tok, 1)
            pe.wait_ge(w_lo_done, 2 * S_A)
            for m in range(MT):
                d0, a0 = D_S1 + DPC * m, A_S1 + APC * m
                t = slice(m * P, (m + 1) * P)
                pe.wait_ge(d_tok, d0 - DPC + DC_SC[3] if m else d0)
                for g in range(SG):
                    nc.tensor.matmul(PS[:, 4, g * P:(g + 1) * P], BCT[0][64 * g:64 * g + 64, t], BCT[1][64 * g:64 * g + 64, t],
                                     start=True, stop=True).then_inc(cb_done, 1)
                    pe.wait_ge(cb_done, 2 * m + g + 1)
                nc.tensor.transpose(PS[:, 4, 2 * P:3 * P], BCT[0][:, t], IDENT).then_inc(p_tok, 1)
                if m >= 2:
                    pe.wait_ge(n_lo, 2 * (T_SSD + m - 2) + 2)
                    pe.wait_ge(n_hi, 2 * (T_SSD + m - 2) + 2)

                def decay_rows(q):
                    for i in range(4):
                        nc.tensor.matmul(PS[:, 6 + q % 2, i * P:(i + 1) * P],
                                         ADT[:, m, 4 * q + i:4 * q + i + 1].to_broadcast([P, P]), UINC,
                                         start=(i == 0), stop=False, skip_group_check=True)
                    mm = nc.tensor.matmul(PS[:, 6 + q % 2, :], IDENTB, NEGB.unsqueeze(1).to_broadcast([P, 4, P]),
                                          start=False, stop=True, skip_group_check=True)
                    mm.then_inc(p_tok, 1)

                def z_half(n):
                    for k in range(KD):
                        slot, c = 2 * ((S_Z + n) % 2) + k // 4, k % 4
                        mm = three(PS[:, 5, :], ATH[:, k, t], ATL[:, k, t], WHI[:, slot, c, :], WLO[:, slot, c, :],
                                   k == 0, k == KD - 1)
                    mm.then_inc(p_tok, 1)

                def y_diag(q):
                    pe.wait_ge(d_tok, d0 + DC_SC[q])
                    for i in range(4):
                        h = 4 * q + i
                        mm = nc.tensor.matmul(PS[:, h // 8, (h % 8) * HP:(h % 8 + 1) * HP], EX[q % 2][:, i, :], XD[:, h, :],
                                              start=True, stop=True)
                    mm.then_inc(p_tok, 1)

                decay_rows(0)
                decay_rows(1)
                if m:
                    pe.wait_ge(d_tok, d0 - DPC + DC_ST)
                z_half(0)
                pe.wait_ge(d_tok, d0)
                for g in range(SG):
                    mm = nc.tensor.matmul(PS[:, 2 + g, :], BCT[1][64 * g:64 * g + 64, t],
                                          STATE[64 * g:64 * g + 64].rearrange("p h n -> p (h n)"), start=True, stop=True)
                mm.then_inc(p_tok, 1)
                y_diag(0)
                decay_rows(2)
                pe.wait_ge(a_tok, a0 + AC_Z[0])
                z_half(1)
                y_diag(1)
                decay_rows(3)
                y_diag(2)
                y_diag(3)
                pe.wait_ge(a_tok, a0 + AC_Z[1])
                for g in range(SG):
                    mm = nc.tensor.matmul(PS[64 * g:64 * g + 64, 5, :], BM[:, 64 * g:64 * g + 64],
                                          XDD[:, 8 * g:8 * g + 8, :].rearrange("p h n -> p (h n)"), start=True, stop=True)
                mm.then_inc(p_tok, 1)
                if m:
                    pe.wait_ge(n_h, Q_SSD + m)
                    pe_turn(pe, T_SSD + m - 1, V[:, m - 1, :])
            pe_pass_end(S_Z)
            pe_pass_end(S_Z + 1)
            pe.wait_ge(n_h, Q_SSD + MT)
            pe_turn(pe, T_SSD + MT - 1, V[:, MT - 1, :])

        def act_phase5(act):
            act.wait_ge(d_tok, D_S + 1)
            for t in (ECL, ECS):
                nc.scalar.activation(t[:], t[:], ACT.Exp)
            nc.scalar.activation(DEC[:], DEC[:], ACT.Exp).then_inc(a_tok, 1)
            for m in range(MT):
                d0, p0, a0 = D_S1 + DPC * m, P_S1 + PPC * m, A_S1 + APC * m

                def exp(q):
                    act.wait_ge(d_tok, d0 + DC_DIFF[q])
                    nc.scalar.activation(EX[q % 2][:], EX[q % 2][:], ACT.Exp).then_inc(a_tok, 1)

                def z_copy(n):
                    act.wait_ge(p_tok, p0 + PC_Z[n])
                    nc.scalar.activation(ZS[:, n * 512:(n + 1) * 512], PS[:, 5, :], ACT.Copy).then_inc(a_tok, 1)

                exp(0)
                exp(1)
                if m:
                    act.wait_ge(n_sq, sq_index(Q_SSD + m - 1))
                z_copy(0)
                exp(2)
                z_copy(1)
                exp(3)
                act.wait_ge(a_tok, a0 + AC_Z[1])
                nc.scalar.activation(ZS[:], ZS[:], ACT.Silu).then_inc(a_tok, 1)
                if m:
                    act_turn_hi(act, T_SSD + m - 1, m - 1)
                act.wait_ge(d_tok, d0 + DC_Y)
                act_square(Q_SSD + m, V[:, m, :], ZS[:])
            act_split(act, S_A)
            act_turn_hi(act, T_SSD + MT - 1, MT - 1)

        def dve_phase5(dve):
            ch = dve_chain
            dve.wait_ge(gain_in[1], 32)
            dve.wait_ge(p_tok, P_S + 1)
            ch.add(nc.vector.memset(STATE[:], 0.0))
            ch.add(nc.vector.tensor_copy(CSC[:].rearrange("p m h -> p (m h)"), PS[:, 0, 0:P]))
            ch.add(nc.vector.tensor_copy(ECL[:].rearrange("p m h -> p (m h)"), PS[:, 1, 0:P]))
            ch.wait()
            ch.step(nc.vector.tensor_copy(ECS[:], CSC[:]))
            nc.vector.tensor_tensor(DEC[:], ECL[:], CSC[:], ALU.subtract).then_inc(d_tok, 1)
            dve.wait_ge(a_tok, A_S1)
            ch.step(nc.vector.tensor_copy(ECL2[0:64], ECL[0:64, :, 0:8]))
            nc.vector.tensor_copy(ECL2[64:128], ECL[64:128, :, 8:16]).then_inc(d_tok, 1)
            for m in range(MT):
                d0, p0, a0 = D_S1 + DPC * m, P_S1 + PPC * m, A_S1 + APC * m
                dve.wait_ge(d_tok, d0)
                xs = V[:, m, :].rearrange("p (h n) -> p h n", h=H)
                nc.vector.tensor_tensor(XD[:], xs, head_bc(DT, m, HP), ALU.mult).then_inc(d_tok, 1)
                dve.wait_ge(d_tok, d0 + 1)
                nc.vector.tensor_tensor(XDD[:], XD[:], head_bc(DEC, m, HP), ALU.mult).then_inc(d_tok, 1)
                dve.wait_ge(p_tok, p0 + PC_CB)
                nc.vector.tensor_copy(BM[:], PS[:, 4, 2 * P:3 * P]).then_inc(d_tok, 1)
                for q in range(4):
                    e = EX[q % 2]
                    dve.wait_ge(p_tok, p0 + PC_DEC[q])
                    nc.vector.tensor_tensor(e[:], PS[:, 6 + q % 2, :].rearrange("p (i t) -> p i t", i=4),
                                            CSC[:, m, 4 * q:4 * q + 4].unsqueeze(2).to_broadcast([P, 4, P]),
                                            ALU.subtract).then_inc(d_tok, 1)
                    if q == 0 and m:
                        dve_scale(dve, Q_SSD + m - 1, V[:, m - 1, :], V[:, m - 1, :], GAM[1][:])
                    dve.wait_ge(a_tok, a0 + AC_EXP[q])
                    g = q // 2
                    nc.vector.tensor_tensor(e[:], e[:], PS[:, 4, g * P:(g + 1) * P].unsqueeze(1).to_broadcast([P, 4, P]),
                                            ALU.mult).then_inc(d_tok, 1)
                ch.step(nc.vector.tensor_tensor(STATE[:], STATE[:], ECL2[:, m, :].unsqueeze(2).to_broadcast([P, 8, HP]),
                                                ALU.mult))
                dve.wait_ge(p_tok, p0 + PC_ST)
                nc.vector.tensor_tensor(STATE[:], STATE[:], PS[:, 5, :].rearrange("p (h n) -> p h n", n=HP),
                                        ALU.add).then_inc(d_tok, 1)
                yo = PS[:, 2:4, :].rearrange("p b (h n) -> p (b h) n", n=HP)
                yd = PS[:, 0:2, :].rearrange("p b (h n) -> p (b h) n", n=HP)
                ch.step(nc.vector.tensor_tensor(XD[:], xs, HROW[:, 2, :].unsqueeze(2).to_broadcast([P, H, HP]), ALU.mult))
                ch.step(nc.vector.tensor_tensor(xs, yo, head_bc(ECS, m, HP), ALU.mult))
                ch.step(nc.vector.tensor_tensor(xs, yd, xs, ALU.add))
                ch.step(nc.vector.tensor_tensor(xs, xs, XD[:], ALU.add))
                dve.wait_ge(a_tok, a0 + AC_SILU)
                nc.vector.tensor_tensor(V[:, m, :], V[:, m, :], ZS[:], ALU.mult).then_inc(d_tok, 1)
                if m:
                    dve_turn_lo(dve, T_SSD + m - 1, m - 1)
                dve_mean(dve, Q_SSD + m)
            dve_scale(dve, Q_SSD + MT - 1, V[:, MT - 1, :], V[:, MT - 1, :], GAM[1][:])
            dve_split(dve, S_A)
            dve_turn_lo(dve, T_SSD + MT - 1, MT - 1)

        def pool_phase5(pool):
            for m in range(MT):
                pool_rstd(pool, Q_SSD + m)

        def sp_router_w(sp, layer):
            if layer:
                sp.wait_ge(r_mm, 8)
            sp.dma_start(WR[:, :, 0:EG], A["moe_w_group"][layer].rearrange("(c p) g -> p c g", p=P)).then_inc(wr_in, 16)
            sp.dma_start(WR[:, :, EG:], A["moe_w_expert"][layer].rearrange("(c p) g -> p c g", p=P)).then_inc(wr_in, 16)

        def sp_residual(sp, layer, n):
            src = A["x"][0] if layer == 0 else X2
            for m in range(MT):
                j = 8 * n + m
                if j >= 2:
                    sp.wait_ge(step_use, (U_O if layer else U_A) + j - 1)
                sp.dma_start(RES[m % 2][:], rows(src, m)[:, n * 512:(n + 1) * 512]).then_inc(res_in[m % 2], 16)

        def res_count(layer, j):
            return 16 * (8 * layer + j // 2 + 1)

        def sp_phase6(sp):
            sp_slice(sp, 10)
            sp.dma_start(GAM[0][:], A["norm_ffn"][0:1, :].to_broadcast([P, D])).then_inc(gain_in[0], 16)
            sp_router_w(sp, 0)
            sp_residual(sp, 0, 0)
            sp_slice(sp, 11)
            for m in range(MT):
                if m >= 2:
                    sp.wait_ge(n_tr, 2 * (T_SGU + m - 1))
                sp.dma_start(HM[m % 2][:], rows(YG, m)).then_inc(yg_in[m % 2], 16)
                j = 8 + m
                sp.wait_ge(step_use, U_A + j - 1)
                sp.dma_start(RES[m % 2][:], rows(A["x"][0], m)[:, 512:1024]).then_inc(res_in[m % 2], 16)
            sp_slice(sp, 12)

        def yg_count(m):
            return 16 * (m // 2 + 1)

        def pe_phase6(pe):
            for m in range(MT):
                pe_token_step(pe, 9, m, U_A + m, U_A)
            pe_pass_end(9)
            for m in range(MT):
                pe_token_step(pe, 10, m, U_A + 8 + m, U_A)
                pe.wait_ge(yg_in[m % 2], yg_count(m))
                pe_turn(pe, T_SGU + m, HM[m % 2])
            pe_pass_end(10)
            for m in range(MT):
                pe.wait_ge(n_lo, 2 * (T_SGU + m) + 2)
                pe_token_step(pe, 11, m, U_A + 16 + m, U_A)
            pe_pass_end(11)
            pe_last_pass(pe, 0, 12, U_A + 24, U_A)

        def pe_last_pass(pe, layer, s, u, u0):
            for m in range(MT + 2):
                if m < MT:
                    pe_token_step(pe, s, m, u + m, u0)
                if 1 <= m <= MT:
                    pe.wait_ge(n_h, Q_FFN[layer] + m)
                    pe_turn(pe, T_FFN[layer] + m - 1, HM[(m - 1) % 2])
                if m >= 2:
                    i = m - 2
                    if i == 0:
                        pe.wait_ge(wr_in, 32 * (layer + 1))
                    pe.wait_ge(n_hi, 2 * (T_FFN[layer] + i) + 2)
                    if 8 * layer + i:
                        pe.wait_ge(r_log, 8 * layer + i)
                    for k in range(KD):
                        mm = nc.tensor.matmul(PS[:, 5, 0:EG + NE], HTF[:, k, :], WR[:, k, :], start=(k == 0), stop=(k == KD - 1))
                    mm.then_inc(r_mm, 1)
            pe_pass_end(s)

        def act_last_pass(act, layer, u):
            for m in range(MT + 1):
                if m < MT:
                    act.wait_ge(step_use, u + m + 1)
                    if m >= 2:
                        act.wait_ge(n_tr, 2 * (T_FFN[layer] + m - 1))
                        act.wait_ge(h_st[m % 2], 16 * (4 * layer + m // 2))
                    act_square(Q_FFN[layer] + m, V[:, m, :], HM[m % 2][:])
                if m >= 1:
                    i = m - 1
                    if 8 * layer + i:
                        act.wait_ge(r_mm, 8 * layer + i)
                    for hb in range(2):
                        act.wait_ge(n_tr, 2 * (T_FFN[layer] + i) + hb + 1)
                        nc.scalar.activation(HTF[:, 4 * hb:4 * hb + 4, :], PS[:, 6 + hb, :].rearrange("p (c t) -> p c t", c=4),
                                             ACT.Copy).then_inc(n_hi, 1)

        def dve_last_pass(dve, layer, u, add):
            dve.wait_ge(gain_in[0], 48 + 16 * layer)
            for m in range(MT + 2):
                if m < MT:
                    add(m)
                if 1 <= m <= MT:
                    dve_scale(dve, Q_FFN[layer] + m - 1, V[:, m - 1, :], HM[(m - 1) % 2][:], GAM[0][:])
                if m < MT:
                    dve_mean(dve, Q_FFN[layer] + m)
                if m >= 2:
                    i = m - 2
                    dve.wait_ge(r_mm, 8 * layer + i + 1)
                    nc.vector.tensor_tensor(LOG[:, i, :], PS[:, 5, 0:EG + NE], RB[:, layer, :], ALU.add).then_inc(r_log, 1)

        def pool_last_pass(pool, layer, u):
            for m in range(MT + 1):
                if m < MT:
                    pool_rstd(pool, Q_FFN[layer] + m)
                    pool.dma_start(rows(XM, m), V[:, m, :]).then_inc(xm_st, 16)
                if m >= 1:
                    pool.wait_ge(n_h, Q_FFN[layer] + m)
                    pool.dma_start(rows(HD, m - 1), HM[(m - 1) % 2][:]).then_inc(h_st[(m - 1) % 2], 16)
            pool.wait_ge(xm_st, 16 * 8 * (layer + 1))
            for i in range(2):
                pool.wait_ge(h_st[i], 16 * 4 * (layer + 1))

        def dve_add_res(dve, layer, m, n, u, u0):
            j = 8 * n + m
            dve.wait_ge(step_mm, u + 1)
            dve.wait_ge(res_in[m % 2], res_count(layer, j))
            nc.vector.tensor_tensor(V[:, m, n * 512:(n + 1) * 512], PS[:, (u - u0) % 4, :], RES[m % 2][:],
                                    ALU.add).then_inc(step_use, 1)

        def act_phase6(act):
            act_split(act, 10)
            act_split(act, 11)
            for m in range(MT):
                act.wait_ge(step_mm, U_A + 8 + m + 1)
                act_turn_hi(act, T_SGU + m, m)
            act_split(act, 12)
            act_last_pass(act, 0, U_A + 24)

        def dve_phase6(dve):
            dve_split(dve, 10)
            for m in range(MT):
                dve_add_res(dve, 0, m, 0, U_A + m, U_A)
            dve_split(dve, 11)
            for m in range(MT):
                dve_add_res(dve, 0, m, 1, U_A + 8 + m, U_A)
                dve_turn_lo(dve, T_SGU + m, m)

            def add(n, m):
                u = U_A + 16 + 8 * n + m
                dve.wait_ge(step_mm, u + 1)
                sl = V[:, m, n * 512:(n + 1) * 512]
                nc.vector.tensor_tensor(sl, PS[:, (u - U_A) % 4, :], sl, ALU.add).then_inc(step_use, 1)

            dve_split(dve, 12)
            for m in range(MT):
                dve.wait_ge(step_use, U_A + 9 + m)
                add(0, m)
            dve_last_pass(dve, 0, U_A + 24, lambda m: add(1, m))

        def pool_phase6(pool):
            pool_last_pass(pool, 0, U_A + 24)

        OV_R, OP_R = 0, 0
        P_R = (P_S1 + PPC * MT, P_S1 + PPC * MT + 2)
        D_R = (D_S1 + DPC * MT, D_S1 + DPC * MT + 4)
        A_R = (A_S1 + APC * MT, A_S1 + APC * MT + 1)

        def act_route(act, layer):
            act.wait_ge(d_tok, D_R[layer] + 1)
            nc.scalar.activation(TMP[:], TMP[:], ACT.Exp)
            nc.scalar.activation(BK[:, :, 0:1], BK[:, :, 0:1], ACT.Exp).then_inc(a_tok, 1)

        def pe_route(pe, layer):
            pe.wait_ge(d_tok, D_R[layer] + 2)
            for i in range(MT - 1):
                nc.tensor.matmul(PS[:, 0, (i + 1) * NE:MT * NE].rearrange("p (m e) -> p m e", e=NE), ONES,
                                 MM[:, i, :].unsqueeze(1).to_broadcast([P, MT - 1 - i, NE]), start=(i == 0), stop=False,
                                 skip_group_check=True)
            nc.tensor.matmul(PS[:, 0, 0:MT * NE], USTR, MM[:].rearrange("p m e -> p (m e)"), start=False, stop=True,
                             skip_group_check=True)
            for i in range(MT):
                mm = nc.tensor.matmul(PS[:, 1, 0:NE], ONES, MM[:, i, :], start=(i == 0), stop=(i == MT - 1))
            mm.then_inc(p_tok, 1)
            for i in range(2 * MT):
                m, k = divmod(i, 2)
                pe.wait_ge(o_v[layer], OV_R + i + 1)
                mm = nc.tensor.matmul(PS[:, 2, 0:NE], PH[:, i % 4, :], OT[:, k, m, :], start=(i == 0), stop=(i == 2 * MT - 1))
                if i < 2 * MT - 1:
                    mm.then_inc(o_p[layer], 1)
            mm.then_inc(p_tok, 1)

        def dve_route(dve, layer):
            ch = dve_chain
            d = D_R[layer]
            bc3 = lambda a, n: a.to_broadcast([P, MT, n])
            ch.add(nc.vector.memset(G8[:, :, EG:], -BIG))
            ch.add(nc.vector.tensor_copy(G8[:, :, 0:EG], LOG[:, :, 0:EG]))
            ch.wait()
            for m in range(MT):
                ch.add(nc.vector.max(GV[:, m, :], G8[:, m, :]))
            ch.wait()
            for m in range(MT):
                ch.add(nc.vector.max_index(GI[:, m, :], GV[:, m, :], G8[:, m, :]))
            ch.wait()
            ch.step(nc.vector.tensor_copy(GIF[:], GI[:, :, 0:1]))
            ch.add(nc.vector.tensor_tensor(TMP[:], LOG[:, :, 0:EG], bc3(GV[:, :, 0:1], EG), ALU.subtract))
            ch.step(nc.vector.tensor_tensor(GM[:], IOTA[:, 0:EG].unsqueeze(1).to_broadcast([P, MT, EG]), bc3(GIF[:], EG),
                                            ALU.is_equal))
            ch.step(nc.vector.tensor_scalar(GM[:], GM[:], BIG, -BIG, ALU.mult, ALU.add))
            ch.step(nc.vector.tensor_tensor(EL[:].rearrange("p m (g e) -> p m g e", g=EG),
                                            LOG[:, :, EG:].rearrange("p m (g e) -> p m g e", g=EG),
                                            GM[:].unsqueeze(3).to_broadcast([P, MT, EG, GE]), ALU.add))
            for m in range(MT):
                ch.add(nc.vector.max(EV[:, m, :], EL[:, m, :]))
            ch.wait()
            for m in range(MT):
                ch.add(nc.vector.max_index(EI[:, m, :], EV[:, m, :], EL[:, m, :]))
            ch.add(nc.vector.tensor_tensor(BK[:, :, 0:1], EV[:, :, 1:2], EV[:, :, 0:1], ALU.subtract))
            ch.wait()
            nc.vector.tensor_copy(EIF[:], EI[:, :, 0:2]).then_inc(d_tok, 1)
            dve.wait_ge(d_tok, d + 1)
            for k in range(2):
                ch.add(nc.vector.tensor_tensor(OH[:, k], IOTA[:, 0:NE].unsqueeze(1).to_broadcast([P, MT, NE]),
                                               bc3(EIF[:, :, k:k + 1], NE), ALU.is_equal))
            ch.wait()
            nc.vector.tensor_tensor(MM[:], OH[:, 0], OH[:, 1], ALU.add).then_inc(d_tok, 1)
            for k in range(2):
                ch.add(nc.vector.tensor_tensor(OT[:, k], OH[:, k], TOKID.unsqueeze(2).to_broadcast([P, MT, NE]), ALU.mult))
            dve.wait_ge(a_tok, A_R[layer] + 1)
            ch.step(nc.vector.tensor_reduce(DEN[:, :, 0:1], TMP[:], AX, ALU.add))
            ch.step(nc.vector.tensor_scalar(DEN[:, :, 1:2], BK[:, :, 0:1], 1.0, None, ALU.add))
            ch.step(nc.vector.tensor_tensor(DEN[:, :, 2:3], DEN[:, :, 0:1], DEN[:, :, 1:2], ALU.mult))
            ch.step(nc.vector.reciprocal(GATE[:, :, 0:1], DEN[:, :, 2:3]))
            ch.step(nc.vector.tensor_tensor(GATE[:, :, 1:2], GATE[:, :, 0:1], BK[:, :, 0:1], ALU.mult))
            dve.wait_ge(p_tok, P_R[layer] + 1)
            pos = PS[:, 0, 0:MT * NE].rearrange("p (m e) -> p m e", e=NE)
            for k in range(2):
                ch.step(nc.vector.tensor_tensor(PR[:], pos, OH[:, k], ALU.mult))
                ch.step(nc.vector.tensor_reduce(POSK[:, :, k:k + 1], PR[:], AX, ALU.add))
            for i in range(2 * MT):
                m, k = divmod(i, 2)
                if i >= 4:
                    dve.wait_ge(o_p[layer], OP_R + i - 3)
                nc.vector.tensor_scalar(PH[:, i % 4, :], IOTA, POSK[:, m, k:k + 1], None, ALU.is_equal).then_inc(o_v[layer], 1)
            ch.step(nc.vector.tensor_copy(NOV[:, 0, :], PS[:, 1, 0:NE]))
            ch.step(nc.vector.tensor_tensor(CMP[:], NOV[:, 0, :].unsqueeze(2).to_broadcast([P, NE, 7]),
                                            THRESH.unsqueeze(1).to_broadcast([P, NE, 7]), ALU.is_gt))
            ch.step(nc.vector.tensor_reduce(NOV[:, 1, :], CMP[:], AX, ALU.add))
            ch.step(nc.vector.tensor_tensor_scan(NOV[:, 2, :], ONES[:, 0:NE], NOV[:, 1, :], 0.0, ALU.mult, ALU.add))
            ch.step(nc.vector.tensor_tensor(CMS[:], NOV[:, 2, :].unsqueeze(1).to_broadcast([P, OVF, NE]),
                                            SLOTI.unsqueeze(2).to_broadcast([P, OVF, NE]), ALU.is_le))
            ch.step(nc.vector.tensor_reduce(ESL[:, 0:OVF], CMS[:], AX, ALU.add))
            ch.step(nc.vector.tensor_scalar(ESL[:, 0:OVF], ESL[:, 0:OVF], float(NE - 1), None, ALU.min))
            ch.step(nc.vector.tensor_copy(ESL[:, OVF:OVF + 1], NOV[:, 2, NE - 1:NE]))
            nc.vector.tensor_copy(REGS[:], ESL[:]).then_inc(d_tok, 1)
            ch.step(nc.vector.tensor_tensor(NOV[:, 0, :], NOV[:, 2, :], NOV[:, 1, :], ALU.subtract))
            ch.step(nc.vector.tensor_scalar(NOV[:, 0, :], NOV[:, 0, :], float(BLK), float((NE - 1) * BLK), ALU.mult, ALU.add))
            for k in range(2):
                ch.step(nc.vector.tensor_tensor(PR[:], OH[:, k], NOV[:, 0, :].unsqueeze(1).to_broadcast([P, MT, NE]), ALU.mult))
                ch.step(nc.vector.tensor_reduce(BK[:, :, k:k + 1], PR[:], AX, ALU.add))
            ch.step(nc.vector.tensor_scalar(EIF[:], EIF[:], float(BLK), None, ALU.mult))
            ch.step(nc.vector.tensor_tensor(BK[:], BK[:], EIF[:], ALU.subtract))
            ch.step(nc.vector.tensor_scalar(VPOS[:], POSK[:], float(BLK), None, ALU.is_ge))
            ch.step(nc.vector.tensor_tensor(BK[:], BK[:], VPOS[:], ALU.mult))
            ch.step(nc.vector.tensor_tensor(BK[:], BK[:], EIF[:], ALU.add))
            ch.step(nc.vector.tensor_tensor(BK[:], BK[:], POSK[:], ALU.add))
            ch.step(nc.vector.tensor_copy(ROWI[:], BK[:]))
            nc.vector.tensor_scalar(VPOS[:], BK[:], -float(NE * BLK), None, ALU.add).then_inc(dve_loop[layer], 1)
            dve.wait_ge(p_tok, P_R[layer] + 2)
            nc.vector.tensor_copy(IDXA[:], PS[:, 2, 0:NE]).then_inc(d_tok, 1)


        UNITS, HALF = 6 * NE, NE // 2

        def unit(i, par, j):
            if isinstance(i, int) and 2 * i + par == 0:
                return j, j, 0
            if isinstance(i, int) and i == HALF:
                n = UNITS - 2 + j
                return n, n % 12, n // 12
            if par:
                return i * 12 + (4 + j), (4 + j) % 12, i + (4 + j) // 12
            return i * 12 + (j - 2), (10 + j) % 12, i + ((10 + j) // 12 - 1)

        def part(i, par, j):
            return unit(i if isinstance(i, int) else 1, par, j)[0] % 4

        def raw_base(layer, slot):
            return 16 * (N_SL0 + (len(SLICES) - N_SL0 + 16) * layer) if slot < 2 else 16 * 16 * layer

        def sp_moe_loads(sp, layer, i, par, j0, j1):
            e = i * 2 + par
            for j in range(j0, j1):
                n, slot, _ = unit(i, par, j)
                if not isinstance(n, int) or n >= 12:
                    sp.wait_ge(m_lo, n + (UNITS * layer - 11))
                if j < 4 and not (isinstance(i, int) and i == HALF):
                    w = A["moe_w1" if j < 2 else "moe_w3"][layer][bass.ds(e, 1)]
                    src = w.rearrange("o (h c p) n -> (o h) p c n", p=P, c=4)[j % 2]
                else:
                    w = A["moe_w2"][layer][bass.ds(e - 1, 1)]
                    src = w.rearrange("o (c p) (h n) -> (o h) p c n", p=P, n=512)[j % 2]
                sp.dma_start(MRAW[slot][:], src).then_inc(raw_in[slot], 16)

        def sp_moe_store(sp, layer, i, par):
            f = i * 2 + par
            sp.wait_ge(m_yev, f * 2 + (2 * NE * layer + 2))
            sp.dma_start(YB[bass.ds(f * BLK, BLK), :], YSB[par][:]).then_inc(y_st[par], 16)

        def sp_moe_prefetch(sp, layer):
            slices = len(SLICES) if layer else N_SL0
            sp.wait_ge(w_lo_done, 2 * slices)
            sp_moe_loads(sp, layer, 0, 0, 0, 2)
            sp.wait_ge(pass_done, slices)
            sp_moe_loads(sp, layer, 0, 0, 2, 4)
            sp_moe_loads(sp, layer, 0, 1, 0, 6)

        def sp_moe(sp, layer):
            if layer == 0:
                sp.wait_ge(n_h, Q_SSD + MT)
                sp.dma_start(GAM[1][:], A["norm_mix"][1:2, :].to_broadcast([P, D])).then_inc(gain_in[1], 16)
            else:
                sp.dma_start(GAM[1][:], A["norm_final"].rearrange("(o n) -> o n", o=1).to_broadcast([P, D]))\
                    .then_inc(gain_in[1], 16)
            for par in range(2):
                sp_moe_loads(sp, layer, 1, par, 0, 6)
            with sp.Fori(2, HALF) as i:
                for par in range(2):
                    sp_moe_loads(sp, layer, i, par, 0, 6)
                    sp_moe_store(sp, layer, i - 2, par)
            sp_moe_loads(sp, layer, HALF, 0, 0, 2)
            for f in range(NE - 4, NE):
                sp_moe_store(sp, layer, f // 2, f % 2)

        def pe_moe(pe, layer):
            c1, c2, cu = NE * layer, 2 * NE * layer, UNITS * layer

            def unit_products(i, par, j, o, lh, ll, k0, first, last):
                pe.wait_ge(m_lo, unit(i, par, j)[0] + (cu + 1))
                slot = part(i, par, j)
                for c in range(4):
                    mm = three(o, lh[:, k0 + c, :], ll[:, k0 + c, :], WHI[:, slot, c, :], WLO[:, slot, c, :],
                               first and c == 0, last and c == 3)
                mm.then_inc(m_unit, 1)

            def turn_x(i, par):
                pe.wait_ge(xg_in[par], i * 16 + 16 * (HALF * layer + 1))
                pe.wait_ge(m_xlo, i * 4 + (2 * par + c2))
                for hb in range(2):
                    for c in range(4):
                        k = 4 * hb + c
                        t = nc.tensor.transpose(PS[:, 5 + hb, c * P:(c + 1) * P], XG[par][:, k * P:(k + 1) * P], IDENT)
                    t.then_inc(m_xtr, 1)

            def up(i, par):
                pe.wait_ge(m_xlo, i * 4 + (2 * par + 2 + c2))
                pe.wait_ge(m_gmul, i * 2 + (par + c1))
                for j in range(4):
                    unit_products(i, par, j, PS[:, j // 2, :], XTH, XTL, 4 * (j % 2), j % 2 == 0, j % 2 == 1)

            def down(i, par, j0):
                pe.wait_ge(m_glo, i * 2 + (par + c1))
                pe.wait_ge(m_yev, i * 4 + (2 * par - 2 + c2))
                for h in range(2):
                    unit_products(i, par, j0 + h, PS[:, 3 + h, :], GTH, GTL, 0, True, True)

            def turn_g(i, par):
                pe.wait_ge(m_gmul, i * 2 + (par + 1 + c1))
                for c in range(4):
                    t = nc.tensor.transpose(PS[:, 2, c * P:(c + 1) * P], GAT[:, c * P:(c + 1) * P], IDENT)
                t.then_inc(m_gtr, 1)

            turn_x(0, 0)
            up(0, 0)
            turn_x(0, 1)
            turn_g(0, 0)
            up(0, 1)
            turn_x(1, 0)
            down(0, 1, 4)
            turn_g(0, 1)
            with pe.Fori(1, HALF - 1) as i:
                up(i, 0)
                turn_x(i, 1)
                down(i, 0, 4)
                turn_g(i, 0)
                up(i, 1)
                turn_x(i + 1, 0)
                down(i, 1, 4)
                turn_g(i, 1)
            i = HALF - 1
            up(i, 0)
            turn_x(i, 1)
            down(i, 0, 4)
            turn_g(i, 0)
            up(i, 1)
            down(i, 1, 4)
            turn_g(i, 1)
            down(HALF, 0, 0)

        def act_moe(act, layer):
            c1, c2, cu = NE * layer, 2 * NE * layer, UNITS * layer

            def hi(i, par, j):
                n, slot, lap = unit(i, par, j)
                act.wait_ge(raw_in[slot], lap * 16 + (raw_base(layer, slot) + 16))
                if not isinstance(n, int) or n >= 4:
                    act.wait_ge(m_unit, n + (cu - 3))
                nc.scalar.activation(WHI[:, part(i, par, j)], MRAW[slot][:], ACT.Copy).then_inc(m_hi, 1)

            def x_hi(i, par):
                for hb in range(2):
                    act.wait_ge(m_xtr, i * 4 + (2 * par + hb + 1 + c2))
                    nc.scalar.activation(XTH[:, 4 * hb:4 * hb + 4, :], PS[:, 5 + hb, :].rearrange("p (c t) -> p c t", c=4),
                                         ACT.Copy).then_inc(m_xhi, 1)

            def g_hi(i, par):
                act.wait_ge(m_gtr, i * 2 + (par + c1))
                nc.scalar.activation(GTH[:], PS[:, 2, :].rearrange("p (c t) -> p c t", c=4), ACT.Copy).then_inc(m_ghi, 1)

            def y_out(i, par, j0):
                si, sp_ = (i, 0) if par else (i - 1, 1)
                if not isinstance(i, int) or i + HALF * layer > 1:
                    act.wait_ge(y_st[par], i * 16 + 16 * (HALF * layer - 1))
                for h in range(2):
                    act.wait_ge(m_unit, unit(si, sp_, j0 + h)[0] + (cu + 1))
                    nc.scalar.activation(YSB[par][:, h * 512:(h + 1) * 512], PS[:, 3 + h, :], ACT.Copy).then_inc(m_yev, 1)

            def silu(i, par):
                act.wait_ge(m_unit, unit(i, par, 1)[0] + (cu + 1))
                act.wait_ge(m_gmul, i * 2 + (par + c1))
                nc.scalar.activation(SIL[:], PS[:, 0, :], ACT.Silu).then_inc(m_silu, 1)

            def step(i, par):
                e = 2 * i + par if isinstance(i, int) else NE
                hi(i, par, 0)
                hi(i, par, 1)
                x_hi(i, par)
                hi(i, par, 2)
                hi(i, par, 3)
                if e >= 1:
                    g_hi(i, par)
                if e >= 2:
                    y_out(i, par, 4)
                if e >= 1:
                    hi(i, par, 4)
                    hi(i, par, 5)
                silu(i, par)

            step(0, 0)
            step(0, 1)
            step(1, 0)
            step(1, 1)
            with act.Fori(2, HALF) as i:
                step(i, 0)
                step(i, 1)
            g_hi(HALF, 0)
            y_out(HALF, 0, 4)
            hi(HALF, 0, 0)
            hi(HALF, 0, 1)
            y_out(HALF, 1, 0)

        def dve_moe(dve, layer):
            c1, c2, cu = NE * layer, 2 * NE * layer, UNITS * layer

            def lo(i, par, j):
                n, slot, _ = unit(i, par, j)
                dve.wait_ge(m_hi, n + (cu + 1))
                q = part(i, par, j)
                nc.vector.tensor_tensor(WLO[:, q], MRAW[slot][:], WHI[:, q].bitcast(F32), ALU.subtract).then_inc(m_lo, 1)

            def x_lo(i, par):
                for hb in range(2):
                    dve.wait_ge(m_xhi, i * 4 + (2 * par + hb + 1 + c2))
                    sl = (slice(None), slice(4 * hb, 4 * hb + 4))
                    nc.vector.tensor_tensor(XTL[sl], PS[:, 5 + hb, :].rearrange("p (c t) -> p c t", c=4),
                                            XTH[sl].bitcast(F32), ALU.subtract).then_inc(m_xlo, 1)

            def g_lo(i, par):
                dve.wait_ge(m_ghi, i * 2 + (par + c1))
                nc.vector.tensor_tensor(GTL[:], PS[:, 2, :].rearrange("p (c t) -> p c t", c=4), GTH[:].bitcast(F32),
                                        ALU.subtract).then_inc(m_glo, 1)

            def gate(i, par):
                si, sp_ = (i, 0) if par else (i - 1, 1)
                dve.wait_ge(m_silu, i * 2 + (par + c1))
                dve.wait_ge(m_unit, unit(si, sp_, 3)[0] + (cu + 1))
                dve.wait_ge(m_gtr, i * 2 + (par - 1 + c1))
                nc.vector.tensor_tensor(GAT[:], SIL[:], PS[:, 1, :], ALU.mult).then_inc(m_gmul, 1)

            def step(i, par):
                e = 2 * i + par if isinstance(i, int) else NE
                lo(i, par, 0)
                lo(i, par, 1)
                if e >= 1:
                    gate(i, par)
                x_lo(i, par)
                lo(i, par, 2)
                lo(i, par, 3)
                if e >= 1:
                    g_lo(i, par)
                    lo(i, par, 4)
                    lo(i, par, 5)

            step(0, 0)
            step(0, 1)
            with dve.Fori(1, HALF) as i:
                step(i, 0)
                step(i, 1)
            gate(HALF, 0)
            g_lo(HALF, 0)
            lo(HALF, 0, 0)
            lo(HALF, 0, 1)

        def pool_moe(pool, layer):
            c2 = 2 * NE * layer

            def gather(i, par):
                e = i * 2 + par
                if not isinstance(i, int) or e >= 2:
                    pool.wait_ge(m_xtr, i * 4 + (2 * par - 2 + c2))
                pool.wait_ge(d_tok, D_R[layer] + 4)
                nc.gpsimd.tensor_copy(CUR[par][:, 0:1], IDXA[:, bass.ds(e, 1)]).then_inc(cur_set, 1)
                pool.wait_ge(cur_set, e + (NE * layer + 1))
                pool.sem_inc(gather_go, 1)
                pool.indirect_dma_start(out=XG[par][:], out_offset=None, in_=HD[:, :],
                                        in_offset=bass.IndirectOffsetOnAxis(ap=CUR[par][:, 0:1], axis=0))\
                    .then_inc(xg_in[par], 16)

            gather(0, 0)
            gather(0, 1)
            with pool.Fori(1, HALF) as i:
                gather(i, 0)
                gather(i, 1)

        OV_B, OP_B = OV_R + 2 * MT, OP_R + 2 * MT - 1
        O_UNITS = [MRAW[2 + i] for i in range(6)]

        def ovf_loop(eng, body, each=None):
            n = eng.value_load(REGS[0:1, OVF:OVF + 1], min_val=0, max_val=OVF)
            with eng.If(n > 0):
                body(0)
                if each:
                    each(0)
                with eng.If(n > 1):
                    with eng.Fori(1, OVF) as s:
                        with eng.If(n > s):
                            body(s)
                        if each:
                            each(s)

        def sp_ovf(sp, layer):
            sp.wait_ge(m_lo, UNITS * (layer + 1))
            if layer == 0:
                sp.wait_ge(zero_st, 16 * OVF)

            def body(s):
                sp.wait_ge(o_p[layer], s * 5 + OP_B)
                e = sp.value_load(REGS[0:1, bass.ds(s, 1)], min_val=0, max_val=NE - 1)
                for i, name in enumerate(("moe_w1", "moe_w3")):
                    w = A[name][layer][bass.ds(e, 1)].rearrange("o (h c p) n -> (o h) p c n", p=P, c=4)
                    for h in range(2):
                        sp.dma_start(O_UNITS[2 * i + h][:], w[h]).then_inc(o_raw[layer], 16)
                w = A["moe_w2"][layer][bass.ds(e, 1)].rearrange("o (c p) (h n) -> (o h) p c n", p=P, n=512)
                for h in range(2):
                    sp.dma_start(O_UNITS[4 + h][:], w[h]).then_inc(o_raw[layer], 16)
                sp.wait_ge(o_v[layer], s * 6 + (OV_B + 6))
                sp.dma_start(YB[bass.ds((s + NE) * BLK, BLK), :], OY[:]).then_inc(o_yst[layer], 16)

            ovf_loop(sp, body)

        def pool_ovf(pool, layer):
            def body(s):
                pool.wait_ge(o_v[layer], s * 6 + (OV_B + 2))
                pool.sem_inc(gather_go, 1)
                pool.indirect_dma_start(out=OXG[:], out_offset=None, in_=HD[:, :],
                                        in_offset=bass.IndirectOffsetOnAxis(ap=OIDX[:, 0:1], axis=0)).then_inc(o_xg[layer], 16)
                pool.wait_ge(o_yst[layer], s * 16 + 16)

            ovf_loop(pool, body)

        def pe_ovf(pe, layer):
            def body(s):
                ov = s * 6 + OV_B
                pe.wait_ge(o_v[layer], ov + 1)
                for i in range(2 * MT):
                    mm = nc.tensor.matmul(PS[:, 2, 0:1], OHB[:, i, :], TOKID[:, i // 2:i // 2 + 1], start=(i == 0),
                                          stop=(i == 2 * MT - 1))
                mm.then_inc(o_p[layer], 1)
                pe.wait_ge(o_xg[layer], s * 16 + 16)
                for k in range(KD):
                    mm = nc.tensor.transpose(PS[:, 5 + k // 4, k % 4 * P:(k % 4 + 1) * P], OXG[:, k * P:(k + 1) * P], IDENT)
                mm.then_inc(o_p[layer], 1)
                pe.wait_ge(o_v[layer], ov + 3)
                pe.wait_ge(o_raw[layer], s * 96 + 96)
                for i in range(2):
                    for k in range(KD):
                        mm = nc.tensor.matmul(PS[:, i, :], OXT[:, k, :], O_UNITS[2 * i + k // 4][:, k % 4, :], start=(k == 0),
                                              stop=(k == KD - 1))
                mm.then_inc(o_p[layer], 1)
                pe.wait_ge(o_v[layer], ov + 4)
                for c in range(4):
                    mm = nc.tensor.transpose(PS[:, 2, c * P:(c + 1) * P], OGAT[:, c * P:(c + 1) * P], IDENT)
                mm.then_inc(o_p[layer], 1)
                pe.wait_ge(o_v[layer], ov + 5)
                for h in range(2):
                    for c in range(4):
                        mm = nc.tensor.matmul(PS[:, 3 + h, :], OGT[:, c, :], O_UNITS[4 + h][:, c, :], start=(c == 0), stop=(c == 3))
                mm.then_inc(o_p[layer], 1)

            ovf_loop(pe, body)

        def act_ovf(act, layer):
            def body(s):
                act.wait_ge(o_p[layer], s * 5 + (OP_B + 3))
                nc.scalar.activation(OSIL[:], PS[:, 0, :], ACT.Silu).then_inc(o_a[layer], 1)

            ovf_loop(act, body)

        def dve_ovf(dve, layer):
            def body(s):
                op = s * 5 + OP_B
                dve.wait_ge(dve_loop[layer], s + 1)
                nc.vector.tensor_tensor(OHB[:], IOTA.unsqueeze(1).to_broadcast([P, 2 * MT, P]),
                                        VPOS[:].rearrange("p m k -> p (m k)").unsqueeze(2).to_broadcast([P, 2 * MT, P]),
                                        ALU.is_equal).then_inc(o_v[layer], 1)
                dve.wait_ge(o_p[layer], op + 1)
                nc.vector.tensor_copy(OIDX[:], PS[:, 2, 0:1]).then_inc(o_v[layer], 1)
                dve.wait_ge(o_p[layer], op + 2)
                nc.vector.tensor_copy(OXT[:].rearrange("p k t -> p (k t)"), two_banks(5)).then_inc(o_v[layer], 1)
                dve.wait_ge(o_a[layer], s + 1)
                nc.vector.tensor_tensor(OGAT[:], OSIL[:], PS[:, 1, :], ALU.mult).then_inc(o_v[layer], 1)
                dve.wait_ge(o_p[layer], op + 4)
                nc.vector.tensor_copy(OGT[:].rearrange("p c t -> p (c t)"), PS[:, 2, :]).then_inc(o_v[layer], 1)
                dve.wait_ge(o_p[layer], op + 5)
                nc.vector.tensor_copy(OY[:], two_banks(3)).then_inc(o_v[layer], 1)

            def each(s):
                dve.wait_ge(dve_loop[layer], s + 1)
                nc.vector.tensor_scalar(VPOS[:], VPOS[:], -float(BLK), None, ALU.add).then_inc(dve_loop[layer], 1)

            ovf_loop(dve, body, each)

        Q_NEXT = (Q_MIX1, Q_FIN)

        def sp_combine(sp, layer):
            for m in range(MT + 2):
                if m < MT:
                    if m >= 4:
                        sp.wait_ge(n_h, Q_NEXT[layer] + m - 3)
                        if layer == 0:
                            sp.wait_ge(x2_st[m % 4], 16)
                    sp.dma_start(CX[m % 4][:], rows(XM, m)).then_inc(cx_in[m % 4], 16)
                if m >= 2:
                    i = m - 2
                    if layer == 0:
                        sp.wait_ge(c_add, 2 * i + 2)
                        sp.dma_start(rows(X2, i), CX[i % 4][:]).then_inc(x2_st[i % 4], 16)
                    else:
                        sp.wait_ge(n_h, Q_FIN + i + 1)
                        sp.dma_start(rows(out, i), HN[i % 2][:]).then_inc(out_st[i % 2], 16)
            for st, n in ([(s, 2) for s in x2_st] if layer == 0 else [(s, 4) for s in out_st]):
                sp.wait_ge(st, 16 * n)

        def pool_combine(pool, layer):
            for i in range(2):
                pool.wait_ge(y_st[i], 16 * HALF * (layer + 1))
            for i in range(2 * MT + 4):
                if i < 2 * MT:
                    m, k = divmod(i, 2)
                    if i >= 4:
                        pool.wait_ge(c_add, 2 * MT * layer + i - 3)
                    pool.indirect_dma_start(out=CY[i % 4][:], out_offset=None, in_=YB[:, :],
                                            in_offset=bass.IndirectOffsetOnAxis(ap=ROWI[:, m, k:k + 1], axis=0))\
                        .then_inc(cy_in[i % 4], 16)
                if i >= 4 and i % 2 == 1:
                    pool_rstd(pool, Q_NEXT[layer] + (i - 5) // 2)

        def dve_combine(dve, layer):
            q0 = Q_NEXT[layer]
            dve.wait_ge(gain_in[1], 48 + 16 * layer)

            def scale(m):
                if m >= 2:
                    if layer == 0:
                        dve.wait_ge(n_tr, 2 * (T_MIX1 + m - 1))
                    else:
                        dve.wait_ge(out_st[m % 2], 16 * (m // 2))
                dve_scale(dve, q0 + m, CX[m % 4][:], HN[m % 2][:], GAM[1][:])

            for m in range(MT + 2):
                if m < MT:
                    dve.wait_ge(cx_in[m % 4], 16 * (2 * layer + m // 4 + 1))
                    for k in range(2):
                        i = 2 * m + k
                        dve.wait_ge(cy_in[i % 4], 16 * (4 * layer + i // 4 + 1))
                        if k:
                            dve.wait_ge(c_add, 2 * MT * layer + i)
                        nc.vector.scalar_tensor_tensor(out=CX[m % 4][:], in0=CY[i % 4][:], scalar=GATE[:, m, k:k + 1],
                                                       in1=CX[m % 4][:], op0=ALU.mult, op1=ALU.add).then_inc(c_add, 1)
                if 1 <= m <= MT:
                    dve_mean(dve, q0 + m - 1)
                if 1 <= m <= MT:
                    scale(m - 1)
                if layer == 0 and m >= 2:
                    dve_turn_lo(dve, T_MIX1 + m - 2, m - 2)
            if layer == 0:
                dve_split(dve, S_I)

        def act_combine(act, layer):
            if layer == 0:
                act_split(act, S_I)
            for m in range(MT + 1):
                if m < MT:
                    act.wait_ge(c_add, 2 * MT * layer + 2 * m + 2)
                    if m >= 2:
                        if layer == 0:
                            act.wait_ge(n_tr, 2 * (T_MIX1 + m - 1))
                        else:
                            act.wait_ge(out_st[m % 2], 16 * (m // 2))
                    act_square(Q_NEXT[layer] + m, CX[m % 4][:], HN[m % 2][:])
                if layer == 0 and m >= 1:
                    act_turn_hi(act, T_MIX1 + m - 1, m - 1)

        def pe_combine(pe, layer):
            if layer == 0:
                for m in range(MT):
                    pe.wait_ge(n_h, Q_MIX1 + m + 1)
                    pe_turn(pe, T_MIX1 + m, HN[m % 2])

        def ident_n(t):
            return 1 if t == 0 else 6 * t - 4

        def lru_n(t, i):
            return min(t + 2, KD) + 5 * t + i

        def sp_phase11(sp):
            sp_slice(sp, 14)
            sp.wait_ge(phase_s, 4 * 10)
            for t in range(4):
                sp_gate_w(sp, t)
            for s in (15, 16, 17):
                sp_slice(sp, s)
            sp_router_w(sp, 1)
            for t in range(4, KD):
                sp_gate_w(sp, t)
            sp_slice(sp, 18)

        def sp_gate_w(sp, t):
            if t >= 4:
                sp.wait_ge(l_p, 2 * (t - 4) + 2)
            for i, n in enumerate(("od_w_a", "od_w_i")):
                sp.dma_start(LW[:, t % 4, i, :], A[n][0, t]).then_inc(l_w[t % 4], 16)

        def pe_phase11(pe):
            for j in range(2 * KD + 1):
                if j < 2 * KD:
                    s = S_I + j // 4
                    pe_chan_step(pe, s, j % 4, U_I + j, U_I)
                    if j % 4 == 3:
                        pe_pass_end(s)
                if j >= KD + 1:
                    t = j - KD - 1
                    pe.wait_ge(l_w[t % 4], 32 * (t // 4 + 1))
                    pe.wait_ge(step_use, U_I + KD + t + 1)
                    if t:
                        pe.wait_ge(l_a, lru_n(t - 1, 2))
                    for i in range(2):
                        for nh in range(2):
                            mm = nc.tensor.matmul(PS[:, 4 + 2 * i + nh, :], LW[:, t % 4, i, :], XRC[t % 2][:, nh * 512:(nh + 1) * 512],
                                                  start=True, stop=True)
                        mm.then_inc(l_p, 1)

        def act_phase11(act):
            act.wait_ge(l_taps, 1)
            nc.scalar.activation(LSP[:, 1, :], LSP[:, 0, :], ACT.Exp, scale=-1.0).then_inc(l_taps, 1)
            for j in range(2 * KD + 1):
                if j in (0, 4, 8, 12):
                    act_split(act, S_I + 1 + j // 4)
                if j < KD:
                    act.wait_ge(step_mm, U_I + j + 1)
                    nc.scalar.activation(V[:, j, :], two_banks(2 * (j % 2)), ACT.Gelu_apprx_tanh).then_inc(step_use, 1)
                    continue
                if j < 2 * KD:
                    t = j - KD
                    act.wait_ge(step_mm, U_I + j + 1)
                    if t >= 2:
                        act.wait_ge(l_v, t - 1)
                    nc.scalar.activation(XRC[t % 2][:], two_banks(2 * (j % 2)), ACT.Identity,
                                         bias=COLV[:, CV_OB + t:CV_OB + t + 1],
                                         scale=COLV[:, CV_OW + 24 + t:CV_OW + 25 + t]).then_inc(l_a, 1)
                if j > KD:
                    act_lru(act, j - KD - 1)

        def act_lru(act, t):
            a, ig, th = RGA[:], RGI[:], RGT[:]
            if t == 0:
                act.wait_ge(l_taps, 3)
            if t:
                act.wait_ge(l_v, t)
            act.wait_ge(l_p, 2 * t + 1)
            nc.scalar.activation(a, two_banks(4), ACT.Sigmoid, bias=COLV[:, CV_BA + t:CV_BA + t + 1]).then_inc(l_a, 1)
            act.wait_ge(l_p, 2 * t + 2)
            nc.scalar.activation(ig, two_banks(6), ACT.Sigmoid, bias=COLV[:, CV_BI + t:CV_BI + t + 1]).then_inc(l_a, 1)
            act.wait_ge(l_a, lru_n(t, 1))
            nc.scalar.activation(th, a, ACT.Tanh, scale=LSP[:, 2, t:t + 1]).then_inc(l_a, 1)
            nc.scalar.activation(a, a, ACT.Exp, scale=LSP[:, 3, t:t + 1]).then_inc(l_a, 1)
            act.wait_ge(l_a, lru_n(t, 3))
            nc.scalar.activation(th, th, ACT.Sqrt).then_inc(l_a, 1)

        def dve_phase11(dve):
            ch = dve_chain
            lam = COLV[:, CV_LAM:CV_LAM + KD]
            nc.vector.scalar_tensor_tensor(out=LSP[:, 0, :], in0=lam, scalar=-1.0, in1=lam, op0=ALU.mult, op1=ALU.max).then_inc(l_taps, 1)
            dve_split(dve, S_I + 1)
            dve.wait_ge(l_taps, 2)
            log1p_of(ch, LSP[:, 1, :], LSP[:, 2, :], LSP[:, 3, :])
            ch.step(nc.vector.tensor_scalar(LSP[:, 0, :], lam, -1.0, 0.0, ALU.mult, ALU.max))
            ch.step(nc.vector.tensor_tensor(LSP[:, 0, :], LSP[:, 0, :], LSP[:, 1, :], ALU.add))
            ch.step(nc.vector.tensor_scalar(LSP[:, 2, :], LSP[:, 0, :], LRU_C / 2, None, ALU.mult))
            nc.vector.tensor_scalar(LSP[:, 3, :], LSP[:, 0, :], -LRU_C, None, ALU.mult).then_inc(l_taps, 1)
            for j in range(2 * KD + 1):
                if j in (4, 8, 12):
                    dve_split(dve, S_I + 1 + j // 4)
                if KD <= j < 2 * KD:
                    t = j - KD
                    dve.wait_ge(l_a, ident_n(t))
                    src, acc = two_banks(2 * (j % 2)), XRC[t % 2]
                    for tap in (2, 1, 0):
                        sh = 3 - tap
                        w = COLV[:, CV_OW + 8 * tap + t:CV_OW + 8 * tap + t + 1]
                        ins = nc.vector.scalar_tensor_tensor(out=acc[:, sh:], in0=src[:, :T - sh], scalar=w, in1=acc[:, sh:],
                                                             op0=ALU.mult, op1=ALU.add)
                        if tap:
                            ch.step(ins)
                        else:
                            ins.then_inc(step_use, 1)
                if j > KD:
                    t = j - KD - 1
                    x, a, ig, th = XRC[t % 2][:], RGA[:], RGI[:], RGT[:]
                    dve.wait_ge(l_a, lru_n(t, 2))
                    dve.wait_ge(step_use, U_I + KD + t + 1)
                    ch.step(nc.vector.tensor_tensor(ig, ig, x, ALU.mult))
                    dve.wait_ge(l_a, lru_n(t, 5))
                    ch.step(nc.vector.scalar_tensor_tensor(out=th, in0=a, scalar=1.0, in1=th, op0=ALU.add, op1=ALU.mult))
                    ch.step(nc.vector.tensor_tensor(ig, ig, th, ALU.mult))
                    ch.step(nc.vector.tensor_tensor_scan(th, a, ig, 0.0, ALU.mult, ALU.add))
                    nc.vector.tensor_tensor(V[:, t, :], th, V[:, t, :], ALU.mult).then_inc(l_v, 1)

        def sp_phase12(sp):
            sp.wait_ge(phase_s, 4 * 11)
            sp.dma_start(GAM[0][:], A["norm_ffn"][1:2, :].to_broadcast([P, D])).then_inc(gain_in[0], 16)
            for n in range(2):
                sp_residual(sp, 1, n)

        def pe_phase12(pe):
            pe.wait_ge(l_lo, KD)
            for m in range(MT):
                pe_token_step(pe, S_O, m, U_O + m, U_O)
            pe_pass_end(S_O)
            pe_last_pass(pe, 1, S_O + 1, U_O + 8, U_O)

        def act_phase12(act):
            for k in range(KD):
                nc.scalar.activation(ATH[:, k, :], V[:, k, :], ACT.Copy).then_inc(l_hi, 1)
            act_split(act, S_O + 1)
            act_last_pass(act, 1, U_O + 8)

        def dve_phase12(dve):
            for k in range(KD):
                dve.wait_ge(l_hi, k + 1)
                nc.vector.tensor_tensor(ATL[:, k, :], V[:, k, :], ATH[:, k, :].bitcast(F32), ALU.subtract).then_inc(l_lo, 1)
            for m in range(MT):
                if m == 1:
                    dve_split(dve, S_O + 1)
                dve_add_res(dve, 1, m, 0, U_O + m, U_O)
            dve_last_pass(dve, 1, U_O + 8, lambda m: dve_add_res(dve, 1, m, 1, U_O + 8 + m, U_O))

        def pool_phase12(pool):
            pool_last_pass(pool, 1, U_O + 8)

        @block.sync
        def _(sp):
            sp_phase0(sp)
            sp_phase1(sp)
            sp_phase2(sp)
            sp_phase4(sp)
            sp_phase5(sp)
            sp_phase6(sp)
            for layer in range(2):
                if layer:
                    sp_phase11(sp)
                    sp_phase12(sp)
                sp_moe_prefetch(sp, layer)
                sp.wait_ge(phase_s, 4 * (7 + 6 * layer))
                sp_moe(sp, layer)
                sp_ovf(sp, layer)
                if layer == 0:
                    sp_slice(sp, S_I)
                sp.wait_ge(phase_s, 4 * (9 + 6 * layer))
                sp_combine(sp, layer)

        @block.scalar
        def _(act):
            act_phase0(act)
            finished(act, 1)
            act_phase1(act)
            finished(act, 2)
            act_phase2(act)
            finished(act, 3)
            act_phase4(act)
            finished(act, 4)
            act_phase5(act)
            finished(act, 5)
            act_phase6(act)
            finished(act, 6)
            for layer in range(2):
                if layer:
                    act_phase11(act)
                    finished(act, 11)
                    act_phase12(act)
                    finished(act, 12)
                act_route(act, layer)
                finished(act, 7 + 6 * layer)
                act_moe(act, layer)
                finished(act, 8 + 6 * layer)
                act_ovf(act, layer)
                finished(act, 9 + 6 * layer)
                act_combine(act, layer)
                if layer == 0:
                    finished(act, 10)

        @block.vector
        def _(dve):
            dve_phase0(dve)
            finished(dve, 1)
            dve_phase1(dve)
            finished(dve, 2)
            dve_phase2(dve)
            finished(dve, 3)
            dve_phase4(dve)
            finished(dve, 4)
            dve_phase5(dve)
            finished(dve, 5)
            dve_phase6(dve)
            finished(dve, 6)
            for layer in range(2):
                if layer:
                    dve_phase11(dve)
                    finished(dve, 11)
                    dve_phase12(dve)
                    finished(dve, 12)
                dve_route(dve, layer)
                finished(dve, 7 + 6 * layer)
                dve_moe(dve, layer)
                finished(dve, 8 + 6 * layer)
                dve_ovf(dve, layer)
                finished(dve, 9 + 6 * layer)
                dve_combine(dve, layer)
                if layer == 0:
                    finished(dve, 10)

        @block.gpsimd
        def _(pool):
            pool_phase0(pool)
            finished(pool, 1)
            pool_phase1(pool)
            finished(pool, 2)
            pool_phase2(pool)
            finished(pool, 3)
            pool_phase4(pool)
            finished(pool, 4)
            pool_phase5(pool)
            finished(pool, 5)
            pool_phase6(pool)
            finished(pool, 6)
            for layer in range(2):
                if layer:
                    finished(pool, 11)
                    pool_phase12(pool)
                    finished(pool, 12)
                finished(pool, 7 + 6 * layer)
                pool_moe(pool, layer)
                finished(pool, 8 + 6 * layer)
                pool_ovf(pool, layer)
                finished(pool, 9 + 6 * layer)
                pool_combine(pool, layer)
                if layer == 0:
                    finished(pool, 10)

        @block.tensor
        def _(pe):
            pe_phase0(pe)
            finished(pe, 1)
            pe_phase1(pe)
            finished(pe, 2)
            pe_phase2(pe)
            finished(pe, 3)
            pe_phase4(pe)
            finished(pe, 4)
            pe_phase5(pe)
            finished(pe, 5)
            pe_phase6(pe)
            finished(pe, 6)
            for layer in range(2):
                if layer:
                    pe_phase11(pe)
                    finished(pe, 11)
                    pe_phase12(pe)
                    finished(pe, 12)
                pe_route(pe, layer)
                finished(pe, 7 + 6 * layer)
                pe_moe(pe, layer)
                finished(pe, 8 + 6 * layer)
                pe_ovf(pe, layer)
                finished(pe, 9 + 6 * layer)
                pe_combine(pe, layer)
                if layer == 0:
                    finished(pe, 10)


def constants():
    c = np.zeros((P, 5 * P + 64), np.float32)
    r = np.arange(P)
    c[:, 0:P] = np.eye(P)
    c[:, P:2 * P] = r[:, None] <= r[None, :]
    c[:, 2 * P:3 * P] = r[:, None] < r[None, :]
    c[:, 3 * P:4 * P] = r[None, :]
    c[:, 4 * P:5 * P] = 1.0
    misc = c[:, 5 * P:]
    misc[:, 0:MT] = P * np.arange(MT)[None, :] + r[:, None]
    misc[:, 8:15] = BLK * (np.arange(7) + 1)
    misc[:, 16:16 + OVF] = np.arange(OVF)
    misc[:, 32] = -0.5
    return c


def kernel(**inputs):
    import concourse.bacc as bacc
    from concourse.bass_utils import run_bass_kernel_spmd

    nc = bacc.Bacc("TRN2", target_bir_lowering=False, num_devices=1)
    arrays, aps = {}, {}
    for name, a in list(inputs.items()) + [("c_f32", constants())]:
        a = np.ascontiguousarray(a)
        arrays[f"in_{name}_dram"] = a
        aps[name] = nc.dram_tensor(f"in_{name}_dram", a.shape, mybir.dt.from_np(a.dtype), kind="ExternalInput").ap()
    out = nc.dram_tensor("out_0_dram", (1, T, D), F32, kind="ExternalOutput").ap()
    trunk(nc, aps, out[0])
    r = run_bass_kernel_spmd(nc, [arrays], core_ids=[0])
    return r.results[0]["out_0_dram"]
```

```python
from contextlib import ExitStack

import numpy as np

import concourse.bass as bass
from concourse import mybir

F32 = mybir.dt.float32
F32R = mybir.dt.float32r
BF16 = mybir.dt.bfloat16
I32 = mybir.dt.int32
U32 = mybir.dt.uint32
ALU = mybir.AluOpType
ACT = mybir.ActivationFunctionType
AX = mybir.AxisListType.X

P = 128
T = 1024
D = 1024
MT = T // P
KD = D // P
H = 16
HP = 64
SG = 2
NG = 8
XBC0, U0, V0 = 1024, 2320, 3344
NE, EG, GE = 32, 4, 8
F = 512
LRU_C = 8.0
BLK = 128
OVF = (2 * T) // BLK - 1
YROWS = (NE + OVF) * BLK
EPS_RMS, EPS_LN = 1e-6, 1e-5
BIG = 1e30

SLICES = (
    [("ev_w_in", 0, V0, 512), ("ev_w_in", 0, V0 + 512, 512),
     ("ev_w_in", 0, U0, 512), ("ev_w_in", 0, U0 + 512, 512),
     ("ev_w_in", 0, XBC0 + 1024, 272), ("ev_w_in", 0, XBC0, 512), ("ev_w_in", 0, XBC0 + 512, 512),
     ("ev_w_in", 0, 0, 512), ("ev_w_in", 0, 512, 512),
     ("ev_w_out", 0, 0, 512), ("ev_w_out", 0, 512, 512),
     ("ev_w_out", 1024, 0, 512), ("ev_w_out", 1024, 512, 512)]
    + [("od_w_in", 0, c, 512) for c in (1024, 1536, 0, 512)]
    + [("od_w_out", 0, 0, 512), ("od_w_out", 0, 512, 512)]
)
S_U, S_X2, S_X0, S_Z, S_A, S_I, S_O = 2, 4, 5, 7, 9, 13, 17
N_SL0 = 13

CV_CW, CV_CB, CV_SB = 0, 40, 50
CV_OW, CV_OB, CV_BA, CV_BI, CV_LAM, CV_N = 58, 90, 98, 106, 114, 122


class Chain:

    def __init__(self, eng, sem):
        self.eng, self.sem, self.n = eng, sem, 0

    def add(self, ins):
        self.n += 1
        ins.then_inc(self.sem, 1)

    def wait(self):
        self.eng.wait_ge(self.sem, self.n)

    def step(self, ins):
        self.add(ins)
        self.wait()


def trunk(nc, A, out):
    with ExitStack() as ctx:
        base = (nc.sbuf_base + 63) // 64 * 64
        place = [base]

        def region(nbytes):
            at = place[0]
            place[0] = at + (nbytes + 31) // 32 * 32
            assert place[0] <= nc.sbuf_usable_end
            return at

        def at(name, shape, dtype, offset):
            return nc.alloc_sbuf_tensor_at(name, shape, dtype, offset=offset)

        def sem(name):
            return ctx.enter_context(nc.semaphore(name))

        r_at = region(65536)
        r_raw = region(16384)
        r_whi = region(32768)
        r_wlo = region(32768)
        r_v = region(32768)
        ATH = at("act_t_hi", [P, KD, T], F32R, r_at)
        ATL = at("act_t_lo", [P, KD, T], F32R, r_at + 32768)
        WRAW = at("w_raw", [P, 2, 4, 512], F32, r_raw)
        WHI = at("w_hi", [P, 4, 4, 512], F32R, r_whi)
        WLO = at("w_lo", [P, 4, 4, 512], F32R, r_wlo)
        V = at("wide", [P, MT, D], F32, r_v)
        SP1, SP2 = (V[:, i, D - P:] for i in range(2))
        AT32 = at("act_t_raw", [P, 2, KD, T], F32, r_at)
        MRAW = ([at(f"moe_raw{i}", [P, 4, 512], F32, r_raw + 8192 * i) for i in range(2)]
                + [AT32[:, i // 2 % 2, 4 * (i % 2):4 * (i % 2) + 4, 512 * (i // 4):512 * (i // 4) + 512] for i in range(8)]
                + [at(f"moe_raw{i}", [P, 4, 512], F32, r_v + 8192 * (i - 10)) for i in range(10, 12)])
        XTH = at("moe_xt_hi", [P, KD, P], F32R, r_v + 16384)
        XTL = at("moe_xt_lo", [P, KD, P], F32R, r_v + 20480)
        GTH = at("moe_gt_hi", [P, 4, P], F32R, r_v + 24576)
        GTL = at("moe_gt_lo", [P, 4, P], F32R, r_v + 26624)
        SIL = at("moe_silu", [P, F], F32, r_v + 28672)
        GAT = at("moe_gated", [P, F], F32, r_v + 30720)
        CX = [at(f"comb_x{i}", [P, D], F32, (r_wlo if i >= 4 else r_whi) + 4096 * (i % 4)) for i in range(MT)]
        CY = [at(f"comb_y{i}", [P, D], F32, r_v + 16384 + 4096 * i) for i in range(4)]
        EX = [at(f"ssd_e{i}", [P, 4, P], F32, r_raw + 8192 + 2048 * i) for i in range(2)]
        ZS = at("ssd_z", [P, D], F32, r_raw + 12288)

        def small(name, shape, dtype=F32):
            n = int(np.prod(shape[1:])) * (2 if dtype == BF16 else 4)
            return at(name, shape, dtype, region(n))

        CONST = small("const", [P, 5 * P + 64])
        IDENT, UINC, USTR, IOTA, ONES = (CONST[:, P * i:P * (i + 1)] for i in range(5))
        MISC = CONST[:, 5 * P:]
        TOKID, THRESH, SLOTI, MHALF = MISC[:, 0:8], MISC[:, 8:15], MISC[:, 16:31], MISC[:, 32:33]
        CBF = small("const_bf", [P, 2 * P], BF16)
        IDENTB, NEGB = CBF[:, 0:P], CBF[:, P:2 * P]
        USTRB, ONESB = IDENTB, NEGB
        COLV = small("colvecs", [P, CV_N])
        HROW = small("head_rows", [P, 3, H])
        RB = small("router_bias", [P, 2, EG + NE])
        BM = at("ssd_b", [P, P], F32, place[0])
        WR = small("router_w", [P, KD, EG + NE])
        XDD = at("ssd_xdd", [P, H, HP], F32, place[0])
        ECL = at("ssd_ecl", [P, MT, H], F32, place[0])
        GAM = [small(f"gain{i}", [P, D]) for i in range(2)]
        SS = small("ss", [P, 56])
        MS = small("ms", [P, 56])
        RSTD = small("rstd", [P, 56])
        ROWI = small("row_index", [P, MT, 2], I32)
        GATE = small("gates", [P, MT, 2])
        VPOS = small("ovf_pos", [P, MT, 2])
        IDXA = small("block_tokens", [P, NE], I32)
        CUR = [small(f"cur_idx{i}", [P, 2], I32) for i in range(2)]
        REGS = small("ovf_table", [P, 16], I32)
        r_s = region(0)
        s_room = nc.sbuf_usable_end - r_s
        plans = {}

        def scratch(plan, name, shape, dtype=F32):
            n = (int(np.prod(shape[1:])) * 4 + 31) // 32 * 32
            o = plans.get(plan, 0)
            plans[plan] = o + n
            assert plans[plan] <= s_room, (plan, name, plans[plan], s_room)
            return at(f"{plan}_{name}", shape, dtype, r_s + o)

        VECS = scratch("norm", "vecs", [P, P])
        HTILE = [scratch("norm", f"h{i}", [P, D]) for i in range(2)]
        UT = [scratch("uz", f"t{i}", [P, 512]) for i in range(2)]
        BNS = scratch("uz", "bn", [P, 2, 6])
        MV = scratch("uz", "mv", [P, MT, 2])
        WSP = scratch("uz", "spatial", [P, NG, P])
        WSPT = scratch("uz", "spatial_t", [P, NG, P])
        BCT = [scratch("ssd", n, [P, T]) for n in ("bt", "ct")]
        DT = scratch("ssd", "dt", [P, MT, H])
        ADT = scratch("ssd", "adt", [P, MT, H])
        CACC = [scratch("ssd", f"conv{i}", [P, T]) for i in range(2)]
        o_c = plans["ssd"] - 8192 + r_s
        CSC = at("ssd_cs", [P, MT, H], F32, o_c)
        DEC = at("ssd_dec", [P, MT, H], F32, o_c + 512)
        ECS = at("ssd_ecs", [P, MT, H], F32, o_c + 1024)
        ECL2 = at("ssd_ecl2", [P, MT, 8], F32, o_c + 1536)
        XD = at("ssd_xd", [P, H, HP], F32, o_c + 1792)
        STATE = at("ssd_state", [P, 8, HP], F32, o_c + 5888)
        RES = [scratch("moe", f"res{i}", [P, 512]) for i in range(2)]
        HM = [scratch("moe", f"h{i}", [P, D]) for i in range(2)]
        HTF = scratch("moe", "ht", [P, KD, P])
        LOG = scratch("moe", "logits", [P, MT, EG + NE])
        G8 = scratch("route", "g8", [P, MT, 8])
        GV = scratch("route", "gv", [P, MT, 8])
        GI = scratch("route", "gi", [P, MT, 8], U32)
        EV = scratch("route", "ev", [P, MT, 8])
        EI = scratch("route", "ei", [P, MT, 8], U32)
        GIF = scratch("route", "gif", [P, MT, 1])
        GM = scratch("route", "gmask", [P, MT, EG])
        EL = scratch("route", "el", [P, MT, NE])
        MM = scratch("route", "mask", [P, MT, NE], BF16)
        OT = scratch("route", "oht", [P, 2, MT, NE])
        assert plans["route"] <= 8192
        plans["route"] = 8192
        OH = scratch("route", "onehot", [P, 2, MT, NE])
        PR = scratch("route", "prod", [P, MT, NE])
        EIF = scratch("route", "eif", [P, MT, 2])
        POSK = scratch("route", "posk", [P, MT, 2])
        BK = scratch("route", "bk", [P, MT, 2])
        TMP = scratch("route", "tmp", [P, MT, 4])
        DEN = scratch("route", "den", [P, MT, 4])
        assert plans["route"] <= plans["moe"] - MT * 36 * 4
        o_r = r_v + 24576
        PH = at("route_ph", [P, 4, P], F32, o_r)
        NOV = at("route_nov", [P, 3, NE], F32, o_r + 2048)
        CMP = at("route_cmp", [P, NE, 7], F32, o_r + 2560)
        CMS = at("route_cms", [P, OVF, NE], F32, o_r + 3584)
        ESL = at("route_esl", [P, 16], F32, o_r + 6144)
        XG = [scratch("loop", f"xg{i}", [P, D]) for i in range(2)]
        YSB = [scratch("loop", f"y{i}", [P, D]) for i in range(2)]
        XRC = [scratch("lru", "xr", [P, T]), GAM[1]]
        RGA, RGI, RGT = (scratch("lru", n, [P, T]) for n in ("a", "i", "t"))
        LW = GAM[0][:].rearrange("p (s w j) -> p s w j", s=4, w=2)
        LSP = scratch("lru", "sp", [P, 4, 8])
        HN = [scratch("comb", f"h{i}", [P, D]) for i in range(2)]
        OHB = at("ovf_onehot", [P, 2 * MT, P], F32, r_v)
        OXG = at("ovf_xg", [P, D], F32, r_v + 8192)
        OXT = at("ovf_xt", [P, KD, P], F32, r_v + 12288)
        OSIL = at("ovf_silu", [P, F], F32, r_v + 16384)
        OGAT = at("ovf_gated", [P, F], F32, r_v + 18432)
        OGT = at("ovf_gt", [P, 4, P], F32, r_v + 20480)
        OY = at("ovf_y", [P, D], F32, r_v + 22528)
        OIDX = at("ovf_idx", [P, 1], I32, r_v + 26624)

        PS = ctx.enter_context(nc.psum_tensor("psum", [P, 8, 512], F32))

        YG = nc.dram_tensor("scratch_ysgu", [T, D], F32).ap()
        XM = nc.dram_tensor("scratch_xmid", [T, D], F32).ap()
        X2 = nc.dram_tensor("scratch_x2", [T, D], F32).ap()
        HD = nc.dram_tensor("scratch_h", [T, D], F32).ap()
        YB = nc.dram_tensor("scratch_yb", [YROWS, D], F32).ap()

        phase_s = sem("phase_finished")
        const_in, vec_in, wsp_in, wr_in = sem("const_in"), sem("vectors_in"), sem("spatial_w_in"), sem("router_w_in")
        gain_in = [sem("gain_in0"), sem("gain_in1")]
        dve_ch, cb_done = sem("dve_chain"), sem("cb_done")
        dve_loop = [sem("ovf_pos_set0"), sem("ovf_pos_set1")]
        raw_in = [sem(f"raw_in{i}") for i in range(12)]
        w_hi_done, w_lo_done, pass_done = sem("w_hi_done"), sem("w_lo_done"), sem("pass_done")
        step_mm, step_use = sem("step_products"), sem("step_consumed")
        n_sq, n_ms, n_rstd, n_h = sem("norm_sq"), sem("norm_ms"), sem("norm_rstd"), sem("norm_h")
        n_tr, n_hi, n_lo = sem("tile_turned"), sem("turned_hi"), sem("turned_lo")
        x_in = [sem(f"x_in{m}") for m in range(MT)]
        colv_set = sem("colvecs_set")
        tile_st = [sem("tile_stored0"), sem("tile_stored1")]
        yg_in = [sem("ysgu_in0"), sem("ysgu_in1")]
        res_in = [sem("residual_in0"), sem("residual_in1")]
        a_tok, d_tok, p_tok, g_tok = sem("act_step"), sem("dve_step"), sem("pe_step"), sem("pool_step")
        h_st, xm_st = [sem("h_stored0"), sem("h_stored1")], sem("xmid_stored")
        zero_st = sem("zeros_stored")
        r_mm, r_log = sem("router_products"), sem("router_logits")
        m_hi, m_lo, m_unit = sem("moe_hi"), sem("moe_lo"), sem("moe_unit_used")
        m_xtr, m_xhi, m_xlo = sem("moe_x_turned"), sem("moe_x_hi"), sem("moe_x_lo")
        m_silu, m_gmul, m_gtr = sem("moe_silu"), sem("moe_gated"), sem("moe_g_turned")
        m_ghi, m_glo, m_yev = sem("moe_g_hi"), sem("moe_g_lo"), sem("moe_y_out_of_psum")
        y_st = [sem("y_stored0"), sem("y_stored1")]
        xg_in = [sem("xg_in0"), sem("xg_in1")]
        cur_set, gather_go = sem("cur_idx_set"), sem("gather_go")
        o_raw, o_w2, o_xg, o_yst, o_v, o_a, o_p = ([sem(f"ovf_{n}{i}") for i in range(2)]
                                             for n in ("w13_in", "w2_in", "x_in", "y_stored", "dve", "act", "pe"))
        cx_in = [sem(f"comb_x_in{i}") for i in range(MT)]
        cy_in = [sem(f"comb_y_in{i}") for i in range(4)]
        c_add = sem("comb_added")
        x2_st = sem("x2_stored")
        out_st = [sem(f"out_stored{i}") for i in range(2)]
        l_w = [sem(f"lru_w_in{i}") for i in range(4)]
        l_a, l_v, l_p = sem("lru_act"), sem("lru_tile"), sem("lru_gates")
        l_hi, l_lo, l_taps = sem("lru_hi"), sem("lru_lo"), sem("lru_sp")

        block = ctx.enter_context(nc.Block())

        dve_chain = Chain(nc.vector, dve_ch)

        def finished(eng, k):
            eng.drain().then_inc(phase_s, 1)
            eng.wait_ge(phase_s, 4 * k)

        def rows(t, m):
            return t[m * P:(m + 1) * P, :]

        Q_MIX0, Q_LN, Q_SSD, Q_FFN, Q_MIX1, Q_FIN = 0, 8, 16, (24, 40), 32, 48
        T_MIX0, T_SSD, T_SGU, T_FFN, T_MIX1 = 0, 8, 16, (24, 40), 32
        U_V, U_U, U_X, U_A, U_I, U_O = 0, 16, 32, 43, 75, 91

        def sq_index(q):
            return q + 1 if q < 8 else q - 7

        def act_square(q, x, h):
            nc.scalar.activation(h, x, ACT.Square, accum_out=SS[:, q:q + 1]).then_inc(n_sq, 1)

        def dve_mean(dve, q):
            dve.wait_ge(n_sq, sq_index(q))
            nc.vector.tensor_scalar(MS[:, q:q + 1], SS[:, q:q + 1], 1.0 / D, EPS_RMS, ALU.mult, ALU.add).then_inc(n_ms, 1)

        def pool_rstd(pool, q):
            pool.wait_ge(n_ms, q + 1)
            nc.gpsimd.tensor_tensor(RSTD[:, q:q + 1], MS[:, q:q + 1], MHALF, ALU.pow).then_inc(n_rstd, 1)

        def dve_scale(dve, q, x, h, gain):
            dve.wait_ge(n_rstd, q + 1)
            nc.vector.scalar_tensor_tensor(out=h, in0=x, scalar=RSTD[:, q:q + 1], in1=gain, op0=ALU.mult,
                                           op1=ALU.mult).then_inc(n_h, 1)

        def pe_turn(pe, ti, tile):
            if ti:
                pe.wait_ge(n_hi, 2 * ti)
                if lo_before(ti):
                    pe.wait_ge(n_lo, 2 * lo_before(ti))
            for hb in range(2):
                for c in range(4):
                    k = 4 * hb + c
                    last = nc.tensor.transpose(PS[:, 6 + hb, c * P:(c + 1) * P], tile[:, k * P:(k + 1) * P], IDENT)
                last.then_inc(n_tr, 1)

        def lo_before(ti):
            return ti - 8 * (ti > T_FFN[0] + 7) if ti <= T_FFN[0] or ti > T_FFN[0] + 7 and ti <= T_FFN[1] else \
                24 if ti <= T_FFN[0] + 7 else 32

        def act_turn_hi(act, ti, m):
            for hb in range(2):
                act.wait_ge(n_tr, 2 * ti + hb + 1)
                nc.scalar.activation(ATH[:, 4 * hb:4 * hb + 4, m * P:(m + 1) * P],
                                     PS[:, 6 + hb, :].rearrange("p (c t) -> p c t", c=4), ACT.Copy).then_inc(n_hi, 1)

        def dve_turn_lo(dve, ti, m):
            for hb in range(2):
                dve.wait_ge(n_hi, 2 * ti + hb + 1)
                sl = (slice(None), slice(4 * hb, 4 * hb + 4), slice(m * P, (m + 1) * P))
                nc.vector.tensor_tensor(ATL[sl], PS[:, 6 + hb, :].rearrange("p (c t) -> p c t", c=4),
                                        ATH[sl].bitcast(F32), ALU.subtract).then_inc(n_lo, 1)

        def sp_half_slice(sp, s, h):
            name, r0, c0, w = SLICES[s]
            src = A[name][0, r0:r0 + D, c0:c0 + w].rearrange("(h c p) n -> h p c n", p=P, c=4)
            sp.dma_start(WRAW[:, h, :, 0:w], src[h]).then_inc(raw_in[h], 16)

        def sp_slice(sp, s):
            for h in range(2):
                n = 2 * s + h
                if n >= 2:
                    sp.wait_ge(w_lo_done, n - 1)
                sp_half_slice(sp, s, h)

        def mixer_raw(s):
            return 16 * (s + 1 + (16 if s >= N_SL0 else 0))

        def act_split(act, s, halves=range(2)):
            w = SLICES[s][3]
            for h in halves:
                act.wait_ge(raw_in[h], mixer_raw(s))
                if s >= 2:
                    act.wait_ge(pass_done, s - 1)
                nc.scalar.activation(WHI[:, 2 * (s % 2) + h, :, 0:w], WRAW[:, h, :, 0:w], ACT.Copy).then_inc(w_hi_done, 1)

        def dve_split(dve, s, halves=range(2)):
            w = SLICES[s][3]
            for h in halves:
                dve.wait_ge(w_hi_done, 2 * s + h + 1)
                slot = 2 * (s % 2) + h
                nc.vector.tensor_tensor(WLO[:, slot, :, 0:w], WRAW[:, h, :, 0:w], WHI[:, slot, :, 0:w].bitcast(F32),
                                        ALU.subtract).then_inc(w_lo_done, 1)

        def three(o, lh, ll, rh, rl, first, last):
            nc.tensor.matmul(o, lh, rh, start=first, stop=False)
            nc.tensor.matmul(o, lh, rl, start=False, stop=False)
            return nc.tensor.matmul(o, ll, rh, start=False, stop=last)

        def pe_token_step(pe, s, m, u, u0, ready=None):
            if m == 0:
                pe.wait_ge(w_lo_done, 2 * s + 2)
            if u - u0 >= 4:
                pe.wait_ge(step_use, u - 3)
            bank = (u - u0) % 4
            for k in range(KD):
                if ready:
                    ready(k)
                slot, c = 2 * (s % 2) + k // 4, k % 4
                mm = three(PS[:, bank, :], ATH[:, k, m * P:(m + 1) * P], ATL[:, k, m * P:(m + 1) * P],
                           WHI[:, slot, c, :], WLO[:, slot, c, :], k == 0, k == KD - 1)
            mm.then_inc(step_mm, 1)

        def pe_pass_end(s):
            nc.tensor.drain().then_inc(pass_done, 1)

        def pe_chan_step(pe, s, j, u, u0):
            if j == 0:
                pe.wait_ge(w_lo_done, 2 * s + 2)
            if u - u0 >= 2:
                pe.wait_ge(step_use, u - 1)
            b0 = 2 * ((u - u0) % 2)
            for nh in range(2):
                for k in range(KD):
                    slot, c = 2 * (s % 2) + k // 4, k % 4
                    mm = three(PS[:, b0 + nh, :], WHI[:, slot, c, j * P:(j + 1) * P], WLO[:, slot, c, j * P:(j + 1) * P],
                               ATH[:, k, nh * 512:(nh + 1) * 512], ATL[:, k, nh * 512:(nh + 1) * 512],
                               k == 0, k == KD - 1)
            mm.then_inc(step_mm, 1)

        def two_banks(b0):
            return PS[:, b0:b0 + 2, :].rearrange("p b n -> p (b n)")

        def head_bc(t, m, n):
            return t[:, m, :].unsqueeze(2).to_broadcast([P, H, n])

        def sp_phase0(sp):
            sp.dma_start(CONST[:], A["c_f32"]).then_inc(const_in, 16)
            for m in range(MT):
                sp.dma_start(V[:, m, :], rows(A["x"][0], m)).then_inc(x_in[m], 16)
                if m == 0:
                    sp.dma_start(GAM[0][:], A["norm_mix"][0:1, :].to_broadcast([P, D])).then_inc(gain_in[0], 16)
                    sp_slice(sp, 0)
            for r0, src in ((CV_CW, A["ev_conv_w"][0].rearrange("k (j p) -> (k j) p", p=P)),
                            (CV_CB, A["ev_conv_b"][0].rearrange("(j p) -> j p", p=P)),
                            (CV_SB, A["ev_spatial_b"][0]),
                            (CV_OW, A["od_conv_w"][0].rearrange("k (j p) -> (k j) p", p=P)),
                            (CV_OB, A["od_conv_b"][0].rearrange("(j p) -> j p", p=P)),
                            (CV_BA, A["od_b_a"][0].rearrange("(j p) -> j p", p=P)),
                            (CV_BI, A["od_b_i"][0].rearrange("(j p) -> j p", p=P)),
                            (CV_LAM, A["od_lam"][0].rearrange("(j p) -> j p", p=P))):
                sp.dma_start(VECS[r0:r0 + src.shape[0], :], src).then_inc(vec_in, 16)
            for i, n in enumerate(("ev_dt_bias", "ev_a_log", "ev_d_skip")):
                sp.dma_start(HROW[:, i, :], A[n].to_broadcast([P, H])).then_inc(vec_in, 16)
            for l in range(2):
                sp.dma_start(RB[:, l, 0:EG], A["moe_b_group"][l:l + 1, :].to_broadcast([P, EG])).then_inc(vec_in, 16)
                sp.dma_start(RB[:, l, EG:], A["moe_b_expert"][l:l + 1, :].to_broadcast([P, NE])).then_inc(vec_in, 16)

        VEC_DMAS = 8 + 3 + 4

        def act_phase0(act):
            for m in range(MT + 3):
                if m < MT:
                    act.wait_ge(x_in[m], 16)
                    if m >= 2:
                        act.wait_ge(n_tr, 2 * (m - 1))
                    act_square(m, V[:, m, :], HTILE[m % 2][:])
                if m == 0:
                    act_split(act, 0)
                if 1 <= m <= MT:
                    act_turn_hi(act, m - 1, m - 1)
                if m == MT - 2:
                    act_split(act, 1)
                if m >= 3:
                    act_gelu_v(act, 0, m - 3)

        def act_gelu_v(act, n, m):
            act.wait_ge(step_mm, U_V + 8 * n + m + 1)
            nc.scalar.activation(V[:, m, n * 512:(n + 1) * 512], PS[:, m % 4, :], ACT.Gelu_apprx_tanh).then_inc(step_use, 1)

        def dve_phase0(dve):
            dve.wait_ge(gain_in[0], 16)
            for m in range(MT + 2):
                if m == 0:
                    dve_mean(dve, 0)
                if 1 <= m <= MT:
                    dve_scale(dve, m - 1, V[:, m - 1, :], HTILE[(m - 1) % 2][:], GAM[0][:])
                if m == 1:
                    dve_split(dve, 0)
                if 1 <= m < MT:
                    dve_mean(dve, m)
                if m >= 2:
                    dve_turn_lo(dve, m - 2, m - 2)
            dve.wait_ge(p_tok, 1)
            nc.vector.tensor_copy(COLV[:], PS[:, 5, 0:CV_N]).then_inc(colv_set, 1)
            dve.wait_ge(const_in, 16)
            nc.vector.tensor_copy(IDENTB, IDENT)
            nc.vector.tensor_scalar(NEGB, UINC, -1.0, BIG, ALU.add, ALU.mult)

        def pool_phase0(pool):
            pool.wait_ge(const_in, 16)
            for m in range(MT):
                pool_rstd(pool, m)

        def pe_phase0(pe):
            pe.wait_ge(const_in, 16)
            for m in range(MT + 1):
                if m < MT:
                    pe.wait_ge(n_h, m + 1)
                    pe_turn(pe, m, HTILE[m % 2])
                if m == 2:
                    pe.wait_ge(vec_in, 16 * VEC_DMAS)
                    nc.tensor.transpose(PS[:, 5, 0:CV_N], VECS[0:CV_N, :], IDENT[0:CV_N, 0:CV_N]).then_inc(p_tok, 1)
                if m >= 1:
                    pe.wait_ge(n_lo, 2 * m)
                    pe_token_step(pe, 0, m - 1, U_V + m - 1, U_V)
            pe_pass_end(0)

        def sp_phase1(sp):
            sp_slice(sp, 1)
            sp.wait_ge(n_h, MT)
            sp.dma_start(GAM[0][:], A["ev_ln_v_b"].to_broadcast([P, D])).then_inc(gain_in[0], 16)
            sp.dma_start(GAM[1][:], A["ev_ln_v_g"].to_broadcast([P, D])).then_inc(gain_in[1], 16)
            sp.wait_ge(n_tr, 2 * MT)
            sp.wait_ge(p_tok, 1)
            sp.dma_start(WSP[:], A["ev_spatial_w"][0].rearrange("g t s -> t g s")).then_inc(wsp_in, 16)
            sp_slice(sp, 2)

        def act_phase1(act):
            act_split(act, 2)
            for m in range(MT):
                act_gelu_v(act, 1, m)

        def dve_phase1(dve):
            ch = dve_chain
            dve_split(dve, 1)
            for hb in range(2):
                dve.wait_ge(p_tok, 2 + hb)
                nc.vector.tensor_tensor(WSPT[:, 4 * hb:4 * hb + 4, :], PS[:, 4 + hb, :].rearrange("p (g t) -> p g t", g=4),
                                        UINC.unsqueeze(1).to_broadcast([P, 4, P]), ALU.mult).then_inc(d_tok, 1)
            dve_split(dve, 2)
            dve.wait_ge(gain_in[0], 32)
            dve.wait_ge(gain_in[1], 16)
            dve.wait_ge(colv_set, 1)
            for m in range(MT):
                dve.wait_ge(step_use, U_V + 8 + m + 1)
                ch.add(nc.vector.bn_stats(BNS[:, 0, :], V[:, m, 0:512]))
                ch.step(nc.vector.bn_stats(BNS[:, 1, :], V[:, m, 512:1024]))
                ch.step(nc.vector.bn_aggr(MV[:, m, :], BNS[:]))
                nc.vector.tensor_scalar(MS[:, Q_LN + m:Q_LN + m + 1], MV[:, m, 1:2], EPS_LN, None, ALU.add).then_inc(n_ms, 1)
                dve.wait_ge(n_rstd, Q_LN + m + 1)
                ch.step(nc.vector.tensor_scalar(V[:, m, :], V[:, m, :], MV[:, m, 0:1], RSTD[:, Q_LN + m:Q_LN + m + 1],
                                                ALU.subtract, ALU.mult))
                ch.step(nc.vector.tensor_tensor(V[:, m, :], V[:, m, :], GAM[1][:], ALU.mult))
                nc.vector.tensor_tensor(V[:, m, :], V[:, m, :], GAM[0][:], ALU.add).then_inc(n_h, 1)
                if m >= 1:
                    dve_spatial(dve, m - 1)
            dve_spatial(dve, MT - 1)

        def dve_spatial(dve, m):
            for hb in range(2):
                dve.wait_ge(p_tok, 4 + 2 * m + hb)
                nc.vector.tensor_tensor(V[:, m, hb * 512:(hb + 1) * 512].rearrange("p (g d) -> p g d", g=4),
                                        PS[:, 4 + hb, :].rearrange("p (g d) -> p g d", g=4),
                                        COLV[:, CV_SB + 4 * hb:CV_SB + 4 * hb + 4].unsqueeze(2).to_broadcast([P, 4, P]),
                                        ALU.add).then_inc(d_tok, 1)

        def pool_phase1(pool):
            for m in range(MT):
                pool_rstd(pool, Q_LN + m)

        def pe_phase1(pe):
            pe.wait_ge(wsp_in, 16)
            pe.wait_ge(colv_set, 1)
            for hb in range(2):
                for g in range(4):
                    mm = nc.tensor.transpose(PS[:, 4 + hb, g * P:(g + 1) * P], WSP[:, 4 * hb + g, :], IDENT)
                mm.then_inc(p_tok, 1)
            for m in range(MT + 1):
                if m < MT:
                    pe_token_step(pe, 1, m, U_V + 8 + m, U_V)
                if m >= 1:
                    pe_spatial(pe, m - 1)
            pe_pass_end(1)

        def pe_spatial(pe, m):
            pe.wait_ge(n_h, Q_LN + m + 1)
            for hb in range(2):
                pe.wait_ge(d_tok, 2 + 2 * (m - 1) + hb + 1 if m else 2)
                for g in range(4):
                    mm = nc.tensor.matmul(PS[:, 4 + hb, g * P:(g + 1) * P], WSPT[:, 4 * hb + g, :],
                                          V[:, m, (4 * hb + g) * P:(4 * hb + g + 1) * P], start=True, stop=True)
                mm.then_inc(p_tok, 1)

        def sp_phase2(sp):
            sp.wait_ge(n_h, Q_LN + MT)
            sp.dma_start(GAM[1][:], A["ev_ssd_norm"].to_broadcast([P, D])).then_inc(gain_in[1], 16)
            for s in (3, 4):
                sp_slice(sp, s)

        def act_phase2(act):
            for n in range(2):
                act_split(act, S_U + n + 1)
                for m in range(MT):
                    u = U_U + 8 * n + m
                    act.wait_ge(step_mm, u + 1)
                    if 8 * n + m >= 2:
                        act.wait_ge(d_tok, D_U + 8 * n + m - 1)
                    nc.scalar.activation(UT[m % 2][:], PS[:, (8 * n + m) % 4, :], ACT.Gelu_apprx_tanh).then_inc(step_use, 1)

        D_U = 18

        def dve_phase2(dve):
            for n in range(2):
                dve_split(dve, S_U + n + 1)
                for m in range(MT):
                    u = U_U + 8 * n + m
                    dve.wait_ge(step_use, u + 1)
                    sl = V[:, m, n * 512:(n + 1) * 512]
                    nc.vector.tensor_tensor(sl, UT[m % 2][:], sl, ALU.mult).then_inc(d_tok, 1)

        def pool_phase2(pool):
            for n in range(2):
                for m in range(MT):
                    pool.wait_ge(d_tok, D_U + 8 * n + m + 1)
                    pool.dma_start(rows(YG, m)[:, n * 512:(n + 1) * 512], V[:, m, n * 512:(n + 1) * 512])\
                        .then_inc(tile_st[0], 16)
            pool.wait_ge(tile_st[0], 16 * 16)

        def pe_phase2(pe):
            for n in range(2):
                for m in range(MT):
                    pe_token_step(pe, S_U + n, m, U_U + 8 * n + m, U_U)
                pe_pass_end(S_U + n)

        def sp_phase3(sp):
            for s in (5, 6, 7, 8):
                sp_slice(sp, s)

        CH_OF = {0: 8, 1: 9, **{3 + i: i for i in range(8)}}
        A_X = 0

        def act_phase3(act):
            act_split(act, 5)
            for j in range(11):
                if j in (3, 7):
                    act_split(act, 6 if j == 3 else 7)
                if j == 2:
                    act.wait_ge(step_mm, U_X + 3)
                    nc.scalar.activation(CACC[0][0:H, :], two_banks(0)[0:H], ACT.Copy).then_inc(step_use, 1)
                    continue
                if j == 4:
                    act_softplus(act)
                t, i = CH_OF[j], j if j < 2 else j - 1
                acc = BCT[j] if j < 2 else CACC[j % 2]
                act.wait_ge(step_mm, U_X + j + 1)
                if j >= 5:
                    act.wait_ge(p_tok, P_X + 1 + 2 * (j - 4))
                nc.scalar.activation(acc[:], two_banks(2 * (j % 2)), ACT.Identity, bias=COLV[:, CV_CB + t:CV_CB + t + 1],
                                     scale=COLV[:, CV_CW + 30 + t:CV_CW + 31 + t]).then_inc(a_tok, 1)
                if j == 10:
                    act_split(act, 8)
                act.wait_ge(step_use, U_X + j + 1)
                nc.scalar.activation(acc[:], acc[:], ACT.Silu).then_inc(a_tok, 1)

        P_X = 19
        D_X = D_U + 16

        def a_count(j):
            return A_X + (2 * j + 2 if j < 2 else 6 if j == 3 else 2 * j + 2)

        def act_softplus(act):
            act.wait_ge(d_tok, D_X + 1)
            nc.scalar.activation(SP2, SP1, ACT.Exp, scale=-1.0).then_inc(a_tok, 1)
            nc.scalar.activation(HROW[:, 1, :], HROW[:, 1, :], ACT.Exp).then_inc(a_tok, 1)

        def log1p_of(ch, u, z, w):
            ch.step(nc.vector.tensor_scalar(z, u, 2.0, None, ALU.add))
            ch.step(nc.vector.reciprocal(z, z))
            ch.step(nc.vector.tensor_tensor(z, z, u, ALU.mult))
            ch.step(nc.vector.tensor_tensor(w, z, z, ALU.mult))
            ch.step(nc.vector.tensor_scalar(u, w, 2.0 / 15, 2.0 / 13, ALU.mult, ALU.add))
            for c in (11, 9, 7, 5, 3, 1):
                ch.step(nc.vector.tensor_tensor(u, u, w, ALU.mult))
                ch.step(nc.vector.tensor_scalar(u, u, 2.0 / c, None, ALU.add))
            ch.step(nc.vector.tensor_tensor(u, u, z, ALU.mult))

        def dve_phase3(dve):
            ch = dve_chain
            dve_split(dve, 5)
            for j in range(11):
                if j in (3, 7):
                    dve_split(dve, 6 if j == 3 else 7)
                if j == 2:
                    continue
                if j == 4:
                    dve.wait_ge(p_tok, P_X + 1)
                    ch.step(nc.vector.tensor_tensor(DT[:], PS[:, 4, 0:MT * H].rearrange("p (m h) -> p m h", m=MT),
                                                    HROW[:, 0, :].unsqueeze(1).to_broadcast([P, MT, H]), ALU.add))
                    dt = DT[:].rearrange("p m h -> p (m h)")
                    nc.vector.scalar_tensor_tensor(out=SP1, in0=dt, scalar=-1.0, in1=dt, op0=ALU.mult, op1=ALU.max).then_inc(d_tok, 1)
                if j == 6:
                    dve.wait_ge(a_tok, a_count(3) + 2)
                    log1p_of(ch, SP2, SP1, ADT[:].rearrange("p m h -> p (m h)"))
                    ch.step(nc.vector.tensor_scalar(dt, dt, 0.0, None, ALU.max))
                    ch.step(nc.vector.tensor_tensor(dt, dt, SP2, ALU.add))
                    ch.step(nc.vector.tensor_scalar(HROW[:, 1, :], HROW[:, 1, :], -1.0, None, ALU.mult))
                    ch.step(nc.vector.tensor_tensor(ADT[:], DT[:], HROW[:, 1, :].unsqueeze(1).to_broadcast([P, MT, H]),
                                                    ALU.mult))
                t = CH_OF[j]
                acc = BCT[j] if j < 2 else CACC[j % 2]
                dve.wait_ge(a_tok, a_count(j) - 1)
                src = two_banks(2 * (j % 2))
                for tap in (2, 1, 0):
                    sh = 3 - tap
                    w = COLV[:, CV_CW + 10 * tap + t:CV_CW + 10 * tap + t + 1]
                    ins = nc.vector.scalar_tensor_tensor(out=acc[:, sh:], in0=src[:, :T - sh], scalar=w, in1=acc[:, sh:],
                                                         op0=ALU.mult, op1=ALU.add)
                    if tap:
                        ch.step(ins)
                    else:
                        ins.then_inc(step_use, 1)
                if j >= 4:
                    dve_xs(dve, j - 1)
            dve_split(dve, 8, (0,))
            dve_xs(dve, 10)
            dve_split(dve, 8, (1,))

        def dve_xs(dve, j):
            for hb in range(2):
                dve.wait_ge(p_tok, P_X + 1 + 2 * (j - 3) + hb + 1)
                nc.vector.tensor_copy(V[:, 4 * hb:4 * hb + 4, (j - 3) * P:(j - 2) * P],
                                      PS[:, 4 + hb, :].rearrange("p (m c) -> p m c", m=4)).then_inc(d_tok, 1)

        def pool_phase3(pool):
            nc.gpsimd.memset(GAM[0][:], 0.0).then_inc(g_tok, 1)
            pool.wait_ge(g_tok, 1)
            for b in range(OVF):
                r0 = (NE + b) * BLK
                pool.dma_start(YB[r0:r0 + BLK, :], GAM[0][:]).then_inc(zero_st, 16)
            pool.wait_ge(zero_st, 16 * OVF)

        def pe_phase3(pe):
            for j in range(2):
                pe_chan_step(pe, S_X2, j, U_X + j, U_X)
            pe.wait_ge(step_use, U_X + 1)
            for nh in range(2):
                for k in range(KD):
                    slot, c = k // 4, k % 4
                    mm = three(PS[0:H, nh, :], WHI[:, slot, c, 256:272], WLO[:, slot, c, 256:272],
                               ATH[:, k, nh * 512:(nh + 1) * 512], ATL[:, k, nh * 512:(nh + 1) * 512], k == 0, k == KD - 1)
            mm.then_inc(step_mm, 1)
            pe_pass_end(S_X2)
            for j in range(3, 12):
                if j < 11:
                    s = S_X0 + (j - 3) // 4
                    pe_chan_step(pe, s, (j - 3) % 4, U_X + j, U_X)
                    if j in (6, 10):
                        pe_pass_end(s)
                if j == 3:
                    pe.wait_ge(step_use, U_X + 3)
                    for m in range(MT):
                        mm = nc.tensor.transpose(PS[:, 4, m * H:(m + 1) * H], CACC[0][0:H, m * P:(m + 1) * P], IDENT[0:H, 0:H])
                    mm.then_inc(p_tok, 1)
                if j >= 4:
                    i = j - 1
                    pe.wait_ge(a_tok, a_count(i))
                    for hb in range(2):
                        if i == 3:
                            pe.wait_ge(d_tok, D_X + 1)
                        else:
                            pe.wait_ge(d_tok, D_X + 1 + 2 * (i - 4) + hb + 1)
                        for q in range(4):
                            m = 4 * hb + q
                            mm = nc.tensor.transpose(PS[:, 4 + hb, q * P:(q + 1) * P], CACC[i % 2][:, m * P:(m + 1) * P], IDENT)
                        mm.then_inc(p_tok, 1)

        P_S, D_S, A_S = P_X + 17, D_X + 17, A_X + 6 + 16
        PPC, DPC, APC = 13, 13, 7
        P_S1, D_S1, A_S1 = P_S + 1, D_S + 2, A_S + 1
        PC_CB, PC_DEC, PC_Z, PC_YO, PC_YD, PC_ST = 1, (3, 4, 7, 9), (2, 10), 5, (6, 8, 11, 12), 13
        DC_DIFF, DC_SC, DC_ST, DC_Y = (1, 4, 8, 10), (3, 6, 9, 11), 12, 13
        AC_EXP, AC_Z, AC_SILU = (1, 2, 4, 5), (3, 6), 7

        def sp_phase4(sp):
            sp.wait_ge(w_lo_done, 2 * S_A - 1)
            sp_half_slice(sp, S_A, 0)
            sp.wait_ge(n_sq, sq_index(Q_SSD + MT - 1))
            sp_half_slice(sp, S_A, 1)

        def pe_phase4(pe):
            adt = ADT[:].rearrange("p m h -> p (m h)")
            nc.tensor.matmul(PS[:, 0, 0:P], UINC, adt, start=True, stop=True)
            nc.tensor.matmul(PS[:, 1, 0:P], ONES, adt, start=True, stop=True).then_inc(p_tok, 1)
            pe.wait_ge(w_lo_done, 2 * S_A)
            for m in range(MT):
                d0, a0 = D_S1 + DPC * m, A_S1 + APC * m
                t = slice(m * P, (m + 1) * P)
                pe.wait_ge(d_tok, d0 - DPC + DC_SC[3] if m else d0)
                for g in range(SG):
                    nc.tensor.matmul(PS[:, 4, g * P:(g + 1) * P], BCT[0][64 * g:64 * g + 64, t], BCT[1][64 * g:64 * g + 64, t],
                                     start=True, stop=True).then_inc(cb_done, 1)
                    pe.wait_ge(cb_done, 2 * m + g + 1)
                nc.tensor.transpose(PS[:, 4, 2 * P:3 * P], BCT[0][:, t], IDENT).then_inc(p_tok, 1)

                def decay_rows(q):
                    for i in range(4):
                        nc.tensor.matmul(PS[:, 6 + q % 2, i * P:(i + 1) * P],
                                         ADT[:, m, 4 * q + i:4 * q + i + 1].to_broadcast([P, P]), UINC,
                                         start=(i == 0), stop=False, skip_group_check=True)
                    mm = nc.tensor.matmul(PS[:, 6 + q % 2, :], IDENTB, NEGB.unsqueeze(1).to_broadcast([P, 4, P]),
                                          start=False, stop=True, skip_group_check=True)
                    mm.then_inc(p_tok, 1)

                def z_half(n, k0=0, k1=KD):
                    for k in range(k0, k1):
                        slot, c = 2 * ((S_Z + n) % 2) + k // 4, k % 4
                        mm = three(PS[:, 5, :], ATH[:, k, t], ATL[:, k, t], WHI[:, slot, c, :], WLO[:, slot, c, :],
                                   k == 0, k == KD - 1)
                    if k1 == KD:
                        mm.then_inc(p_tok, 1)

                def y_diag(q):
                    pe.wait_ge(d_tok, d0 + DC_SC[q])
                    for i in range(4):
                        h = 4 * q + i
                        mm = nc.tensor.matmul(PS[:, h // 8, (h % 8) * HP:(h % 8 + 1) * HP], EX[q % 2][:, i, :], XD[:, h, :],
                                              start=True, stop=True)
                    mm.then_inc(p_tok, 1)

                if m:
                    pe.wait_ge(d_tok, d0 - DPC + DC_ST)
                z_half(0)
                if m >= 2:
                    pe.wait_ge(n_lo, 2 * (T_SSD + m - 2) + 2)
                    pe.wait_ge(n_hi, 2 * (T_SSD + m - 2) + 2)
                decay_rows(0)
                decay_rows(1)
                pe.wait_ge(d_tok, d0)
                for g in range(SG):
                    mm = nc.tensor.matmul(PS[:, 2 + g, :], BCT[1][64 * g:64 * g + 64, t],
                                          STATE[64 * g:64 * g + 64].rearrange("p h n -> p (h n)"), start=True, stop=True)
                mm.then_inc(p_tok, 1)
                y_diag(0)
                decay_rows(2)
                pe.wait_ge(a_tok, a0 + AC_Z[0])
                z_half(1, 0, KD // 2)
                y_diag(1)
                decay_rows(3)
                z_half(1, KD // 2, KD)
                y_diag(2)
                y_diag(3)
                pe.wait_ge(a_tok, a0 + AC_Z[1])
                for g in range(SG):
                    mm = nc.tensor.matmul(PS[64 * g:64 * g + 64, 5, :], BM[:, 64 * g:64 * g + 64],
                                          XDD[:, 8 * g:8 * g + 8, :].rearrange("p h n -> p (h n)"), start=True, stop=True)
                mm.then_inc(p_tok, 1)
                if m:
                    pe.wait_ge(n_h, Q_SSD + m)
                    pe_turn(pe, T_SSD + m - 1, V[:, m - 1, :])
            pe_pass_end(S_Z)
            pe_pass_end(S_Z + 1)
            pe.wait_ge(n_h, Q_SSD + MT)
            pe_turn(pe, T_SSD + MT - 1, V[:, MT - 1, :])

        def act_phase4(act):
            act.wait_ge(d_tok, D_S + 1)
            for t in (ECL, ECS):
                nc.scalar.activation(t[:], t[:], ACT.Exp)
            nc.scalar.activation(DEC[:], DEC[:], ACT.Exp).then_inc(a_tok, 1)
            for m in range(MT):
                d0, p0, a0 = D_S1 + DPC * m, P_S1 + PPC * m, A_S1 + APC * m

                def exp(q):
                    act.wait_ge(d_tok, d0 + DC_DIFF[q])
                    nc.scalar.activation(EX[q % 2][:], EX[q % 2][:], ACT.Exp).then_inc(a_tok, 1)

                def z_copy(n):
                    act.wait_ge(p_tok, p0 + PC_Z[n])
                    nc.scalar.activation(ZS[:, n * 512:(n + 1) * 512], PS[:, 5, :], ACT.Copy).then_inc(a_tok, 1)

                exp(0)
                exp(1)
                if m:
                    act.wait_ge(n_sq, sq_index(Q_SSD + m - 1))
                z_copy(0)
                exp(2)
                exp(3)
                z_copy(1)
                act.wait_ge(a_tok, a0 + AC_Z[1])
                nc.scalar.activation(ZS[:], ZS[:], ACT.Silu).then_inc(a_tok, 1)
                if m:
                    act_turn_hi(act, T_SSD + m - 1, m - 1)
                act.wait_ge(d_tok, d0 + DC_Y)
                act_square(Q_SSD + m, V[:, m, :], ZS[:])
            act_split(act, S_A)
            act_turn_hi(act, T_SSD + MT - 1, MT - 1)

        def dve_phase4(dve):
            ch = dve_chain
            dve.wait_ge(gain_in[1], 32)
            dve.wait_ge(p_tok, P_S + 1)
            ch.add(nc.vector.memset(STATE[:], 0.0))
            ch.add(nc.vector.tensor_copy(CSC[:].rearrange("p m h -> p (m h)"), PS[:, 0, 0:P]))
            ch.add(nc.vector.tensor_copy(ECL[:].rearrange("p m h -> p (m h)"), PS[:, 1, 0:P]))
            ch.wait()
            ch.step(nc.vector.tensor_copy(ECS[:], CSC[:]))
            nc.vector.tensor_tensor(DEC[:], ECL[:], CSC[:], ALU.subtract).then_inc(d_tok, 1)
            dve.wait_ge(a_tok, A_S1)
            ch.step(nc.vector.tensor_copy(ECL2[0:64], ECL[0:64, :, 0:8]))
            nc.vector.tensor_copy(ECL2[64:128], ECL[64:128, :, 8:16]).then_inc(d_tok, 1)
            for m in range(MT):
                d0, p0, a0 = D_S1 + DPC * m, P_S1 + PPC * m, A_S1 + APC * m
                dve.wait_ge(d_tok, d0)
                xs = V[:, m, :].rearrange("p (h n) -> p h n", h=H)
                for q in range(4):
                    e = EX[q % 2]
                    dve.wait_ge(p_tok, p0 + PC_DEC[q])
                    nc.vector.tensor_tensor(e[:], PS[:, 6 + q % 2, :].rearrange("p (i t) -> p i t", i=4),
                                            CSC[:, m, 4 * q:4 * q + 4].unsqueeze(2).to_broadcast([P, 4, P]),
                                            ALU.subtract).then_inc(d_tok, 1)
                    if q == 0:
                        nc.vector.tensor_tensor(XD[:], xs, head_bc(DT, m, HP), ALU.mult).then_inc(d_tok, 1)
                    if q == 1:
                        dve.wait_ge(d_tok, d0 + 2)
                        nc.vector.tensor_tensor(XDD[:], XD[:], head_bc(DEC, m, HP), ALU.mult).then_inc(d_tok, 1)
                    dve.wait_ge(a_tok, a0 + AC_EXP[q])
                    g = q // 2
                    nc.vector.tensor_tensor(e[:], e[:], PS[:, 4, g * P:(g + 1) * P].unsqueeze(1).to_broadcast([P, 4, P]),
                                            ALU.mult).then_inc(d_tok, 1)
                    if q == 0 and m:
                        dve_mean(dve, Q_SSD + m - 1)
                    if q == 1:
                        nc.vector.tensor_copy(BM[:], PS[:, 4, 2 * P:3 * P]).then_inc(d_tok, 1)
                        if m:
                            dve_scale(dve, Q_SSD + m - 1, V[:, m - 1, :], V[:, m - 1, :], GAM[1][:])
                ch.step(nc.vector.tensor_tensor(STATE[:], STATE[:], ECL2[:, m, :].unsqueeze(2).to_broadcast([P, 8, HP]),
                                                ALU.mult))
                dve.wait_ge(p_tok, p0 + PC_ST)
                nc.vector.tensor_tensor(STATE[:], STATE[:], PS[:, 5, :].rearrange("p (h n) -> p h n", n=HP),
                                        ALU.add).then_inc(d_tok, 1)
                if m:
                    dve_turn_lo(dve, T_SSD + m - 1, m - 1)
                yo = PS[:, 2:4, :].rearrange("p b (h n) -> p (b h) n", n=HP)
                yd = PS[:, 0:2, :].rearrange("p b (h n) -> p (b h) n", n=HP)
                ch.step(nc.vector.tensor_tensor(XD[:], xs, HROW[:, 2, :].unsqueeze(2).to_broadcast([P, H, HP]), ALU.mult))
                ch.step(nc.vector.tensor_tensor(xs, yo, head_bc(ECS, m, HP), ALU.mult))
                ch.step(nc.vector.tensor_tensor(xs, yd, xs, ALU.add))
                ch.step(nc.vector.tensor_tensor(xs, xs, XD[:], ALU.add))
                dve.wait_ge(a_tok, a0 + AC_SILU)
                nc.vector.tensor_tensor(V[:, m, :], V[:, m, :], ZS[:], ALU.mult).then_inc(d_tok, 1)
            dve_mean(dve, Q_SSD + MT - 1)
            dve_scale(dve, Q_SSD + MT - 1, V[:, MT - 1, :], V[:, MT - 1, :], GAM[1][:])
            dve_split(dve, S_A)
            dve_turn_lo(dve, T_SSD + MT - 1, MT - 1)

        def pool_phase4(pool):
            for m in range(MT):
                pool_rstd(pool, Q_SSD + m)

        def sp_router_w(sp, layer):
            if layer:
                sp.wait_ge(r_mm, 8)
            sp.dma_start(WR[:, :, 0:EG], A["moe_w_group"][layer].rearrange("(c p) g -> p c g", p=P)).then_inc(wr_in, 16)
            sp.dma_start(WR[:, :, EG:], A["moe_w_expert"][layer].rearrange("(c p) g -> p c g", p=P)).then_inc(wr_in, 16)

        def sp_residual(sp, layer, n):
            src = A["x"][0] if layer == 0 else X2
            for m in range(MT):
                j = 8 * n + m
                if j >= 2:
                    sp.wait_ge(step_use, (U_O if layer else U_A) + j - 1)
                sp.dma_start(RES[m % 2][:], rows(src, m)[:, n * 512:(n + 1) * 512]).then_inc(res_in[m % 2], 16)

        def res_count(layer, j):
            return 16 * (8 * layer + j // 2 + 1)

        def sp_phase5(sp):
            sp_slice(sp, 10)
            sp.dma_start(GAM[0][:], A["norm_ffn"][0:1, :].to_broadcast([P, D])).then_inc(gain_in[0], 16)
            sp_router_w(sp, 0)
            sp_residual(sp, 0, 0)
            sp_slice(sp, 11)
            for m in range(MT):
                if m >= 2:
                    sp.wait_ge(n_tr, 2 * (T_SGU + m - 1))
                sp.dma_start(HM[m % 2][:], rows(YG, m)).then_inc(yg_in[m % 2], 16)
                j = 8 + m
                sp.wait_ge(step_use, U_A + j - 1)
                sp.dma_start(RES[m % 2][:], rows(A["x"][0], m)[:, 512:1024]).then_inc(res_in[m % 2], 16)
            sp_slice(sp, 12)

        def yg_count(m):
            return 16 * (m // 2 + 1)

        def pe_phase5(pe):
            for m in range(MT):
                pe_token_step(pe, 9, m, U_A + m, U_A)
            pe_pass_end(9)
            for m in range(MT):
                pe_token_step(pe, 10, m, U_A + 8 + m, U_A)
                pe.wait_ge(yg_in[m % 2], yg_count(m))
                pe_turn(pe, T_SGU + m, HM[m % 2])
            pe_pass_end(10)
            for m in range(MT):
                pe.wait_ge(n_lo, 2 * (T_SGU + m) + 2)
                pe_token_step(pe, 11, m, U_A + 16 + m, U_A)
            pe_pass_end(11)
            pe_last_pass(pe, 0, 12, U_A + 24, U_A)

        def pe_last_pass(pe, layer, s, u, u0):
            for m in range(MT + 3):
                if m < MT:
                    pe_token_step(pe, s, m, u + m, u0)
                if 2 <= m <= MT + 1:
                    pe.wait_ge(n_h, Q_FFN[layer] + m - 1)
                    pe_turn(pe, T_FFN[layer] + m - 2, HM[m % 2])
                if m >= 3:
                    i = m - 3
                    if i == 0:
                        pe.wait_ge(wr_in, 32 * (layer + 1))
                    pe.wait_ge(n_hi, 2 * (T_FFN[layer] + i) + 2)
                    if 8 * layer + i:
                        pe.wait_ge(r_log, 8 * layer + i)
                    for k in range(KD):
                        mm = nc.tensor.matmul(PS[:, 5, 0:EG + NE], HTF[:, k, :], WR[:, k, :], start=(k == 0), stop=(k == KD - 1))
                    mm.then_inc(r_mm, 1)
            pe_pass_end(s)

        def act_last_pass(act, layer, u):
            for m in range(MT + 2):
                if m < MT:
                    act.wait_ge(step_use, u + m + 1)
                    if m >= 2:
                        act.wait_ge(n_tr, 2 * (T_FFN[layer] + m - 1))
                        act.wait_ge(h_st[m % 2], 16 * (4 * layer + m // 2))
                    act_square(Q_FFN[layer] + m, V[:, m, :], HM[m % 2][:])
                if m >= 2:
                    i = m - 2
                    if 8 * layer + i:
                        act.wait_ge(r_mm, 8 * layer + i)
                    for hb in range(2):
                        act.wait_ge(n_tr, 2 * (T_FFN[layer] + i) + hb + 1)
                        nc.scalar.activation(HTF[:, 4 * hb:4 * hb + 4, :], PS[:, 6 + hb, :].rearrange("p (c t) -> p c t", c=4),
                                             ACT.Copy).then_inc(n_hi, 1)

        def dve_last_pass(dve, layer, u, add):
            dve.wait_ge(gain_in[0], 48 + 16 * layer)
            for m in range(MT + 3):
                if m < MT:
                    add(m)
                if 1 <= m <= MT:
                    dve_scale(dve, Q_FFN[layer] + m - 1, V[:, m - 1, :], HM[(m - 1) % 2][:], GAM[0][:])
                if m < MT:
                    dve_mean(dve, Q_FFN[layer] + m)
                if m >= 3:
                    i = m - 3
                    dve.wait_ge(r_mm, 8 * layer + i + 1)
                    nc.vector.tensor_tensor(LOG[:, i, :], PS[:, 5, 0:EG + NE], RB[:, layer, :], ALU.add).then_inc(r_log, 1)

        def pool_last_pass(pool, layer, u):
            for m in range(MT + 1):
                if m < MT:
                    pool_rstd(pool, Q_FFN[layer] + m)
                    pool.dma_start(rows(XM, m), V[:, m, :]).then_inc(xm_st, 16)
                if m >= 1:
                    pool.wait_ge(n_h, Q_FFN[layer] + m)
                    pool.dma_start(rows(HD, m - 1), HM[(m - 1) % 2][:]).then_inc(h_st[(m - 1) % 2], 16)
            pool.wait_ge(xm_st, 16 * 8 * (layer + 1))
            for i in range(2):
                pool.wait_ge(h_st[i], 16 * 4 * (layer + 1))

        def dve_add_res(dve, layer, m, n, u, u0):
            j = 8 * n + m
            dve.wait_ge(step_mm, u + 1)
            dve.wait_ge(res_in[m % 2], res_count(layer, j))
            nc.vector.tensor_tensor(V[:, m, n * 512:(n + 1) * 512], PS[:, (u - u0) % 4, :], RES[m % 2][:],
                                    ALU.add).then_inc(step_use, 1)

        def act_phase5(act):
            act_split(act, 10)
            act_split(act, 11)
            for m in range(MT):
                act.wait_ge(step_mm, U_A + 8 + m + 1)
                act_turn_hi(act, T_SGU + m, m)
            act_split(act, 12)
            act_last_pass(act, 0, U_A + 24)

        def dve_phase5(dve):
            dve_split(dve, 10)
            for m in range(MT):
                dve_add_res(dve, 0, m, 0, U_A + m, U_A)
            dve_split(dve, 11)
            for m in range(MT):
                dve_add_res(dve, 0, m, 1, U_A + 8 + m, U_A)
                dve_turn_lo(dve, T_SGU + m, m)

            def add(n, m):
                u = U_A + 16 + 8 * n + m
                dve.wait_ge(step_mm, u + 1)
                sl = V[:, m, n * 512:(n + 1) * 512]
                nc.vector.tensor_tensor(sl, PS[:, (u - U_A) % 4, :], sl, ALU.add).then_inc(step_use, 1)

            dve_split(dve, 12)
            for m in range(MT):
                dve.wait_ge(step_use, U_A + 9 + m)
                add(0, m)
            dve_last_pass(dve, 0, U_A + 24, lambda m: add(1, m))

        def pool_phase5(pool):
            pool_last_pass(pool, 0, U_A + 24)

        OV_R, OP_R = 0, 0
        P_R = (P_S1 + PPC * MT, P_S1 + PPC * MT + 2)
        D_R = (D_S1 + DPC * MT, D_S1 + DPC * MT + 3)
        A_R = (A_S1 + APC * MT, A_S1 + APC * MT + 1)

        def act_route(act, layer):
            act.wait_ge(d_tok, D_R[layer] + 1)
            nc.scalar.activation(TMP[:], TMP[:], ACT.Exp)
            nc.scalar.activation(BK[:, :, 0:1], BK[:, :, 0:1], ACT.Exp).then_inc(a_tok, 1)

        def pe_route(pe, layer):
            pe.wait_ge(d_tok, D_R[layer] + 2)
            for i in range(MT - 1):
                nc.tensor.matmul(PS[:, 0, (i + 1) * NE:MT * NE].rearrange("p (m e) -> p m e", e=NE), ONESB,
                                 MM[:, i, :].unsqueeze(1).to_broadcast([P, MT - 1 - i, NE]), start=(i == 0), stop=False,
                                 skip_group_check=True)
            nc.tensor.matmul(PS[:, 0, 0:MT * NE], USTRB, MM[:].rearrange("p m e -> p (m e)"), start=False, stop=True,
                             skip_group_check=True).then_inc(p_tok, 1)
            for i in range(MT):
                nc.tensor.matmul(PS[:, 1, 0:NE], ONESB, MM[:, i, :], start=(i == 0), stop=(i == MT - 1))
            for i in range(2 * MT):
                m, k = divmod(i, 2)
                pe.wait_ge(o_v[layer], OV_R + i + 1)
                mm = nc.tensor.matmul(PS[:, 2, 0:NE], PH[:, i % 4, :], OT[:, k, m, :], start=(i == 0), stop=(i == 2 * MT - 1))
                if i < 2 * MT - 1:
                    mm.then_inc(o_p[layer], 1)
            mm.then_inc(p_tok, 1)

        def dve_route(dve, layer):
            ch = dve_chain
            d = D_R[layer]
            bc3 = lambda a, n: a.to_broadcast([P, MT, n])
            ch.add(nc.vector.tensor_copy(USTRB, USTR))
            ch.add(nc.vector.tensor_copy(ONESB, ONES))
            ch.add(nc.vector.memset(G8[:, :, EG:], -BIG))
            ch.add(nc.vector.tensor_copy(G8[:, :, 0:EG], LOG[:, :, 0:EG]))
            ch.wait()
            for m in range(MT):
                ch.add(nc.vector.max(GV[:, m, :], G8[:, m, :]))
            ch.wait()
            for m in range(MT):
                ch.add(nc.vector.max_index(GI[:, m, :], GV[:, m, :], G8[:, m, :]))
            ch.wait()
            ch.step(nc.vector.tensor_copy(GIF[:], GI[:, :, 0:1]))
            ch.add(nc.vector.tensor_tensor(TMP[:], LOG[:, :, 0:EG], bc3(GV[:, :, 0:1], EG), ALU.subtract))
            ch.step(nc.vector.tensor_tensor(GM[:], IOTA[:, 0:EG].unsqueeze(1).to_broadcast([P, MT, EG]), bc3(GIF[:], EG),
                                            ALU.is_equal))
            ch.step(nc.vector.tensor_scalar(GM[:], GM[:], BIG, -BIG, ALU.mult, ALU.add))
            ch.step(nc.vector.tensor_tensor(EL[:].rearrange("p m (g e) -> p m g e", g=EG),
                                            LOG[:, :, EG:].rearrange("p m (g e) -> p m g e", g=EG),
                                            GM[:].unsqueeze(3).to_broadcast([P, MT, EG, GE]), ALU.add))
            for m in range(MT):
                ch.add(nc.vector.max(EV[:, m, :], EL[:, m, :]))
            ch.wait()
            for m in range(MT):
                ch.add(nc.vector.max_index(EI[:, m, :], EV[:, m, :], EL[:, m, :]))
            ch.add(nc.vector.tensor_tensor(BK[:, :, 0:1], EV[:, :, 1:2], EV[:, :, 0:1], ALU.subtract))
            ch.wait()
            nc.vector.tensor_copy(EIF[:], EI[:, :, 0:2]).then_inc(d_tok, 1)
            dve.wait_ge(d_tok, d + 1)
            for k in range(2):
                ch.add(nc.vector.tensor_tensor(OH[:, k], IOTA[:, 0:NE].unsqueeze(1).to_broadcast([P, MT, NE]),
                                               bc3(EIF[:, :, k:k + 1], NE), ALU.is_equal))
            ch.wait()
            nc.vector.tensor_tensor(MM[:], OH[:, 0], OH[:, 1], ALU.add).then_inc(d_tok, 1)
            for k in range(2):
                ch.add(nc.vector.tensor_tensor(OT[:, k], OH[:, k], TOKID.unsqueeze(2).to_broadcast([P, MT, NE]), ALU.mult))
            dve.wait_ge(a_tok, A_R[layer] + 1)
            ch.step(nc.vector.tensor_reduce(DEN[:, :, 0:1], TMP[:], AX, ALU.add))
            ch.step(nc.vector.tensor_scalar(DEN[:, :, 1:2], BK[:, :, 0:1], 1.0, None, ALU.add))
            ch.step(nc.vector.tensor_tensor(DEN[:, :, 2:3], DEN[:, :, 0:1], DEN[:, :, 1:2], ALU.mult))
            ch.step(nc.vector.reciprocal(GATE[:, :, 0:1], DEN[:, :, 2:3]))
            ch.step(nc.vector.tensor_tensor(GATE[:, :, 1:2], GATE[:, :, 0:1], BK[:, :, 0:1], ALU.mult))
            dve.wait_ge(p_tok, P_R[layer] + 1)
            pos = PS[:, 0, 0:MT * NE].rearrange("p (m e) -> p m e", e=NE)
            for k in range(2):
                ch.step(nc.vector.tensor_tensor(PR[:], pos, OH[:, k], ALU.mult))
                ch.step(nc.vector.tensor_reduce(POSK[:, :, k:k + 1], PR[:], AX, ALU.add))
            for i in range(2 * MT):
                m, k = divmod(i, 2)
                if i >= 4:
                    dve.wait_ge(o_p[layer], OP_R + i - 3)
                nc.vector.tensor_scalar(PH[:, i % 4, :], IOTA, POSK[:, m, k:k + 1], None, ALU.is_equal).then_inc(o_v[layer], 1)
            dve.wait_ge(p_tok, P_R[layer] + 2)
            nc.vector.tensor_copy(IDXA[:], PS[:, 2, 0:NE]).then_inc(d_tok, 1)

        def dve_route_rest(layer):
            ch = dve_chain
            ch.step(nc.vector.tensor_copy(NOV[:, 0, :], PS[:, 1, 0:NE]))
            ch.step(nc.vector.tensor_tensor(CMP[:], NOV[:, 0, :].unsqueeze(2).to_broadcast([P, NE, 7]),
                                            THRESH.unsqueeze(1).to_broadcast([P, NE, 7]), ALU.is_gt))
            ch.step(nc.vector.tensor_reduce(NOV[:, 1, :], CMP[:], AX, ALU.add))
            ch.step(nc.vector.tensor_tensor_scan(NOV[:, 2, :], ONES[:, 0:NE], NOV[:, 1, :], 0.0, ALU.mult, ALU.add))
            ch.step(nc.vector.tensor_tensor(CMS[:], NOV[:, 2, :].unsqueeze(1).to_broadcast([P, OVF, NE]),
                                            SLOTI.unsqueeze(2).to_broadcast([P, OVF, NE]), ALU.is_le))
            ch.step(nc.vector.tensor_reduce(ESL[:, 0:OVF], CMS[:], AX, ALU.add))
            ch.step(nc.vector.tensor_scalar(ESL[:, 0:OVF], ESL[:, 0:OVF], float(NE - 1), None, ALU.min))
            ch.step(nc.vector.tensor_copy(ESL[:, OVF:OVF + 1], NOV[:, 2, NE - 1:NE]))
            ch.add(nc.vector.tensor_copy(REGS[:], ESL[:]))
            ch.step(nc.vector.tensor_tensor(NOV[:, 0, :], NOV[:, 2, :], NOV[:, 1, :], ALU.subtract))
            ch.step(nc.vector.tensor_scalar(NOV[:, 0, :], NOV[:, 0, :], float(BLK), float((NE - 1) * BLK), ALU.mult, ALU.add))
            for k in range(2):
                ch.step(nc.vector.tensor_tensor(PR[:], OH[:, k], NOV[:, 0, :].unsqueeze(1).to_broadcast([P, MT, NE]), ALU.mult))
                ch.step(nc.vector.tensor_reduce(BK[:, :, k:k + 1], PR[:], AX, ALU.add))
            ch.step(nc.vector.tensor_scalar(EIF[:], EIF[:], float(BLK), None, ALU.mult))
            ch.step(nc.vector.tensor_tensor(BK[:], BK[:], EIF[:], ALU.subtract))
            ch.step(nc.vector.tensor_scalar(VPOS[:], POSK[:], float(BLK), None, ALU.is_ge))
            ch.step(nc.vector.tensor_tensor(BK[:], BK[:], VPOS[:], ALU.mult))
            ch.step(nc.vector.tensor_tensor(BK[:], BK[:], EIF[:], ALU.add))
            ch.step(nc.vector.tensor_tensor(BK[:], BK[:], POSK[:], ALU.add))
            ch.step(nc.vector.tensor_copy(ROWI[:], BK[:]))
            nc.vector.tensor_scalar(VPOS[:], BK[:], -float(NE * BLK), None, ALU.add).then_inc(dve_loop[layer], 1)


        UNITS, HALF = 6 * NE, NE // 2

        def unit(i, par, j):
            if isinstance(i, int) and 2 * i + par == 0:
                return j, j, 0
            if isinstance(i, int) and i == HALF:
                n = UNITS - 2 + j
                return n, n % 12, n // 12
            if par:
                return i * 12 + (4 + j), (4 + j) % 12, i + (4 + j) // 12
            return i * 12 + (j - 2), (10 + j) % 12, i + ((10 + j) // 12 - 1)

        def part(i, par, j):
            return unit(i if isinstance(i, int) else 1, par, j)[0] % 4

        def raw_base(layer, slot):
            return 16 * (N_SL0 + (len(SLICES) - N_SL0 + 16) * layer) if slot < 2 else 16 * 16 * layer

        def sp_moe_loads(sp, layer, i, par, j0, j1):
            e = i * 2 + par
            for j in range(j0, j1):
                n, slot, _ = unit(i, par, j)
                if not isinstance(n, int) or n >= 12:
                    sp.wait_ge(m_lo, n + (UNITS * layer - 11))
                if j < 4 and not (isinstance(i, int) and i == HALF):
                    w = A["moe_w1" if j < 2 else "moe_w3"][layer][bass.ds(e, 1)]
                    src = w.rearrange("o (h c p) n -> (o h) p c n", p=P, c=4)[j % 2]
                else:
                    w = A["moe_w2"][layer][bass.ds(e - 1, 1)]
                    src = w.rearrange("o (c p) (h n) -> (o h) p c n", p=P, n=512)[j % 2]
                sp.dma_start(MRAW[slot][:], src).then_inc(raw_in[slot], 16)

        def sp_moe_store(sp, layer, i, par):
            f = i * 2 + par
            sp.wait_ge(m_yev, f * 2 + (2 * NE * layer + 2))
            sp.dma_start(YB[bass.ds(f * BLK, BLK), :], YSB[par][:]).then_inc(y_st[par], 16)

        def sp_moe_prefetch(sp, layer):
            slices = len(SLICES) if layer else N_SL0
            sp.wait_ge(w_lo_done, 2 * slices)
            sp_moe_loads(sp, layer, 0, 0, 0, 2)
            sp.wait_ge(step_mm, (U_O + 8 if layer else U_A + 24) + 4)
            sp_moe_loads(sp, layer, 0, 0, 2, 4)
            sp_moe_loads(sp, layer, 0, 1, 0, 2)
            sp.wait_ge(step_mm, (U_O + 8 if layer else U_A + 24) + MT)
            sp_moe_loads(sp, layer, 0, 1, 2, 6)

        def sp_moe(sp, layer):
            if layer == 0:
                sp.wait_ge(n_h, Q_SSD + MT)
                sp.dma_start(GAM[1][:], A["norm_mix"][1:2, :].to_broadcast([P, D])).then_inc(gain_in[1], 16)
            else:
                sp.dma_start(GAM[1][:], A["norm_final"].rearrange("(o n) -> o n", o=1).to_broadcast([P, D]))\
                    .then_inc(gain_in[1], 16)
            for par in range(2):
                sp_moe_loads(sp, layer, 1, par, 0, 6)
            with sp.Fori(2, HALF) as i:
                for par in range(2):
                    sp_moe_loads(sp, layer, i, par, 0, 6)
                    sp_moe_store(sp, layer, i - 2, par)
            sp_moe_loads(sp, layer, HALF, 0, 0, 2)
            for f in range(NE - 4, NE):
                sp_moe_store(sp, layer, f // 2, f % 2)

        def pe_moe(pe, layer):
            c1, c2, cu = NE * layer, 2 * NE * layer, UNITS * layer

            def unit_products(i, par, j, o, lh, ll, k0, first, last):
                pe.wait_ge(m_lo, unit(i, par, j)[0] + (cu + 1))
                slot = part(i, par, j)
                for c in range(4):
                    mm = three(o, lh[:, k0 + c, :], ll[:, k0 + c, :], WHI[:, slot, c, :], WLO[:, slot, c, :],
                               first and c == 0, last and c == 3)
                mm.then_inc(m_unit, 1)

            def turn_x(i, par):
                pe.wait_ge(xg_in[par], i * 16 + 16 * (HALF * layer + 1))
                pe.wait_ge(m_xlo, i * 4 + (2 * par + c2))
                for hb in range(2):
                    for c in range(4):
                        k = 4 * hb + c
                        t = nc.tensor.transpose(PS[:, 5 + hb, c * P:(c + 1) * P], XG[par][:, k * P:(k + 1) * P], IDENT)
                    t.then_inc(m_xtr, 1)

            def up(i, par):
                pe.wait_ge(m_xlo, i * 4 + (2 * par + 2 + c2))
                pe.wait_ge(m_gmul, i * 2 + (par + c1))
                for j in range(4):
                    unit_products(i, par, j, PS[:, j // 2, :], XTH, XTL, 4 * (j % 2), j % 2 == 0, j % 2 == 1)

            def down(i, par, j0):
                pe.wait_ge(m_glo, i * 2 + (par + c1))
                pe.wait_ge(m_yev, i * 4 + (2 * par - 2 + c2))
                for h in range(2):
                    unit_products(i, par, j0 + h, PS[:, 3 + h, :], GTH, GTL, 0, True, True)

            def turn_g(i, par):
                pe.wait_ge(m_gmul, i * 2 + (par + 1 + c1))
                for c in range(4):
                    t = nc.tensor.transpose(PS[:, 2, c * P:(c + 1) * P], GAT[:, c * P:(c + 1) * P], IDENT)
                t.then_inc(m_gtr, 1)

            turn_x(0, 0)
            up(0, 0)
            turn_x(0, 1)
            turn_g(0, 0)
            up(0, 1)
            turn_x(1, 0)
            down(0, 1, 4)
            turn_g(0, 1)
            with pe.Fori(1, HALF - 1) as i:
                up(i, 0)
                turn_x(i, 1)
                down(i, 0, 4)
                turn_g(i, 0)
                up(i, 1)
                turn_x(i + 1, 0)
                down(i, 1, 4)
                turn_g(i, 1)
            i = HALF - 1
            up(i, 0)
            turn_x(i, 1)
            down(i, 0, 4)
            turn_g(i, 0)
            up(i, 1)
            down(i, 1, 4)
            turn_g(i, 1)
            down(HALF, 0, 0)

        def act_hi(act, layer, i, par, j):
            n, slot, lap = unit(i, par, j)
            act.wait_ge(raw_in[slot], lap * 16 + (raw_base(layer, slot) + 16))
            if not isinstance(n, int) or n >= 4:
                act.wait_ge(m_unit, n + (UNITS * layer - 3))
            nc.scalar.activation(WHI[:, part(i, par, j)], MRAW[slot][:], ACT.Copy).then_inc(m_hi, 1)

        def pool_first_lo(pool, layer):
            for j in range(4):
                n, slot, _ = unit(0, 0, j)
                pool.wait_ge(m_hi, n + (UNITS * layer + 1))
                nc.gpsimd.tensor_tensor(WLO[:, n], MRAW[slot][:], WHI[:, n].bitcast(F32), ALU.subtract).then_inc(m_lo, 1)

        def act_moe(act, layer):
            c1, c2, cu = NE * layer, 2 * NE * layer, UNITS * layer

            def hi(i, par, j):
                act_hi(act, layer, i, par, j)

            def x_hi(i, par):
                for hb in range(2):
                    act.wait_ge(m_xtr, i * 4 + (2 * par + hb + 1 + c2))
                    nc.scalar.activation(XTH[:, 4 * hb:4 * hb + 4, :], PS[:, 5 + hb, :].rearrange("p (c t) -> p c t", c=4),
                                         ACT.Copy).then_inc(m_xhi, 1)

            def g_hi(i, par):
                act.wait_ge(m_gtr, i * 2 + (par + c1))
                nc.scalar.activation(GTH[:], PS[:, 2, :].rearrange("p (c t) -> p c t", c=4), ACT.Copy).then_inc(m_ghi, 1)

            def y_out(i, par, j0):
                si, sp_ = (i, 0) if par else (i - 1, 1)
                if not isinstance(i, int) or i + HALF * layer > 1:
                    act.wait_ge(y_st[par], i * 16 + 16 * (HALF * layer - 1))
                for h in range(2):
                    act.wait_ge(m_unit, unit(si, sp_, j0 + h)[0] + (cu + 1))
                    nc.scalar.activation(YSB[par][:, h * 512:(h + 1) * 512], PS[:, 3 + h, :], ACT.Copy).then_inc(m_yev, 1)

            def silu(i, par):
                act.wait_ge(m_unit, unit(i, par, 1)[0] + (cu + 1))
                act.wait_ge(m_gmul, i * 2 + (par + c1))
                nc.scalar.activation(SIL[:], PS[:, 0, :], ACT.Silu).then_inc(m_silu, 1)

            def step(i, par):
                e = 2 * i + par if isinstance(i, int) else NE
                if e:
                    hi(i, par, 0)
                    hi(i, par, 1)
                x_hi(i, par)
                if e:
                    hi(i, par, 2)
                    hi(i, par, 3)
                if e >= 1:
                    g_hi(i, par)
                if e >= 2:
                    y_out(i, par, 4)
                if e >= 1:
                    hi(i, par, 4)
                    hi(i, par, 5)
                silu(i, par)

            step(0, 0)
            step(0, 1)
            step(1, 0)
            step(1, 1)
            with act.Fori(2, HALF) as i:
                step(i, 0)
                step(i, 1)
            g_hi(HALF, 0)
            y_out(HALF, 0, 4)
            hi(HALF, 0, 0)
            hi(HALF, 0, 1)
            y_out(HALF, 1, 0)

        def dve_moe(dve, layer):
            c1, c2, cu = NE * layer, 2 * NE * layer, UNITS * layer

            def lo(i, par, j):
                n, slot, _ = unit(i, par, j)
                dve.wait_ge(m_hi, n + (cu + 1))
                q = part(i, par, j)
                nc.vector.tensor_tensor(WLO[:, q], MRAW[slot][:], WHI[:, q].bitcast(F32), ALU.subtract).then_inc(m_lo, 1)

            def x_lo(i, par):
                for hb in range(2):
                    dve.wait_ge(m_xhi, i * 4 + (2 * par + hb + 1 + c2))
                    sl = (slice(None), slice(4 * hb, 4 * hb + 4))
                    nc.vector.tensor_tensor(XTL[sl], PS[:, 5 + hb, :].rearrange("p (c t) -> p c t", c=4),
                                            XTH[sl].bitcast(F32), ALU.subtract).then_inc(m_xlo, 1)

            def g_lo(i, par):
                dve.wait_ge(m_ghi, i * 2 + (par + c1))
                nc.vector.tensor_tensor(GTL[:], PS[:, 2, :].rearrange("p (c t) -> p c t", c=4), GTH[:].bitcast(F32),
                                        ALU.subtract).then_inc(m_glo, 1)

            def gate(i, par):
                si, sp_ = (i, 0) if par else (i - 1, 1)
                dve.wait_ge(m_silu, i * 2 + (par + c1))
                dve.wait_ge(m_unit, unit(si, sp_, 3)[0] + (cu + 1))
                dve.wait_ge(m_gtr, i * 2 + (par - 1 + c1))
                nc.vector.tensor_tensor(GAT[:], SIL[:], PS[:, 1, :], ALU.mult).then_inc(m_gmul, 1)

            def step(i, par):
                e = 2 * i + par if isinstance(i, int) else NE
                if e >= 1:
                    lo(i, par, 0)
                    lo(i, par, 1)
                    gate(i, par)
                x_lo(i, par)
                if e >= 1:
                    lo(i, par, 2)
                    lo(i, par, 3)
                if e >= 1:
                    g_lo(i, par)
                    lo(i, par, 4)
                    lo(i, par, 5)

            step(0, 0)
            step(0, 1)
            with dve.Fori(1, HALF) as i:
                step(i, 0)
                step(i, 1)
            gate(HALF, 0)
            g_lo(HALF, 0)
            lo(HALF, 0, 0)
            lo(HALF, 0, 1)

        def pool_moe(pool, layer):
            c2 = 2 * NE * layer

            def gather(i, par):
                e = i * 2 + par
                if not isinstance(i, int) or e >= 2:
                    pool.wait_ge(m_xtr, i * 4 + (2 * par - 2 + c2))
                pool.wait_ge(d_tok, D_R[layer] + 3)
                nc.gpsimd.tensor_copy(CUR[par][:, 0:1], IDXA[:, bass.ds(e, 1)]).then_inc(cur_set, 1)
                pool.wait_ge(cur_set, e + (NE * layer + 1))
                pool.sem_inc(gather_go, 1)
                pool.indirect_dma_start(out=XG[par][:], out_offset=None, in_=HD[:, :],
                                        in_offset=bass.IndirectOffsetOnAxis(ap=CUR[par][:, 0:1], axis=0))\
                    .then_inc(xg_in[par], 16)

            gather(0, 0)
            gather(0, 1)
            with pool.Fori(1, HALF) as i:
                gather(i, 0)
                gather(i, 1)

        OV_B, OP_B = OV_R + 2 * MT, OP_R + 2 * MT - 1
        O_UNITS = [MRAW[2 + i] for i in range(6)]

        def ovf_loop(eng, body, each=None):
            n = eng.value_load(REGS[0:1, OVF:OVF + 1], min_val=0, max_val=OVF)
            with eng.If(n > 0):
                body(0)
                if each:
                    each(0)
                with eng.If(n > 1):
                    with eng.Fori(1, OVF) as s:
                        with eng.If(n > s):
                            body(s)
                        if each:
                            each(s)

        def sp_ovf(sp, layer):
            if layer == 0:
                sp.wait_ge(zero_st, 16 * OVF)

            def body(s):
                if isinstance(s, int):
                    sp.wait_ge(m_lo, UNITS * (layer + 1))
                else:
                    sp.wait_ge(o_p[layer], s * 5 + OP_B)
                e = sp.value_load(REGS[0:1, bass.ds(s, 1)], min_val=0, max_val=NE - 1)
                for i, name in enumerate(("moe_w1", "moe_w3")):
                    w = A[name][layer][bass.ds(e, 1)].rearrange("o (h c p) n -> (o h) p c n", p=P, c=4)
                    for h in range(2):
                        sp.dma_start(O_UNITS[2 * i + h][:], w[h]).then_inc(o_raw[layer], 16)
                w = A["moe_w2"][layer][bass.ds(e, 1)].rearrange("o (c p) (h n) -> (o h) p c n", p=P, n=512)
                sp.wait_ge(o_xg[layer], s * 16 + 16)
                for h in range(2):
                    sp.dma_start(O_UNITS[4 + h][:], w[h]).then_inc(o_w2[layer], 16)
                sp.wait_ge(o_v[layer], s * 6 + (OV_B + 6))
                sp.dma_start(YB[bass.ds((s + NE) * BLK, BLK), :], OY[:]).then_inc(o_yst[layer], 16)

            ovf_loop(sp, body)

        def pool_ovf(pool, layer):
            def body(s):
                pool.wait_ge(o_v[layer], s * 6 + (OV_B + 2))
                pool.sem_inc(gather_go, 1)
                pool.indirect_dma_start(out=OXG[:], out_offset=None, in_=HD[:, :],
                                        in_offset=bass.IndirectOffsetOnAxis(ap=OIDX[:, 0:1], axis=0)).then_inc(o_xg[layer], 16)
                pool.wait_ge(o_yst[layer], s * 16 + 16)

            ovf_loop(pool, body)

        def pe_ovf(pe, layer):
            def body(s):
                ov = s * 6 + OV_B
                pe.wait_ge(o_v[layer], ov + 1)
                for i in range(2 * MT):
                    mm = nc.tensor.matmul(PS[:, 2, 0:1], OHB[:, i, :], TOKID[:, i // 2:i // 2 + 1], start=(i == 0),
                                          stop=(i == 2 * MT - 1))
                mm.then_inc(o_p[layer], 1)
                pe.wait_ge(o_xg[layer], s * 16 + 16)
                for k in range(KD):
                    mm = nc.tensor.transpose(PS[:, 5 + k // 4, k % 4 * P:(k % 4 + 1) * P], OXG[:, k * P:(k + 1) * P], IDENT)
                mm.then_inc(o_p[layer], 1)
                pe.wait_ge(o_v[layer], ov + 3)
                pe.wait_ge(o_raw[layer], s * 64 + 64)
                for i in range(2):
                    for k in range(KD):
                        mm = nc.tensor.matmul(PS[:, i, :], OXT[:, k, :], O_UNITS[2 * i + k // 4][:, k % 4, :], start=(k == 0),
                                              stop=(k == KD - 1))
                mm.then_inc(o_p[layer], 1)
                pe.wait_ge(o_v[layer], ov + 4)
                for c in range(4):
                    mm = nc.tensor.transpose(PS[:, 2, c * P:(c + 1) * P], OGAT[:, c * P:(c + 1) * P], IDENT)
                mm.then_inc(o_p[layer], 1)
                pe.wait_ge(o_v[layer], ov + 5)
                pe.wait_ge(o_w2[layer], s * 32 + 32)
                for h in range(2):
                    for c in range(4):
                        mm = nc.tensor.matmul(PS[:, 3 + h, :], OGT[:, c, :], O_UNITS[4 + h][:, c, :], start=(c == 0), stop=(c == 3))
                mm.then_inc(o_p[layer], 1)

            ovf_loop(pe, body)

        def act_ovf(act, layer):
            def body(s):
                act.wait_ge(o_p[layer], s * 5 + (OP_B + 3))
                nc.scalar.activation(OSIL[:], PS[:, 0, :], ACT.Silu).then_inc(o_a[layer], 1)

            ovf_loop(act, body)

        def dve_ovf(dve, layer):
            def body(s):
                op = s * 5 + OP_B
                dve.wait_ge(dve_loop[layer], s + 1)
                nc.vector.tensor_tensor(OHB[:], IOTA.unsqueeze(1).to_broadcast([P, 2 * MT, P]),
                                        VPOS[:].rearrange("p m k -> p (m k)").unsqueeze(2).to_broadcast([P, 2 * MT, P]),
                                        ALU.is_equal).then_inc(o_v[layer], 1)
                dve.wait_ge(o_p[layer], op + 1)
                nc.vector.tensor_copy(OIDX[:], PS[:, 2, 0:1]).then_inc(o_v[layer], 1)
                dve.wait_ge(o_p[layer], op + 2)
                nc.vector.tensor_copy(OXT[:].rearrange("p k t -> p (k t)"), two_banks(5)).then_inc(o_v[layer], 1)
                dve.wait_ge(o_a[layer], s + 1)
                nc.vector.tensor_tensor(OGAT[:], OSIL[:], PS[:, 1, :], ALU.mult).then_inc(o_v[layer], 1)
                dve.wait_ge(o_p[layer], op + 4)
                nc.vector.tensor_copy(OGT[:].rearrange("p c t -> p (c t)"), PS[:, 2, :]).then_inc(o_v[layer], 1)
                dve.wait_ge(o_p[layer], op + 5)
                nc.vector.tensor_copy(OY[:], two_banks(3)).then_inc(o_v[layer], 1)

            def each(s):
                dve.wait_ge(dve_loop[layer], s + 1)
                nc.vector.tensor_scalar(VPOS[:], VPOS[:], -float(BLK), None, ALU.add).then_inc(dve_loop[layer], 1)

            ovf_loop(dve, body, each)

        Q_NEXT = (Q_MIX1, Q_FIN)

        def sp_comb_x(sp, m):
            sp.dma_start(CX[m][:], rows(XM, m)).then_inc(cx_in[m], 16)

        def sp_combine(sp, layer):
            for m in range(MT + 2):
                if 3 <= m < MT:
                    sp.wait_ge(c_add, 2 * MT * layer + 2 * m - 4)
                    sp_comb_x(sp, m)
                if layer and m >= 2:
                    i = m - 2
                    sp.wait_ge(n_h, Q_FIN + i + 1)
                    sp.dma_start(rows(out, i), HN[i % 2][:]).then_inc(out_st[i % 2], 16)
            if layer:
                for st in out_st:
                    sp.wait_ge(st, 16 * 4)
            else:
                sp.wait_ge(c_add, 2 * MT - 2)
                sp_slice(sp, S_I)
                for m in range(MT):
                    sp.wait_ge(c_add, 2 * m + 2)
                    sp.dma_start(rows(X2, m), CX[m][:]).then_inc(x2_st, 16)

        def pool_combine(pool, layer):
            for i in range(2):
                pool.wait_ge(y_st[i], 16 * HALF * (layer + 1))
            for i in range(2 * MT + 4):
                if i < 2 * MT:
                    m, k = divmod(i, 2)
                    if i >= 4:
                        pool.wait_ge(c_add, 2 * MT * layer + i - 3)
                    pool.indirect_dma_start(out=CY[i % 4][:], out_offset=None, in_=YB[:, :],
                                            in_offset=bass.IndirectOffsetOnAxis(ap=ROWI[:, m, k:k + 1], axis=0))\
                        .then_inc(cy_in[i % 4], 16)
                if i >= 4 and i % 2 == 1:
                    pool_rstd(pool, Q_NEXT[layer] + (i - 5) // 2)

        def dve_combine(dve, layer):
            q0 = Q_NEXT[layer]
            dve.wait_ge(gain_in[1], 48 + 16 * layer)

            def scale(m):
                if m >= 2:
                    if layer == 0:
                        dve.wait_ge(n_tr, 2 * (T_MIX1 + m - 1))
                    else:
                        dve.wait_ge(out_st[m % 2], 16 * (m // 2))
                dve_scale(dve, q0 + m, CX[m][:], HN[m % 2][:], GAM[1][:])

            for m in range(MT + 2):
                if m < MT:
                    dve.wait_ge(cx_in[m], 16 * (layer + 1))
                    for k in range(2):
                        i = 2 * m + k
                        dve.wait_ge(cy_in[i % 4], 16 * (4 * layer + i // 4 + 1))
                        if k:
                            dve.wait_ge(c_add, 2 * MT * layer + i)
                        if k and m:
                            dve_mean(dve, q0 + m - 1)
                        nc.vector.scalar_tensor_tensor(out=CX[m][:], in0=CY[i % 4][:], scalar=GATE[:, m, k:k + 1],
                                                       in1=CX[m][:], op0=ALU.mult, op1=ALU.add).then_inc(c_add, 1)
                if m == MT:
                    dve_mean(dve, q0 + m - 1)
                if layer == 0 and m == MT + 1:
                    dve_split(dve, S_I)
                if layer == 0 and m >= 2:
                    dve_turn_lo(dve, T_MIX1 + m - 2, m - 2)
                if 1 <= m <= MT:
                    scale(m - 1)

        def act_combine(act, layer):
            for m in range(MT + 1):
                if m < MT:
                    act.wait_ge(c_add, 2 * MT * layer + 2 * m + 2)
                    if m >= 2:
                        if layer == 0:
                            act.wait_ge(n_tr, 2 * (T_MIX1 + m - 1))
                        else:
                            act.wait_ge(out_st[m % 2], 16 * (m // 2))
                    act_square(Q_NEXT[layer] + m, CX[m][:], HN[m % 2][:])
                if layer == 0 and m == MT:
                    act_split(act, S_I)
                if layer == 0 and m >= 1:
                    act_turn_hi(act, T_MIX1 + m - 1, m - 1)

        def pe_combine(pe, layer):
            if layer == 0:
                for m in range(MT):
                    pe.wait_ge(n_h, Q_MIX1 + m + 1)
                    pe_turn(pe, T_MIX1 + m, HN[m % 2])

        def ident_n(t):
            return 1 if t == 0 else 6 * t - 4

        def lru_n(t, i):
            return min(t + 2, KD) + 5 * t + i

        def sp_phase10(sp):
            sp_slice(sp, 14)
            sp.wait_ge(phase_s, 4 * 8)
            for t in range(4):
                sp_gate_w(sp, t)
            sp_slice(sp, 15)
            for t in range(4, KD):
                sp_gate_w(sp, t)
            sp_slice(sp, 16)
            sp_slice(sp, 17)
            sp_router_w(sp, 1)
            sp_slice(sp, 18)

        def sp_gate_w(sp, t):
            if t >= 4:
                sp.wait_ge(l_p, 2 * (t - 4) + 2)
            for i, n in enumerate(("od_w_a", "od_w_i")):
                sp.dma_start(LW[:, t % 4, i, :], A[n][0, t]).then_inc(l_w[t % 4], 16)

        def pe_phase10(pe):
            for j in range(2 * KD):
                if j < 2 * KD:
                    s = S_I + j // 4
                    pe_chan_step(pe, s, j % 4, U_I + j, U_I)
                    if j % 4 == 3:
                        pe_pass_end(s)
                if 1 <= j <= KD:
                    t = j - 1
                    pe.wait_ge(l_w[t % 4], 32 * (t // 4 + 1))
                    pe.wait_ge(step_use, U_I + t + 1)
                    if t:
                        pe.wait_ge(l_a, lru_n(t - 1, 2))
                    for i in range(2):
                        for nh in range(2):
                            mm = nc.tensor.matmul(PS[:, 4 + 2 * i + nh, :], LW[:, t % 4, i, :], XRC[t % 2][:, nh * 512:(nh + 1) * 512],
                                                  start=True, stop=True)
                        mm.then_inc(l_p, 1)

        def act_phase10(act):
            act.wait_ge(l_taps, 1)
            nc.scalar.activation(LSP[:, 1, :], LSP[:, 0, :], ACT.Exp, scale=-1.0).then_inc(l_taps, 1)
            for j in range(2 * KD):
                if j == 1:
                    act.wait_ge(x2_st, 16 * MT)
                if j in (1, 4, 8, 12):
                    act_split(act, S_I + 1 + j // 4)
                if j < KD:
                    t = j
                    act.wait_ge(step_mm, U_I + j + 1)
                    if t >= 2:
                        act.wait_ge(l_v, t - 1)
                    nc.scalar.activation(XRC[t % 2][:], two_banks(2 * (j % 2)), ACT.Identity,
                                         bias=COLV[:, CV_OB + t:CV_OB + t + 1],
                                         scale=COLV[:, CV_OW + 24 + t:CV_OW + 25 + t]).then_inc(l_a, 1)
                if 1 <= j <= KD:
                    act_lru(act, j - 1)
                if j >= KD:
                    act.wait_ge(step_mm, U_I + j + 1)
                    act.wait_ge(l_v, j - 1)
                    nc.scalar.activation(XRC[j % 2][:], two_banks(2 * (j % 2)), ACT.Gelu_apprx_tanh).then_inc(step_use, 1)

        def act_lru(act, t):
            a, ig, th = RGA[:], RGI[:], RGT[:]
            if t == 0:
                act.wait_ge(l_taps, 3)
            if t:
                act.wait_ge(l_v, t)
            act.wait_ge(l_p, 2 * t + 1)
            nc.scalar.activation(a, two_banks(4), ACT.Sigmoid, bias=COLV[:, CV_BA + t:CV_BA + t + 1]).then_inc(l_a, 1)
            act.wait_ge(l_p, 2 * t + 2)
            nc.scalar.activation(ig, two_banks(6), ACT.Sigmoid, bias=COLV[:, CV_BI + t:CV_BI + t + 1]).then_inc(l_a, 1)
            act.wait_ge(l_a, lru_n(t, 1))
            nc.scalar.activation(th, a, ACT.Tanh, scale=LSP[:, 2, t:t + 1]).then_inc(l_a, 1)
            nc.scalar.activation(a, a, ACT.Exp, scale=LSP[:, 3, t:t + 1]).then_inc(l_a, 1)
            act.wait_ge(l_a, lru_n(t, 3))
            nc.scalar.activation(th, th, ACT.Sqrt).then_inc(l_a, 1)

        def dve_phase10(dve):
            ch = dve_chain
            lam = COLV[:, CV_LAM:CV_LAM + KD]
            nc.vector.scalar_tensor_tensor(out=LSP[:, 0, :], in0=lam, scalar=-1.0, in1=lam, op0=ALU.mult, op1=ALU.max).then_inc(l_taps, 1)
            dve.wait_ge(l_taps, 2)
            log1p_of(ch, LSP[:, 1, :], LSP[:, 2, :], LSP[:, 3, :])
            ch.step(nc.vector.tensor_scalar(LSP[:, 0, :], lam, -1.0, 0.0, ALU.mult, ALU.max))
            ch.step(nc.vector.tensor_tensor(LSP[:, 0, :], LSP[:, 0, :], LSP[:, 1, :], ALU.add))
            ch.step(nc.vector.tensor_scalar(LSP[:, 2, :], LSP[:, 0, :], LRU_C / 2, None, ALU.mult))
            nc.vector.tensor_scalar(LSP[:, 3, :], LSP[:, 0, :], -LRU_C, None, ALU.mult).then_inc(l_taps, 1)
            for j in range(2 * KD):
                if j in (1, 4, 8, 12):
                    dve_split(dve, S_I + 1 + j // 4)
                if j < KD:
                    t = j
                    dve.wait_ge(l_a, ident_n(t))
                    src, acc = two_banks(2 * (j % 2)), XRC[t % 2]
                    for tap in (2, 1, 0):
                        sh = 3 - tap
                        w = COLV[:, CV_OW + 8 * tap + t:CV_OW + 8 * tap + t + 1]
                        ins = nc.vector.scalar_tensor_tensor(out=acc[:, sh:], in0=src[:, :T - sh], scalar=w, in1=acc[:, sh:],
                                                             op0=ALU.mult, op1=ALU.add)
                        if tap:
                            ch.step(ins)
                        else:
                            ins.then_inc(step_use, 1)
                if 1 <= j <= KD:
                    t = j - 1
                    x, a, ig, th = XRC[t % 2][:], RGA[:], RGI[:], RGT[:]
                    dve.wait_ge(l_a, lru_n(t, 2))
                    dve.wait_ge(step_use, U_I + t + 1)
                    ch.step(nc.vector.tensor_tensor(ig, ig, x, ALU.mult))
                    dve.wait_ge(l_a, lru_n(t, 5))
                    ch.step(nc.vector.scalar_tensor_tensor(out=th, in0=a, scalar=1.0, in1=th, op0=ALU.add, op1=ALU.mult))
                    ch.step(nc.vector.tensor_tensor(ig, ig, th, ALU.mult))
                    nc.vector.tensor_tensor_scan(V[:, t, :], a, ig, 0.0, ALU.mult, ALU.add).then_inc(l_v, 1)
                if j >= KD:
                    t = j - KD
                    dve.wait_ge(step_use, U_I + j + 1)
                    dve.wait_ge(l_v, t + 1)
                    nc.vector.tensor_tensor(V[:, t, :], XRC[j % 2][:], V[:, t, :], ALU.mult).then_inc(l_v, 1)

        def sp_phase11(sp):
            sp.wait_ge(phase_s, 4 * 9)
            sp.dma_start(GAM[0][:], A["norm_ffn"][1:2, :].to_broadcast([P, D])).then_inc(gain_in[0], 16)
            sp.wait_ge(x2_st, 16 * MT)
            for n in range(2):
                sp_residual(sp, 1, n)

        def pe_phase11(pe):
            def ready(k):
                pe.wait_ge(l_lo, k + 1)

            for m in range(MT):
                pe_token_step(pe, S_O, m, U_O + m, U_O, None if m else ready)
            pe_pass_end(S_O)
            pe_last_pass(pe, 1, S_O + 1, U_O + 8, U_O)

        def act_phase11(act):
            for k in range(KD):
                nc.scalar.activation(ATH[:, k, :], V[:, k, :], ACT.Copy).then_inc(l_hi, 1)
            act_split(act, S_O + 1)
            act_last_pass(act, 1, U_O + 8)

        def dve_phase11(dve):
            for k in range(KD):
                dve.wait_ge(l_hi, k + 1)
                nc.vector.tensor_tensor(ATL[:, k, :], V[:, k, :], ATH[:, k, :].bitcast(F32), ALU.subtract).then_inc(l_lo, 1)
            for m in range(MT):
                if m == 1:
                    dve_split(dve, S_O + 1)
                dve_add_res(dve, 1, m, 0, U_O + m, U_O)
            dve_last_pass(dve, 1, U_O + 8, lambda m: dve_add_res(dve, 1, m, 1, U_O + 8 + m, U_O))

        def pool_phase11(pool):
            pool_last_pass(pool, 1, U_O + 8)

        @block.sync
        def _(sp):
            sp_phase0(sp)
            sp_phase1(sp)
            sp_phase2(sp)
            sp_phase3(sp)
            sp_phase4(sp)
            sp_phase5(sp)
            for layer in range(2):
                if layer:
                    sp_phase10(sp)
                    sp_phase11(sp)
                sp_moe_prefetch(sp, layer)
                sp.wait_ge(phase_s, 4 * (5 + 5 * layer))
                sp_moe(sp, layer)
                sp_ovf(sp, layer)
                sp.wait_ge(m_unit, UNITS * (layer + 1))
                for m in range(3):
                    sp_comb_x(sp, m)
                sp.wait_ge(phase_s, 4 * (7 + 5 * layer))
                sp_combine(sp, layer)

        @block.scalar
        def _(act):
            act_phase0(act)
            act_phase1(act)
            finished(act, 1)
            act_phase2(act)
            finished(act, 2)
            act_phase3(act)
            finished(act, 3)
            act_phase4(act)
            finished(act, 4)
            act_phase5(act)
            finished(act, 5)
            for layer in range(2):
                if layer:
                    act_phase10(act)
                    finished(act, 9)
                    act_phase11(act)
                    finished(act, 10)
                act_hi(act, layer, 0, 0, 0)
                act_hi(act, layer, 0, 0, 1)
                act_route(act, layer)
                act_hi(act, layer, 0, 0, 2)
                act_hi(act, layer, 0, 0, 3)
                act_moe(act, layer)
                finished(act, 6 + 5 * layer)
                act_ovf(act, layer)
                finished(act, 7 + 5 * layer)
                act_combine(act, layer)
                if layer == 0:
                    finished(act, 8)

        @block.vector
        def _(dve):
            dve_phase0(dve)
            dve_phase1(dve)
            finished(dve, 1)
            dve_phase2(dve)
            finished(dve, 2)
            dve_phase3(dve)
            finished(dve, 3)
            dve_phase4(dve)
            finished(dve, 4)
            dve_phase5(dve)
            finished(dve, 5)
            for layer in range(2):
                if layer:
                    dve_phase10(dve)
                    finished(dve, 9)
                    dve_phase11(dve)
                    finished(dve, 10)
                dve_route(dve, layer)
                dve_route_rest(layer)
                dve_moe(dve, layer)
                finished(dve, 6 + 5 * layer)
                dve_ovf(dve, layer)
                finished(dve, 7 + 5 * layer)
                dve_combine(dve, layer)
                if layer == 0:
                    finished(dve, 8)

        @block.gpsimd
        def _(pool):
            pool_phase0(pool)
            pool_phase1(pool)
            finished(pool, 1)
            pool_phase2(pool)
            finished(pool, 2)
            pool_phase3(pool)
            finished(pool, 3)
            pool_phase4(pool)
            finished(pool, 4)
            pool_phase5(pool)
            finished(pool, 5)
            for layer in range(2):
                if layer:
                    finished(pool, 9)
                    pool_phase11(pool)
                    finished(pool, 10)
                pool_first_lo(pool, layer)
                pool_moe(pool, layer)
                finished(pool, 6 + 5 * layer)
                pool_ovf(pool, layer)
                finished(pool, 7 + 5 * layer)
                pool_combine(pool, layer)
                if layer == 0:
                    finished(pool, 8)

        @block.tensor
        def _(pe):
            pe_phase0(pe)
            pe_phase1(pe)
            finished(pe, 1)
            pe_phase2(pe)
            finished(pe, 2)
            pe_phase3(pe)
            finished(pe, 3)
            pe_phase4(pe)
            finished(pe, 4)
            pe_phase5(pe)
            finished(pe, 5)
            for layer in range(2):
                if layer:
                    pe_phase10(pe)
                    finished(pe, 9)
                    pe_phase11(pe)
                    finished(pe, 10)
                pe_route(pe, layer)
                pe_moe(pe, layer)
                finished(pe, 6 + 5 * layer)
                pe_ovf(pe, layer)
                finished(pe, 7 + 5 * layer)
                pe_combine(pe, layer)
                if layer == 0:
                    finished(pe, 8)


def constants():
    c = np.zeros((P, 5 * P + 64), np.float32)
    r = np.arange(P)
    c[:, 0:P] = np.eye(P)
    c[:, P:2 * P] = r[:, None] <= r[None, :]
    c[:, 2 * P:3 * P] = r[:, None] < r[None, :]
    c[:, 3 * P:4 * P] = r[None, :]
    c[:, 4 * P:5 * P] = 1.0
    misc = c[:, 5 * P:]
    misc[:, 0:MT] = P * np.arange(MT)[None, :] + r[:, None]
    misc[:, 8:15] = BLK * (np.arange(7) + 1)
    misc[:, 16:16 + OVF] = np.arange(OVF)
    misc[:, 32] = -0.5
    return c


def kernel(**inputs):
    import concourse.bacc as bacc
    from concourse.bass_utils import run_bass_kernel_spmd

    nc = bacc.Bacc("TRN2", target_bir_lowering=False, num_devices=1)
    arrays, aps = {}, {}
    for name, a in list(inputs.items()) + [("c_f32", constants())]:
        a = np.ascontiguousarray(a)
        arrays[f"in_{name}_dram"] = a
        aps[name] = nc.dram_tensor(f"in_{name}_dram", a.shape, mybir.dt.from_np(a.dtype), kind="ExternalInput").ap()
    out = nc.dram_tensor("out_0_dram", (1, T, D), F32, kind="ExternalOutput").ap()
    trunk(nc, aps, out[0])
    r = run_bass_kernel_spmd(nc, [arrays], core_ids=[0])
    return r.results[0]["out_0_dram"]
```
